# Optimizing a Trainium2 kernel written in Bass

```python
import math
import jax, jax.numpy as jnp
from jax import lax
import numpy as np

D_MODEL = 1024
BATCH = 1
SEQ = 512
DEPTH = 2
DEC_BATCH = 8
DEC_SEQ = 1
PAST_LEN = 1024
PAGE_SIZE = 128

N_MIXERS = 2
N_MLSTM_LAYERS = (DEPTH + 1) // 2
N_DSA_LAYERS = DEPTH // 2
M_HEADS = 4
M_HEAD_DIM = 128
M_WIDTH = M_HEADS * M_HEAD_DIM
CONV_WIDTH = 4
M_CHUNK = 64
M_TOK_PROJ = 4 * M_WIDTH + 2 * M_HEADS
A_HEADS = 8
A_HEAD_DIM = 64
A_WIDTH = A_HEADS * A_HEAD_DIM
IDX_HEADS = 8
IDX_DIM = 64
IDX_TOPK = 256
Q_BLOCK = 128
A_SPLIT = (A_WIDTH, A_WIDTH, A_WIDTH, IDX_HEADS * IDX_DIM, IDX_DIM, IDX_HEADS)
A_TOK_PROJ = sum(A_SPLIT)
REL_BUCKETS = 32
REL_MAX_DIST = 128
MEM_LEN = 256
X_HEADS = 4
X_HEAD_DIM = 128
X_WIDTH = X_HEADS * X_HEAD_DIM
TOK_WIDTH = 512
M_PROJ = M_TOK_PROJ + X_WIDTH
A_PROJ = A_TOK_PROJ + X_WIDTH
N_GROUPS = 4
EXP_PER_GROUP = 8
N_EXPERTS = N_GROUPS * EXP_PER_GROUP
D_EXPERT = 256
TOP_K_EXP = 2
DN_ALPHA = (2 * DEPTH) ** 0.25
DN_BETA = (8 * DEPTH) ** -0.25
LN_EPS = 1e-5

kernel_name = "hybrid_mlstm_dsa_memxattn_hmoe_step"

def layer_norm(x, g, b):
    xf = x.astype(jnp.float32)
    mu = jnp.mean(xf, -1, keepdims=True)
    var = jnp.mean(jnp.square(xf - mu), -1, keepdims=True)
    return ((xf - mu) * lax.rsqrt(var + LN_EPS)).astype(x.dtype) * g + b

def causal_conv(u, buf, w):
    T = u.shape[1]
    ext = jnp.concatenate([buf, u], axis=1)
    out = sum(ext[:, j:j + T] * w[j] for j in range(CONV_WIDTH))
    return out, ext[:, T:]

def mlstm_chunk_step(carry, inp):
    C, n, m = carry
    q, k, v, ig, lf = inp
    L = q.shape[2]
    b = jnp.cumsum(lf, axis=-1)
    causal = jnp.tril(jnp.ones((L, L), dtype=bool))
    logd = jnp.where(causal, b[..., :, None] - b[..., None, :] + ig[..., None, :], -jnp.inf)
    log_prev = b + m[..., None]
    m_t = jnp.maximum(log_prev, jnp.max(logd, axis=-1))
    d = jnp.exp(logd - m_t[..., None])
    w_prev = jnp.exp(log_prev - m_t)
    s = jnp.einsum('bhtd,bhsd->bhts', q, k) * d
    num = w_prev[..., None] * jnp.einsum('bhtk,bhvk->bhtv', q, C) + jnp.einsum('bhts,bhsv->bhtv', s, v)
    den = w_prev * jnp.einsum('bhtk,bhk->bht', q, n) + jnp.sum(s, -1)
    h = num / jnp.maximum(jnp.abs(den), jnp.exp(-m_t))[..., None]
    m_new = m_t[..., -1]
    w_c = jnp.exp(b[..., -1] + m - m_new)
    w_s = jnp.exp(b[..., -1:] - b + ig - m_new[..., None])
    C_new = w_c[..., None, None] * C + jnp.einsum('bhsv,bhsk->bhvk', v * w_s[..., None], k)
    n_new = w_c[..., None] * n + jnp.einsum('bhs,bhsk->bhk', w_s, k)
    return (C_new, n_new, m_new), h

def mlstm_mixer(u, C, n, m, conv_buf, b_gates, conv_w, norm_g, chunk):
    B, T, _ = u.shape
    nc = T // chunk
    qk, conv_new = causal_conv(u[..., :2 * M_WIDTH], conv_buf.astype(u.dtype), conv_w)
    qk = jax.nn.silu(qk).astype(jnp.float32)
    v = u[..., 2 * M_WIDTH:3 * M_WIDTH].astype(jnp.float32)
    o = u[..., 3 * M_WIDTH:4 * M_WIDTH].astype(jnp.float32)
    gates = u[..., 4 * M_WIDTH:].astype(jnp.float32) + b_gates.astype(jnp.float32)

    def to_chunks(z):
        return z.reshape(B, nc, chunk, M_HEADS, M_HEAD_DIM).transpose(1, 0, 3, 2, 4)

    def gate_chunks(g):
        return g.reshape(B, nc, chunk, M_HEADS).transpose(1, 0, 3, 2)

    q = to_chunks(qk[..., :M_WIDTH])
    k = to_chunks(qk[..., M_WIDTH:]) * (M_HEAD_DIM ** -0.5)
    ig = gate_chunks(gates[..., :M_HEADS])
    lf = gate_chunks(jax.nn.log_sigmoid(gates[..., M_HEADS:]))
    carry0 = (C.astype(jnp.float32), n.astype(jnp.float32), m.astype(jnp.float32))
    (C1, n1, m1), h = lax.scan(mlstm_chunk_step, carry0, (q, k, to_chunks(v), ig, lf))
    h = h.transpose(1, 0, 3, 2, 4).reshape(B, T, M_HEADS, M_HEAD_DIM)
    mu = jnp.mean(h, -1, keepdims=True)
    var = jnp.mean(jnp.square(h - mu), -1, keepdims=True)
    h = ((h - mu) * lax.rsqrt(var + LN_EPS)).reshape(B, T, M_WIDTH) * norm_g
    out = (h * jax.nn.sigmoid(o)).astype(u.dtype)
    return out, (C1, n1, m1, conv_new)

def t5_bucket(dist):
    exact = REL_BUCKETS // 2
    d = jnp.maximum(dist, 0)
    far = exact + (jnp.log(jnp.maximum(d, 1).astype(jnp.float32) / exact)
                   / math.log(REL_MAX_DIST / exact) * (REL_BUCKETS - exact)).astype(jnp.int32)
    return jnp.where(d < exact, d, jnp.minimum(far, REL_BUCKETS - 1))

def dsa_split(u):
    B, T, _ = u.shape
    o = [0]
    for w in A_SPLIT:
        o.append(o[-1] + w)
    q, k, v, qi, ki, wi = [u[..., o[i]:o[i + 1]] for i in range(6)]
    return (q.reshape(B, T, A_HEADS, A_HEAD_DIM), k.reshape(B, T, A_HEADS, A_HEAD_DIM),
            v.reshape(B, T, A_HEADS, A_HEAD_DIM), qi.reshape(B, T, IDX_HEADS, IDX_DIM), ki, wi)

def index_scores(qi, wi, ki):
    s = jax.nn.relu(jnp.einsum('bthd,bsd->bths', qi, ki) * (IDX_DIM ** -0.5))
    return jnp.einsum('bth,bths->bts', wi * (IDX_HEADS ** -0.5), s).astype(jnp.float32)

def sparse_attend(q, kg, vg, sel, tpos, rel_bias):
    dist = tpos[None, :, None] - sel
    bias = jnp.swapaxes(rel_bias[t5_bucket(dist)], -1, -2).astype(jnp.float32)
    logits = jnp.einsum('bthd,btkhd->bthk', q, kg).astype(jnp.float32) * (A_HEAD_DIM ** -0.5) + bias
    logits = jnp.where((dist >= 0)[:, :, None, :], logits, -jnp.inf)
    p = jax.nn.softmax(logits, axis=-1).astype(vg.dtype)
    return jnp.einsum('bthk,btkhd->bthd', p, vg)

def dsa_prompt(q, k, v, qi, ki, wi, rel_bias):
    B, T = q.shape[:2]
    topk = min(IDX_TOPK, T // 4)
    spos = jnp.arange(T)

    def block(i):
        t0 = i * Q_BLOCK
        tpos = t0 + jnp.arange(Q_BLOCK)
        qb = lax.dynamic_slice_in_dim(q, t0, Q_BLOCK, 1)
        qib = lax.dynamic_slice_in_dim(qi, t0, Q_BLOCK, 1)
        wib = lax.dynamic_slice_in_dim(wi, t0, Q_BLOCK, 1)
        sc = index_scores(qib, wib, ki)
        sc = jnp.where(spos[None, None, :] <= tpos[None, :, None], sc, -jnp.inf)
        _, sel = lax.top_k(sc, topk)
        kg = jax.vmap(lambda a, s: a[s])(k, sel)
        vg = jax.vmap(lambda a, s: a[s])(v, sel)
        return sparse_attend(qb, kg, vg, sel, tpos, rel_bias)

    out = lax.map(block, jnp.arange(T // Q_BLOCK))
    return out.transpose(1, 0, 2, 3, 4).reshape(B, T, A_WIDTH)

def dsa_sample(q, k, v, qi, ki, wi, k_pool, v_pool, ki_pool, page_table, rel_bias):
    DB, T = q.shape[:2]
    past = page_table.shape[1] * PAGE_SIZE
    L = past + T
    topk = min(IDX_TOPK, L // 4)
    tpos = past + jnp.arange(T)
    ki_past = ki_pool[page_table].reshape(DB, past, IDX_DIM).astype(ki.dtype)
    ki_all = jnp.concatenate([ki_past, ki], axis=1)
    sc = index_scores(qi, wi, ki_all)
    sc = jnp.where(jnp.arange(L)[None, None, :] <= tpos[None, :, None], sc, -jnp.inf)
    _, sel = lax.top_k(sc, topk)
    in_past = sel < past
    sp = jnp.minimum(sel, past - 1)
    phys = jax.vmap(lambda pt, s: pt[s // PAGE_SIZE])(page_table, sp)
    row = sp % PAGE_SIZE
    sn = jnp.clip(sel - past, 0, T - 1)

    def pick(pool, new):
        from_pool = pool[phys, row].astype(new.dtype)
        from_new = jax.vmap(lambda a, s: a[s])(new, sn)
        return jnp.where(in_past[..., None, None], from_pool, from_new)

    out = sparse_attend(q, pick(k_pool, k), pick(v_pool, v), sel, tpos, rel_bias)
    return out.reshape(DB, T, A_WIDTH)

def memory_attend(qm, mk, mv):
    B, T, _ = qm.shape
    qh = qm.reshape(B, T, X_HEADS, X_HEAD_DIM)
    logits = jnp.einsum('bthd,bshd->bhts', qh, mk.astype(qm.dtype)).astype(jnp.float32) * (X_HEAD_DIM ** -0.5)
    p = jax.nn.softmax(logits, axis=-1).astype(qm.dtype)
    return jnp.einsum('bhts,bshd->bthd', p, mv.astype(qm.dtype)).reshape(B, T, X_WIDTH)

def hier_moe(x, wg, bg, we, be, w_up, w_gate, w_down):
    shp = x.shape
    xf = x.reshape(-1, D_MODEL)
    g_prob = jax.nn.softmax((xf @ wg + bg).astype(jnp.float32), axis=-1)
    g_sel = jnp.argmax(g_prob, axis=-1)
    g_w = jnp.take_along_axis(g_prob, g_sel[:, None], axis=1)
    e_logits = (xf @ we + be).astype(jnp.float32).reshape(-1, N_GROUPS, EXP_PER_GROUP)
    e_logits = jnp.take_along_axis(e_logits, g_sel[:, None, None], axis=1)[:, 0]
    top_p, top_i = lax.top_k(jax.nn.softmax(e_logits, axis=-1), TOP_K_EXP)
    top_p = top_p / jnp.sum(top_p, -1, keepdims=True)
    within = jnp.sum(jax.nn.one_hot(top_i, EXP_PER_GROUP, dtype=jnp.float32) * top_p[..., None], axis=1)
    gate = jax.nn.one_hot(g_sel, N_GROUPS, dtype=jnp.float32)[:, :, None] * (g_w * within)[:, None, :]
    out = jnp.zeros_like(xf)
    for g in range(N_GROUPS):
        sl = slice(g * EXP_PER_GROUP, (g + 1) * EXP_PER_GROUP)
        h = jax.nn.silu(jnp.einsum('nd,edf->nef', xf, w_gate[sl])) * jnp.einsum('nd,edf->nef', xf, w_up[sl])
        h = h * gate[:, g, :, None].astype(h.dtype)
        out = out + jnp.einsum('nef,efd->nd', h, w_down[sl])
    return out.reshape(shp)

def residual_layer(x, tok, mem_out, w_o, g1, b1, g2, b2, wg, bg, we, be, wu, wgt, wd):
    y = jnp.concatenate([tok, mem_out], axis=-1) @ w_o
    x = layer_norm(DN_ALPHA * x + y, g1, b1)
    return layer_norm(DN_ALPHA * x + hier_moe(x, wg, bg, we, be, wu, wgt, wd), g2, b2)

def setup_inputs(seed: int = 0) -> dict:
    key = jax.random.key(seed)
    ks = iter(jax.random.split(key, 48))

    def nrm(shape, scale):
        return jax.random.normal(next(ks), shape, jnp.float32) * scale

    n_m, n_a = N_MLSTM_LAYERS, N_DSA_LAYERS
    n_pages = PAST_LEN // PAGE_SIZE
    n_used = DEC_BATCH * n_pages
    n_pool = n_used + (n_used + 3) // 4
    page_table = jax.random.permutation(next(ks), n_pool)[:n_used].reshape(DEC_BATCH, n_pages).astype(jnp.int32)

    w_in_mlstm = nrm((n_m, D_MODEL, M_PROJ), D_MODEL ** -0.5)
    w_in_mlstm = w_in_mlstm.at[:, :, 2 * M_WIDTH:3 * M_WIDTH].multiply(DN_BETA)
    w_in_mlstm = w_in_mlstm.at[:, :, 4 * M_WIDTH:M_TOK_PROJ].multiply(0.1)
    b_gates = jnp.concatenate([nrm((n_m, M_HEADS), 0.1),
                               jnp.linspace(3.0, 6.0, M_HEADS)[None, :] + nrm((n_m, M_HEADS), 0.1)], axis=-1)
    w_in_dsa = nrm((n_a, D_MODEL, A_PROJ), D_MODEL ** -0.5)
    w_in_dsa = w_in_dsa.at[:, :, 2 * A_WIDTH:3 * A_WIDTH].multiply(DN_BETA)
    w_mem_kv = nrm((DEPTH, D_MODEL, 2 * X_WIDTH), D_MODEL ** -0.5)
    w_mem_kv = w_mem_kv.at[:, :, X_WIDTH:].multiply(DN_BETA)

    return {
        "x_prompt": nrm((BATCH, SEQ, D_MODEL), 1.0),
        "x_sample": nrm((DEC_BATCH, DEC_SEQ, D_MODEL), 1.0),
        "cache_k": nrm((n_a, n_pool, PAGE_SIZE, A_HEADS, A_HEAD_DIM), 1.0),
        "cache_v": nrm((n_a, n_pool, PAGE_SIZE, A_HEADS, A_HEAD_DIM), DN_BETA),
        "cache_kidx": nrm((n_a, n_pool, PAGE_SIZE, IDX_DIM), 1.0),
        "state_C": nrm((n_m, DEC_BATCH, M_HEADS, M_HEAD_DIM, M_HEAD_DIM), 0.3),
        "state_n": nrm((n_m, DEC_BATCH, M_HEADS, M_HEAD_DIM), 0.5),
        "state_m": nrm((n_m, DEC_BATCH, M_HEADS), 1.0),
        "state_conv": nrm((n_m, DEC_BATCH, CONV_WIDTH - 1, 2 * M_WIDTH), 1.0),
        "cache_mem_k": nrm((DEPTH, DEC_BATCH, MEM_LEN, X_HEADS, X_HEAD_DIM), 1.0),
        "cache_mem_v": nrm((DEPTH, DEC_BATCH, MEM_LEN, X_HEADS, X_HEAD_DIM), DN_BETA),
        "page_table": page_table,
        "mem_prompt": nrm((BATCH, MEM_LEN, D_MODEL), 1.0),
        "w_in_mlstm": w_in_mlstm,
        "b_gates_mlstm": b_gates,
        "conv_mlstm": nrm((n_m, CONV_WIDTH, 2 * M_WIDTH), CONV_WIDTH ** -0.5),
        "norm_mlstm": 1.0 + nrm((n_m, M_WIDTH), 0.02),
        "w_in_dsa": w_in_dsa,
        "rel_bias": nrm((REL_BUCKETS, A_HEADS), 0.2),
        "w_mem_kv": w_mem_kv,
        "w_out": nrm((DEPTH, TOK_WIDTH + X_WIDTH, D_MODEL), (TOK_WIDTH + X_WIDTH) ** -0.5 * DN_BETA),
        "ln_mix_g": 1.0 + nrm((DEPTH, D_MODEL), 0.02),
        "ln_mix_b": nrm((DEPTH, D_MODEL), 0.02),
        "ln_ffn_g": 1.0 + nrm((DEPTH, D_MODEL), 0.02),
        "ln_ffn_b": nrm((DEPTH, D_MODEL), 0.02),
        "w_router_group": nrm((DEPTH, D_MODEL, N_GROUPS), D_MODEL ** -0.5),
        "b_router_group": nrm((DEPTH, N_GROUPS), 0.01),
        "w_router_expert": nrm((DEPTH, D_MODEL, N_EXPERTS), D_MODEL ** -0.5),
        "b_router_expert": nrm((DEPTH, N_EXPERTS), 0.01),
        "w_exp_up": nrm((DEPTH, N_EXPERTS, D_MODEL, D_EXPERT), D_MODEL ** -0.5),
        "w_exp_gate": nrm((DEPTH, N_EXPERTS, D_MODEL, D_EXPERT), D_MODEL ** -0.5),
        "w_exp_down": nrm((DEPTH, N_EXPERTS, D_EXPERT, D_MODEL), D_EXPERT ** -0.5 * DN_BETA),
    }

def reference(x_prompt, x_sample, cache_k, cache_v, cache_kidx, state_C, state_n, state_m, state_conv,
              cache_mem_k, cache_mem_v, page_table, mem_prompt, w_in_mlstm, b_gates_mlstm, conv_mlstm,
              norm_mlstm, w_in_dsa, rel_bias, w_mem_kv, w_out, ln_mix_g, ln_mix_b, ln_ffn_g, ln_ffn_b,
              w_router_group, b_router_group, w_router_expert, b_router_expert, w_exp_up, w_exp_gate,
              w_exp_down):
    xp, xs = x_prompt, x_sample
    bp, ts = xp.shape[0], xs.shape[1]
    kp, vp, kip, ksm, vsm, kism = [], [], [], [], [], []
    Cp, nP, mP, cP, Cs, nS, mS, cS = [], [], [], [], [], [], [], []
    mkp, mvp = [], []
    for l in range(DEPTH):
        j = l // N_MIXERS
        kv = mem_prompt @ w_mem_kv[l]
        mk_p = kv[..., :X_WIDTH].reshape(bp, -1, X_HEADS, X_HEAD_DIM)
        mv_p = kv[..., X_WIDTH:].reshape(bp, -1, X_HEADS, X_HEAD_DIM)
        mkp.append(mk_p)
        mvp.append(mv_p)
        if l % N_MIXERS == 0:
            up_p = xp @ w_in_mlstm[j]
            up_s = xs @ w_in_mlstm[j]
            tok_p, st_p = mlstm_mixer(
                up_p[..., :M_TOK_PROJ],
                jnp.zeros((bp, M_HEADS, M_HEAD_DIM, M_HEAD_DIM), jnp.float32),
                jnp.zeros((bp, M_HEADS, M_HEAD_DIM), jnp.float32),
                jnp.zeros((bp, M_HEADS), jnp.float32),
                jnp.zeros((bp, CONV_WIDTH - 1, 2 * M_WIDTH), xp.dtype),
                b_gates_mlstm[j], conv_mlstm[j], norm_mlstm[j], M_CHUNK)
            tok_s, st_s = mlstm_mixer(up_s[..., :M_TOK_PROJ], state_C[j], state_n[j], state_m[j], state_conv[j],
                                      b_gates_mlstm[j], conv_mlstm[j], norm_mlstm[j], ts)
            Cp.append(st_p[0]); nP.append(st_p[1]); mP.append(st_p[2]); cP.append(st_p[3])
            Cs.append(st_s[0]); nS.append(st_s[1]); mS.append(st_s[2]); cS.append(st_s[3])
        else:
            up_p = xp @ w_in_dsa[j]
            up_s = xs @ w_in_dsa[j]
            q, k, v, qi, ki, wi = dsa_split(up_p[..., :A_TOK_PROJ])
            tok_p = dsa_prompt(q, k, v, qi, ki, wi, rel_bias)
            kp.append(k); vp.append(v); kip.append(ki)
            q, k, v, qi, ki, wi = dsa_split(up_s[..., :A_TOK_PROJ])
            tok_s = dsa_sample(q, k, v, qi, ki, wi, cache_k[j], cache_v[j], cache_kidx[j], page_table, rel_bias)
            ksm.append(k); vsm.append(v); kism.append(ki)
        mo_p = memory_attend(up_p[..., -X_WIDTH:], mk_p, mv_p)
        mo_s = memory_attend(up_s[..., -X_WIDTH:], cache_mem_k[l], cache_mem_v[l])
        xp = residual_layer(xp, tok_p, mo_p, w_out[l], ln_mix_g[l], ln_mix_b[l], ln_ffn_g[l], ln_ffn_b[l],
                            w_router_group[l], b_router_group[l], w_router_expert[l], b_router_expert[l],
                            w_exp_up[l], w_exp_gate[l], w_exp_down[l])
        xs = residual_layer(xs, tok_s, mo_s, w_out[l], ln_mix_g[l], ln_mix_b[l], ln_ffn_g[l], ln_ffn_b[l],
                            w_router_group[l], b_router_group[l], w_router_expert[l], b_router_expert[l],
                            w_exp_up[l], w_exp_gate[l], w_exp_down[l])
    return (xp, xs,
            jnp.stack(kp), jnp.stack(vp), jnp.stack(kip),
            jnp.stack(ksm), jnp.stack(vsm), jnp.stack(kism),
            jnp.stack(Cp), jnp.stack(nP), jnp.stack(mP), jnp.stack(cP),
            jnp.stack(Cs), jnp.stack(nS), jnp.stack(mS), jnp.stack(cS),
            jnp.stack(mkp), jnp.stack(mvp))


_drawn_inputs = setup_inputs


def setup_inputs(seed=0):
    import zlib

    import numpy as np

    out = dict(_drawn_inputs(seed))
    spreads = {}
    factors = {'cache_k': 5.47,
     'cache_v': 4.322,
     'cache_kidx': 4.765,
     'cache_mem_k': 4.014,
     'cache_mem_v': 2.703,
     'norm_mlstm': 8.0,
     'rel_bias': 7.572,
     'b_router_group': 7.355,
     'b_router_expert': 19.305}
    for name, (base, spread) in spreads.items():
        noise = np.random.default_rng([zlib.crc32(name.encode()), seed]).standard_normal(out[name].shape)
        drawn = base * np.exp(spread * noise) if base else spread * noise
        out[name] = __import__('jax').numpy.asarray(drawn.astype(out[name].dtype))
    for name, factor in factors.items():
        out[name] = (out[name] * factor).astype(out[name].dtype)
    return out
```

```python
from contextlib import ExitStack

import concourse.bass as bass
from concourse import mybir

ALU = mybir.AluOpType
ACT = mybir.ActivationFunctionType
AX = mybir.AxisListType
F32 = mybir.dt.float32
I32 = mybir.dt.int32
U32 = mybir.dt.uint32

D = 1024
KD = D // 128
SEQ = 512
NB = 8
TT = SEQ + NB
TILES = [(0, 128), (128, 128), (256, 128), (384, 128), (512, NB)]
NT = len(TILES)
DEPTH = 2
MH, MD, MW = 4, 128, 512
AH, AD, AW = 8, 64, 512
MEM, XH, XD, XW = 256, 4, 128, 512
PAST, PAGE = 1024, 128
NPG = PAST // PAGE
TOPK_P = min(256, SEQ // 4)
TOPK_S = min(256, (PAST + 1) // 4)
NG, EPG, NE, DE = 4, 8, 32, 256
ALPHA = float((2 * DEPTH) ** 0.25)
EPS = 1e-5
NEG = -1e30
NONE = -2e38
TAKEN = -3e38
MTILES = NE + 8
LW = MTILES + 4
GRP = 4


CST = [("ident", 128), ("flip", 128), ("causal", 128), ("ones", 128), ("before", 128), ("del88", 64),
       ("iota", NE), ("e8", 64), ("e84", 32), ("seln", 4 * 128), ("hsel", 8), ("e64", 8), ("tokid", NT),
       ("iota8", 8)]
TBL = [("sdist", PAST), ("self", 2), ("pdist", 640)]


def offsets(parts):
    out, at = {}, 0
    for name, n in parts:
        out[name] = (at, n)
        at += n
    return out, at


def constants():
    import math
    import numpy as np
    off, width = offsets(CST)
    c = np.zeros((128, width), np.float32)
    p = np.arange(128)[:, None]

    def put(name, value):
        a, n = off[name]
        c[:value.shape[0], a:a + n] = value

    j = np.arange(128)[None, :]
    put("ident", (p == j) * 1.0)
    put("flip", (p + j == 127) * 1.0)
    put("causal", np.where(j > p, NEG, 0.0))
    put("ones", np.ones((128, 128)))
    put("before", (p < j) * 1.0)
    put("del88", np.tile(np.eye(8).reshape(1, 64), (128, 1)))
    put("iota", np.tile(np.arange(NE)[None], (128, 1)))
    put("e8", (np.arange(8)[:, None] == np.arange(64)[None] // 8) * 1.0)
    put("e84", (np.arange(8)[:, None] == np.arange(32)[None] // 4) * 1.0)
    put("seln", -np.repeat(np.eye(4), 128, axis=1))
    put("hsel", (np.arange(64)[:, None] % 8 == np.arange(8)[None]) * 1.0)
    put("e64", (np.arange(64)[:, None] // 8 == np.arange(8)[None]) * 1.0)
    put("tokid", 128.0 * np.arange(NT)[None] + p)
    put("iota8", np.tile(np.arange(8)[None], (128, 1)))

    def bucket(dist):
        d = np.maximum(dist, 0)
        far = 16 + (np.log(np.maximum(d, 1).astype(np.float32) / np.float32(16))
                    / np.float32(math.log(8)) * np.float32(16)).astype(np.int32)
        return np.where(d < 16, d, np.minimum(far, 31))

    b = np.arange(32)[:, None]
    t = np.concatenate([
        bucket(PAST - np.arange(PAST))[None] == b,
        np.tile(b == 0, (1, 2)),
        bucket(SEQ - 1 - np.arange(640))[None] == b,
    ], axis=1).astype(np.float32)
    return c, t


class Region:

    def __init__(self, tensor, start, end):
        self.tensor, self.at, self.end = tensor, start, end

    def take(self, *dims, rows=128, dtype=F32):
        n = 1
        for d in dims:
            n *= d
        assert self.at + n <= self.end, (self.at, n, self.end)
        v = self.tensor[:rows, self.at:self.at + n]
        self.at += n
        if dtype != F32:
            v = v.bitcast(dtype)
        if len(dims) == 2:
            v = v.rearrange("p (a b) -> p a b", b=dims[1])
        if len(dims) == 3:
            v = v.rearrange("p (a b c) -> p a b c", b=dims[1], c=dims[2])
        if len(dims) == 4:
            v = v.rearrange("p (a b c d) -> p a b c d", b=dims[1], c=dims[2], d=dims[3])
        return v

    def overlay(self):
        return Region(self.tensor, self.at, self.end)


class PsumRing:

    def __init__(self, ps, filled, freed):
        self.ps, self.filled, self.freed = ps, filled, freed
        self.uses, self.at, self.count, self.done = [], {}, {"act": 0, "dve": 0}, {"act": 0, "dve": 0}

    def open(self, pe, key, reader):
        n = len(self.uses)
        if n >= 8:
            who, k = self.uses[n - 8]
            pe.wait_ge(self.freed[who], k)
        self.count[reader] += 1
        assert key not in self.at, key
        self.at[key] = (n, reader, self.count[reader])
        self.uses.append((reader, self.count[reader]))
        return self.ps[:, n % 8, :]

    def close(self, mm):
        mm.then_inc(self.filled, 1)

    def full(self, eng, key):
        n, _, _ = self.at[key]
        eng.wait_ge(self.filled, n + 1)
        return self.ps[:, n % 8, :]

    def free(self, ins, key):
        _, who, k = self.at[key]
        self.done[who] += 1
        assert self.done[who] == k, (key, who, k, self.done[who])
        ins.then_inc(self.freed[who], 1)

    def read(self, eng, key):
        _, who, k = self.at[key]
        eng.wait_ge(self.freed[who], k)


def bc(ap, axis, n):
    v = ap.unsqueeze(axis)
    shape = list(v.shape)
    shape[axis] = n
    return v.broadcast_to(shape)


def build(nc, a, o, scratch):
    with ExitStack() as ctx:
        def sem(name):
            return ctx.enter_context(nc.semaphore(name))

        psum = ctx.enter_context(nc.psum_tensor("psum", [128, 8, 512], F32))
        WIDTH = 53100
        mem = ctx.enter_context(nc.sbuf_tensor("mem", [128, WIDTH], F32))

        top = Region(mem, 0, WIDTH)
        coff, cwidth = offsets(CST)
        cst = top.take(cwidth)

        def C(name, rows=128):
            at, n = coff[name]
            return cst[:rows, at:at + n]

        ident = C("ident")
        X = top.take(NT, D)
        XT = top.take(KD, TT)
        MT = top.take(KD, MEM)
        small = top.take(48)
        stats = small[:, 0:12].rearrange("p (a b) -> p a b", b=6)
        moments = small[:, 12:22].rearrange("p (a b) -> p a b", b=2)
        rstd, vare, std = small[:, 24:29], small[:, 30:35], small[:, 36:41]

        mix = top.overlay()
        WS = mix.take(2, KD, 512)
        ct_at = mix.at
        CT = mix.take(KD, TT)
        KMT = mix.take(XH, MEM)
        MKROW = mix.take(2, XW)
        VM = mix.take(2, XW)
        QMT = mix.take(XH, TT)
        ln_at = mix.at
        lng = mix.take(2, D)
        ln_end = mix.at = mix.at + 8
        MEMROW = lng
        tok = mix.overlay()
        xt_reuse = Region(mem, cwidth + NT * D, cwidth + NT * D + KD * TT)
        ct_reuse = Region(mem, ct_at, ct_at + KD * TT)

        m0 = tok.overlay()
        QK = m0.take(KD, TT)
        VA = m0.take(4, MH, 130)
        GO = m0.take(NT, MW)
        TOK = m0.take(NT, MW)
        GW = m0.take(KD, 8)
        CW = m0.take(KD, 4)
        SCT = m0.take(KD, 24)
        UST = m0.take(KD, NB)
        CVS = m0.take(3, KD, NB)
        UTAIL = m0.take(KD, 4)
        GB = m0.take(16)
        NGB = m0.take(MW)
        VS = m0.take(MW, rows=NB)
        gcol = m0.take(96)
        aC, mC, mendC = gcol[:, 0:16], gcol[:, 16:32], gcol[:, 32:36]
        emC, wendC, dn = gcol[:, 36:52], gcol[:, 52:68], gcol[:, 68:84]
        dmend = gcol[:4, 84:88]
        ST = m0.take(20, 6)
        MV = m0.take(20, 2)
        hv, hs_, hr = m0.take(20), m0.take(20), m0.take(20)
        sg = m0.take(200, rows=NB)
        m0s = m0.overlay()
        TH = m0.take(2, SEQ)
        G = {n: m0.take(SEQ, rows=4) for n in ("x", "e", "lf", "B", "a", "M")}
        cr = ct_reuse.overlay()
        CWR = cr.take(D, rows=4)
        SCR = cr.take(D, rows=24)
        cr = ct_reuse.overlay()
        NUM = cr.take(16, 130)
        AR = cr.take(2, SEQ)
        DD = cr.take(2, SEQ)
        PT = xt_reuse.overlay().take(2, 4, SEQ)
        CIN = xt_reuse.overlay().take(NB, MW)
        cr = ct_reuse.overlay()
        QKR = cr.take(D, rows=NB)
        UR = cr.take(D, rows=NB)
        QMK = cr.take(2, MW, rows=NB)
        VMK = cr.take(2, MW, rows=NB)
        KW = m0s.take(4, MW)
        CS = m0s.take(MH, MD)
        R = {n: m0s.take(MW, rows=NB) for n in ("vd", "n", "t", "t2")}
        CTMP = m0s.take(MW)
        NNR = m0s.take(MW, rows=1)
        UPR = m0s.take(D, rows=3)
        CQ = m0s.take(NB, MH)
        WPB = m0s.take(NB, MH)
        WPM = m0s.take(NB, MH, rows=NB)

        m1 = tok.overlay()
        R1 = {n: m1.take(AW, rows=NB) for n in ("q", "k", "v", "qi")}
        r1ki = m1.take(AD, rows=NB)
        r1t = m1.take(AW, rows=NB)
        r1wi = m1.take(AH, rows=NB)
        RB = m1.take(AH, rows=32)
        RB64 = m1.take(NB, AH, rows=32)
        WIP = m1.take(4, AH)
        PTB = m1.take(NB * NPG, rows=1, dtype=I32)
        m1a = m1.overlay()
        kw_at = m1a.at
        KW1 = m1a.take(KD, 136)
        AQT = m1a.take(4, TT)
        AKT = m1a.take(4, TT)
        QIT = m1a.take(4, TT)
        KIT = m1a.take(TT)
        VR = m1a.take(4, AW)
        table_at = m1a.at
        OHP = m1a.take(640, rows=32)
        RBT = m1a.take(640, rows=8)
        ring_at = m1a.at
        MASK = m1a.take(4, SEQ)
        HK = m1a.take(2, SEQ)
        PR = m1a.take(2, SEQ)
        SC = m1a.take(2, SEQ)
        relu_at = m1a.at
        RLU = m1a.take(2, SEQ)
        KROW = ct_reuse.overlay().take(4, AW)
        KIROW = m1a.take(4, AD)
        m8 = m1a.take(8)
        anm, asm, ars = m1a.take(32), m1a.take(32), m1a.take(32)
        QIS = m1a.take(8, 8, rows=64)
        WT = m1a.take(8, rows=NB)
        WM = m1a.take(8, 8, rows=NB)
        LN8 = m1a.take(8, rows=NB)
        LNM = m1a.take(8, 8, rows=NB)
        PN = m1a.take(8, rows=64)
        P8 = m1a.take(8, rows=NB)
        PM8 = m1a.take(8, 8, rows=NB)
        s8 = m1a.take(8)
        sst = m1a.take(8, rows=64)
        PTA = xt_reuse.overlay().take(2, 4, SEQ)
        KV = Region(mem, ring_at, relu_at).take(4, 2, AW)
        S_RL = Region(mem, relu_at, mem.shape[1]).take(2, 512, rows=NB)
        OHS = Region(mem, table_at, ring_at).take(PAST + 2, rows=32)
        S_WK = Region(mem, kw_at, kw_at + KD * 136).take(PAST + 2, rows=NB)
        ln_reuse = Region(mem, ln_at, ln_end)
        S_SC = ln_reuse.take(PAST + 2, rows=NB)
        LR = ln_reuse.overlay().take(PAST + 1, rows=64)
        KIX = ln_reuse.take(2, NPG, AD)
        mt_reuse = Region(mem, cwidth + NT * D + KD * TT, cwidth + NT * D + KD * TT + KD * MEM)
        S_QM = mt_reuse.take(2, AW, rows=NB)
        LG = mt_reuse.take(NPG, 64)
        PTS = mt_reuse.take(NPG, 64)
        KXT = Region(mem, ct_at + 4 * TT, ct_at + 8 * TT).take(2, PAST)
        S_T = r1t
        VV = WS[:, 1].rearrange("p (n j) c -> p n j c", j=2)

        mm = tok.overlay()
        MP = mm.take(2, MEM)
        MPT = mm.take(2, 2, SEQ)
        MK2 = mm.take(2, 2, XW)
        MV8 = mm.take(NB, 2, XW)
        MQR = mm.take(XW, rows=NB)
        MQM = mm.take(2, XW, rows=NB)
        MLG = mm.take(2, 32)
        MLR = mm.take(MEM, rows=32)
        MPS = mm.take(2, 32)
        mnm, msm, mrs = mm.take(16), mm.take(16), mm.take(16)
        mst = mm.take(4, rows=32)

        mo = top.overlay()
        we_at = mo.at
        WE = mo.take(GRP, 3, 2 * D)
        XE = mo.take(2, D)
        XET = mo.take(2, KD, 128)
        SG = mo.take(2, DE)
        HH = mo.take(DE)
        HT = mo.take(2, 128)
        OUT = mo.take(2, D)
        WR = mo.take(KD, 36)
        BR = mo.take(36)
        RL = mo.take(NT, 36)
        rt = {n: mo.take(NT, NE) for n in ("l2", "eq", "c", "oh1", "oh2", "l3", "both", "pos", "t")}
        rg = {n: mo.take(NT, NG) for n in ("e", "eq", "c", "oh")}
        rs = {n: mo.take(NT) for n in ("gm", "gw", "m1", "m2", "d", "e2", "w1", "mn", "e", "p", "q", "ot", "t",
                                        "g1", "g2", "cell", "row")}
        cnt, over, incl, excl = mo.take(NE), mo.take(NE), mo.take(NE), mo.take(NE)
        et1, et2, et3 = mo.take(8, NE), mo.take(8, NE), mo.take(8)
        ngf = mo.take(2)
        ROWI = mo.take(2, NT, dtype=U32)
        CELLI = mo.take(2, NT, dtype=U32)
        TOKI = mo.take(NT, dtype=U32)
        ETI = mo.take(8, dtype=I32)
        NGI = mo.take(1, dtype=I32)
        LZ = mo.take(LW, dtype=U32)
        LST = mo.take(LW, dtype=U32)
        IDX = mo.take(GRP, dtype=U32)
        lnf = mo.take(2, D)
        YG = Region(mem, we_at, we_at + 4 * D).take(2, 2, D)

        NPOOL = a["cache_k"].shape[1]

        ring = PsumRing(psum, sem("bank_filled"), {"act": sem("bank_freed_act"), "dve": sem("bank_freed_dve")})
        order = {e: sem(f"{e}_order") for e in ("act", "dve", "pool")}
        at_order = {"act": 0, "dve": 0, "pool": 0}
        stage_done = sem("stage_done")
        n_stage = {}

        def seq(eng, name, ins):
            at_order[name] += 1
            ins.then_inc(order[name], 1)
            eng.wait_ge(order[name], at_order[name])

        def stage_end(eng, name):
            n_stage[name] = n_stage.get(name, 0) + 1
            eng.drain().then_inc(stage_done, 1)
            eng.wait_ge(stage_done, 4 * n_stage[name])

        s_cst, s_x, s_mem = sem("constants_in"), sem("x_in"), sem("mem_in")
        s_l0, s_l1, s_ln = sem("layer0_small_in"), sem("layer1_small_in"), sem("ln_mix_in")
        s_st = sem("stored")
        stored = [0]
        s = {n: sem(n) for n in (
            "gates_lin", "gates_ln", "dmend_done", "conv_done", "tanh_done", "silu_done", "sconv_done",
            "stanh_done", "ssilu_done", "vones", "exp_lin", "exp_col", "go_ready", "arg_done", "decay_done",
            "decay_cut", "sg_lin", "sg_ln", "sg_lin2", "sg_exp", "c_in", "n_in", "masked", "cq_done", "wp_ready",
            "var_ready", "std_ready", "tok_ready", "urow", "mmax", "mnorm", "mk_in0", "mk_in1", "mv_in", "mqmask",
            "mk_used", "msmax", "msexp", "msnorm", "scored", "cut", "mask_ready", "rbt_out", "hk_in0", "hk_in1",
            "amax", "anorm", "lnstd", "x_norm", "x1_out", "kix_in0", "kix_in1", "v_in0", "v_in1", "v_in2", "v_in3", "v_used", "kv_in0", "kv_in1", "kv_in2", "kv_in3",
            "kv_done", "wm_ready", "smask", "sqm", "lnew", "smax", "sexp", "snorm", "pnew", "pm8", "krow_out", "experts_out",
            "ohs_in", "router_in", "lnf_in", "router_lin", "router_exp", "e2_lin", "e2_exp", "route_ready",
            "table_ready", "zeroed", "scattered", "ids_in", "y_in0", "y_in1", "y_used")}
        moe = [{n: sem(f"{n}_{l}") for n in (
            "w_in0", "w_in1", "w_in2", "w_in3", "gathered0", "gathered1", "turned_a", "turned_b", "xe_a", "xe_b",
            "gu_done", "silu", "h_made", "h_turned", "ht_ready", "down_done", "out_a", "out_b", "put0", "put1",
            "picked")}
            for l in range(DEPTH)]

        def w_cols(w, c0):
            return w[:, c0:c0 + 512].rearrange("(p k) n -> p k n", k=KD)

        def w_rows(w, c0):
            return w[:, c0:c0 + 512].rearrange("(k p) n -> p k n", p=128)

        chunks = []
        for l in range(DEPTH):
            kv = a["w_mem_kv"][l]
            chunks += [(l, "km", w_cols(kv, 0)), (l, "vm", w_cols(kv, XW))]
            w = a["w_in_mlstm"][0] if l == 0 else a["w_in_dsa"][0]
            names = [("q", 0), ("k", 512), ("v", 1024), ("o", 1536), ("qm", 2056)] if l == 0 else \
                    [("q", 0), ("qi", 1536), ("k", 512), ("v", 1024), ("qm", 2120)]
            chunks += [(l, n, w_cols(w, c)) for n, c in names]
            chunks += [(l, "wo0", w_rows(a["w_out"][l], 0)), (l, "wo1", w_rows(a["w_out"][l], 512))]
        chunk_no = {(l, n): i for i, (l, n, _) in enumerate(chunks)}
        chunk_last = {}
        chunk_in = [sem("chunk_in0"), sem("chunk_in1")]

        def chunk(pe, l, name):
            i = chunk_no[(l, name)]
            pe.wait_ge(chunk_in[i % 2], 16 * (i // 2 + 1))
            return WS[:, i % 2]

        def mark_chunk(l, name):
            chunk_last[chunk_no[(l, name)]] = len(ring.uses)

        Q4 = [(c * 128, 128) for c in range(4)]
        SOFTMAX_AT = 2
        VALUES_AT = {3 * b + 9: b for b in range(NB)}
        block = ctx.enter_context(nc.Block())

        T = nc.tensor

        def turn_rows(pe, src, key, readers, n):
            v = src.rearrange("r (p k) -> r k p", k=KD)
            for half in range(2):
                bank = ring.open(pe, key + (half,), readers[half])
                for j in range(4):
                    mm_ = T.transpose(bank[:, j * n:j * n + n], v[:, 4 * half + j, :], ident[:n, :n])
                ring.close(mm_)

        def product(pe, key, reader, terms, rows, ncol, at=0):
            bank = ring.open(pe, key, reader)
            for k, (lhs, rhs) in enumerate(terms):
                mm_ = T.matmul(bank[:rows, at:at + ncol], lhs, rhs, start=(k == 0), stop=(k == len(terms) - 1))
            ring.close(mm_)

        def project_cols(pe, l, name, w, c0, reader, ncol=128):
            product(pe, (l, name), reader,
                    [(w[:, k, c0:c0 + ncol], XT[:, k, 0:SEQ]) for k in range(KD)], ncol, SEQ)

        def project_sample(pe, l, name, w, parts, reader):
            bank = ring.open(pe, (l, name), reader)
            for j, (c0, ncol) in enumerate(parts):
                for k in range(KD):
                    mm_ = T.matmul(bank[:ncol, j * NB:j * NB + NB], w[:, k, c0:c0 + ncol], XT[:, k, SEQ:TT],
                                   start=(k == 0), stop=(k == KD - 1))
            ring.close(mm_)

        def project_rows(pe, l, name, w, i, reader):
            t0, n = TILES[i]
            product(pe, (l, name, i), reader,
                    [(XT[:, k, t0:t0 + n], w[:, k, :]) for k in range(KD)], n, w.shape[2])

        def turn_parts(pe, key, reader, parts):
            bank = ring.open(pe, key, reader)
            for at, src in parts:
                p, n = src.shape
                mm_ = T.transpose(bank[:n, at:at + p], src, ident[:p, :p])
            ring.close(mm_)

        def pe_mlstm(pe):
            def nums(h):
                for i in range(4):
                    bank = ring.open(pe, ("num", h, i), "act")
                    for st in range(i + 1):
                        if i == 0:
                            ring.read(pe, ("score", h, 3))
                        mm_ = T.matmul(bank[:, 0:129], PT[:, h % 2, st, (i - st) * 128:(i - st + 1) * 128],
                                       VA[:, st, h, 0:129], start=(st == 0), stop=(st == i))
                    ring.close(mm_)

            pe.wait_ge(s["silu_done"], 8)
            pe.wait_ge(s["vones"], 1)
            for i in range(4):
                ring.read(pe, (0, "v", i))
            for h in range(MH):
                product(pe, ("negm", h), "dve", [(C("seln", 4)[:, h * 128:(h + 1) * 128], G["M"])], 128, SEQ)
                for st in range(4):
                    product(pe, ("score", h, st), "dve",
                            [(QK[:, 4 + h, st * 128:(st + 1) * 128], QK[:, h, st * 128:SEQ])], 128, SEQ - st * 128)
                if h:
                    nums(h - 1)
            nums(MH - 1)
            stage_end(pe, "pe")
            for st in range(4):
                turn_parts(pe, ("krow", st), "dve", [(h * 128, QK[:, 4 + h, st * 128:(st + 1) * 128]) for h in range(MH)])
            pe.wait_ge(s["ssilu_done"], 1)
            turn_parts(pe, ("sq",), "act", [(h * 128, QK[:, h, SEQ:TT]) for h in range(MH)])
            turn_parts(pe, ("sk",), "dve", [(h * 128, QK[:, 4 + h, SEQ:TT]) for h in range(MH)])
            for j in range(2):
                turn_parts(pe, ("su", j), "act", [(c * 128, UST[:, 4 * j + c, :]) for c in range(4)])
            for j in range(2):
                turn_parts(pe, ("pu", j), "act", [(c * 128, UTAIL[:, 4 * j + c, 0:3]) for c in range(4)])
            ring.read(pe, ("krow", 3))
            bank = ring.open(pe, ("newC",), "act")
            for h in range(MH):
                for st in range(4):
                    mm_ = T.matmul(bank[:, h * 128:(h + 1) * 128], VA[:, st, h, 0:128], KW[:, st, h * 128:(h + 1) * 128],
                                   start=(st == 0), stop=(st == 3))
            ring.close(mm_)
            product(pe, ("newn",), "act", [(C("ones")[:, 0:1], KW[:, st, :]) for st in range(4)], 1, MW)
            pe.wait_ge(s["wp_ready"], 1)
            product(pe, ("wp",), "dve", [(C("ones", NB), WPM.rearrange("p b h -> p (b h)"))], 128, 32)
            for b in range(NB):
                pe.wait_ge(s["masked"], b + 1)
                product(pe, ("qb", b), "dve", [(C("ones", NB), QMK[:, b % 2, :])], 128, MW)
                bank = ring.open(pe, ("vk", b), "dve")
                for h in range(MH):
                    mm_ = T.matmul(bank[:, h * 128:(h + 1) * 128], VMK[:, b % 2, h * 128:(h + 1) * 128],
                                   QKR[:, MW + h * 128:MW + (h + 1) * 128], start=True, stop=True)
                ring.close(mm_)
            pe.wait_ge(s["cq_done"], 1)
            turn_parts(pe, ("cqT",), "dve", [(h * 128, CQ[:, :, h]) for h in range(MH)])
            pe.wait_ge(s["tok_ready"], 1)
            for i, (t0, n) in enumerate(TILES):
                turn_parts(pe, (0, "tokT", i), "act", [(c * n, TOK[:n, i, c * 128:(c + 1) * 128]) for c in range(4)])

        def pe_dsa_projections(pe):
            w = chunk(pe, 1, "q")
            for c in range(4):
                project_cols(pe, 1, "q" + str(c), w, c * 128, "act")
            project_sample(pe, 1, "qs", w, Q4, "act")
            mark_chunk(1, "q")
            w = chunk(pe, 1, "qi")
            for c in range(4):
                project_cols(pe, 1, "qi" + str(c), w, c * 128, "dve")
            project_sample(pe, 1, "qis", w, Q4, "dve")
            mark_chunk(1, "qi")
            project_cols(pe, 1, "ki", KW1, 0, "act")
            project_sample(pe, 1, "kis", KW1, [(0, 128)], "act")
            for i in reversed(range(NT)):
                project_rows(pe, 1, "wi", KW1[:, :, 128:136], i, "dve")
            ring.read(pe, (1, "qs"))
            turn_parts(pe, ("sq1",), "act", [(c * 128, AQT[:, c, SEQ:TT]) for c in range(4)])
            ring.read(pe, (1, "qis"))
            turn_parts(pe, ("sqi1",), "act", [(c * 128, QIT[:, c, SEQ:TT]) for c in range(4)])
            ring.read(pe, (1, "kis"))
            turn_parts(pe, ("ski1",), "act", [(0, KIT[0:AD, SEQ:TT])])
            ring.read(pe, ("sqi1",))
            turn_parts(pe, ("qis",), "act", [(g * 8, R1["qi"][:, g * 64:(g + 1) * 64]) for g in range(8)])
            ring.read(pe, (1, "wi", 4))
            turn_parts(pe, ("wT",), "dve", [(0, r1wi)])

            def products():
                w = chunk(pe, 1, "k")
                for c in range(4):
                    project_cols(pe, 1, "k" + str(c), w, c * 128, "act")
                    yield
                project_sample(pe, 1, "ks", w, Q4, "act")
                mark_chunk(1, "k")
                yield
                w = chunk(pe, 1, "v")
                for i in range(NT):
                    project_rows(pe, 1, "v", w, i, "act")
                    if i == NT - 1:
                        mark_chunk(1, "v")
                    yield
                w = chunk(pe, 1, "qm")
                for c in range(4):
                    project_cols(pe, 1, "qm" + str(c), w, c * 128, "act")
                    yield
                project_sample(pe, 1, "qms", w, Q4, "act")
                mark_chunk(1, "qm")
                yield

            def keys(b):
                pe.wait_ge(s["kix_in%d" % (b % 2)], 16 * NPG * (b // 2 + 1))
                for half in range(2):
                    turn_parts(pe, ("kxT", b, half), "act",
                               [(j * 128, KIX[:, b % 2, half * 4 + j, :]) for j in range(4)])

            product_ = products()
            keys(0)
            ring.read(pe, ("qis",))
            for b in range(NB):
                pe.wait_ge(s["sqm"], b + 1)
                product(pe, ("sqb", b), "dve", [(C("ones", NB), S_QM[:, b % 2, :])], 128, AW)
                for half in range(2):
                    ring.read(pe, ("kxT", b, half))
                    product(pe, ("sx", b, half), "act",
                            [(QIS[:, :, b], KXT[0:64, b % 2, half * 512:(half + 1) * 512])], 8, 512)
                if b + 1 < NB:
                    keys(b + 1)
                next(product_)
                pe.wait_ge(s["wm_ready"], 1)
                for half in range(2):
                    ring.read(pe, ("sx", b, half))
                    product(pe, ("sw", b, half), "dve", [(WM[:, b, :], S_RL[:, half, :])], 8, 512)
            for _ in product_:
                pass

        def pe_dsa(pe):
            for c in range(4):
                ring.read(pe, (1, "k%d" % c))
            ring.read(pe, (1, "ks"))
            for i in range(4):
                turn_parts(pe, ("krow1", i), "act", [(c * 128, AKT[:, c, i * 128:(i + 1) * 128]) for c in range(4)])
            turn_parts(pe, ("sk1",), "act", [(c * 128, AKT[:, c, SEQ:TT]) for c in range(4)])
            ring.read(pe, (1, "ki"))
            turn_parts(pe, ("kirow",), "act", [(i * AD, KIT[0:AD, i * 128:(i + 1) * 128]) for i in range(4)])
            for j, (c0, n) in enumerate(((0, 512), (512, 128))):
                product(pe, ("rbt", j), "act", [(RB, OHP[:, c0:c0 + n])], 8, n)
            for c in range(4):
                ring.read(pe, (1, "qi%d" % c))
            for i in range(1, 4):
                w = (i + 1) * 128
                for g in range(8):
                    p0 = (g % 2) * 64
                    product(pe, ("ix", i, g), "act",
                            [(QIT[p0:p0 + 64, g // 2, i * 128:(i + 1) * 128], KIT[p0:p0 + 64, 0:w])], 128, w)
            pe.wait_ge(s["smask"], 1)
            pe.wait_ge(s["ohs_in"], 16)
            for half in range(2):
                bank = ring.open(pe, ("lr", half), "act")
                cols = slice(half * 512, (half + 1) * 512)
                T.matmul(bank[:64, :], RB64.rearrange("p b h -> p (b h)"), OHS[:, cols], start=True, stop=False,
                         skip_group_check=True)
                T.matmul(bank[:64, :], C("e8", NB), S_WK[:, cols], start=False, stop=False, skip_group_check=True)
                for j in range(4):
                    mm_ = T.matmul(bank[:64, j * 128:(j + 1) * 128], LG[:, half * 4 + j, :], ident, start=False,
                                   stop=(j == 3), skip_group_check=True)
                ring.close(mm_)
            pe.wait_ge(s["lnew"], 1)
            product(pe, ("lnew",), "act", [
                (LNM.rearrange("p b h -> p (b h)"), C("ones", NB)[:, 0:1]),
                (C("e8", NB), S_WK[:, PAST:PAST + 1]),
                (RB64.rearrange("p b h -> p (b h)"), OHS[:, PAST:PAST + 1])], 64, 1)
            for c in range(4):
                ring.read(pe, (1, "q%d" % c))
            for i in range(NT):
                ring.read(pe, (1, "v", i))
            units = [(h, i) for h in range(AH) for i in range(4)]

            def logits(n):
                h, i = units[n]
                p0, w = (h % 2) * 64, (i + 1) * 128
                if i == 0:
                    pe.wait_ge(s["hk_in%d" % (h % 2)], 16 * (h // 2 + 1))
                if h == 0:
                    pe.wait_ge(s["mask_ready"], i + 1)
                x0 = 384 - i * 128
                product(pe, ("al", h, i), "act",
                        [(AQT[p0:p0 + 64, h // 2, i * 128:(i + 1) * 128], AKT[p0:p0 + 64, h // 2, 0:w]),
                         (C("flip"), HK[:, h % 2, x0:x0 + w]),
                         (ident, MASK[:, i, 0:w])], 128, w)

            def turn(n):
                h, i = units[n]
                pe.wait_ge(s["anorm"], n + 1)
                turn_parts(pe, ("apT", h, i), "dve",
                           [(j * 128, PR[:, n % 2, j * 128:(j + 1) * 128]) for j in range(i + 1)])

            def values(h):
                for i in range(4):
                    ring.read(pe, ("apT", h, i))
                bank = ring.open(pe, ("apv", h), "act")
                c0 = (h // 2) * 128
                for j in range(4):
                    mm_ = T.matmul(bank[:, j * 128:SEQ], VR[:, j, c0:c0 + 128], PTA[:, h % 2, j, j * 128:SEQ],
                                   start=(j == 0), stop=(j == 3))
                ring.close(mm_)

            def sample_values(b):
                if b == 0:
                    ring.read(pe, ("psT",))
                    pe.wait_ge(s["pm8"], 1)
                bank = ring.open(pe, ("spv", b), "act")
                bv = bank[:, 0:32].rearrange("p (c h) -> p c h", c=4)
                for c in range(4):
                    T.matmul(bv[:, c, :], R1["v"][:, c * 128:(c + 1) * 128], PM8[:, b, :],
                             start=(c == 0), stop=False, skip_group_check=True)
                for qd in range(4):
                    pe.wait_ge(s["v_in%d" % qd], 32 * (b + 1))
                    for j in range(2):
                        for c in range(4):
                            mm_ = T.matmul(bv[:, c, :], VV[:, qd, j, c * 128:(c + 1) * 128],
                                           PTS[:, 2 * qd + j, b * 8:b * 8 + 8], start=False,
                                           stop=(qd == 3 and j == 1), skip_group_check=True)
                    if qd < 3:
                        mm_.then_inc(s["v_used"], 1)
                ring.close(mm_)

            for n in range(len(units) + 2):
                if n < len(units):
                    logits(n)
                if n >= 2:
                    turn(n - 2)
                if n >= 7 and (n - 3) % 4 == 0:
                    values((n - 3) // 4 - 1)
                if n == SOFTMAX_AT + 2:
                    pe.wait_ge(s["snorm"], 1)
                    turn_parts(pe, ("psT",), "act", [(j * 64, LR[:, j * 128:(j + 1) * 128]) for j in range(NPG)])
                    pe.wait_ge(s["pnew"], 1)
                    product(pe, ("p8",), "dve", [(C("e64", 64), PN)], 8, 8)
                if n in VALUES_AT:
                    sample_values(VALUES_AT[n])
            values(AH - 1)

        def pe_memory(pe, l):
            units = [(h, i) for h in range(XH) for i in range(4)]
            base = 16 * l
            for c in range(4):
                ring.read(pe, (l, "qm%d" % c))
            ring.read(pe, (l, "qms"))
            turn_parts(pe, ("mqr", l), "act", [(c * 128, QMT[:, c, SEQ:TT]) for c in range(4)])

            def values(h):
                for i in range(4):
                    ring.read(pe, ("mpT", l, h, i))
                product(pe, ("mpv", l, h), "act",
                        [(VM[:, j, h * 128:(h + 1) * 128], MPT[:, h % 2, j, :]) for j in range(2)], 128, SEQ)

            for n in range(len(units) + 2):
                if n < len(units):
                    h, i = units[n]
                    product(pe, ("ml", l, h, i), "act", [(QMT[:, h, i * 128:(i + 1) * 128], KMT[:, h, :])], 128, MEM)
                if n >= 2:
                    h, i = units[n - 2]
                    pe.wait_ge(s["mnorm"], base + n - 1)
                    turn_parts(pe, ("mpT", l, h, i), "dve",
                               [(j * 128, MP[:, n % 2, j * 128:(j + 1) * 128]) for j in range(2)])
                if n >= 7 and (n - 3) % 4 == 0:
                    values((n - 3) // 4 - 1)
            values(XH - 1)
            for b in range(NB):
                pe.wait_ge(s["mqmask"], NB * l + b + 1)
                product(pe, ("mqb", l, b), "dve", [(C("ones", NB), MQM[:, b % 2, :])], 128, XW)
            pe.wait_ge(s["mk_used"], NB * (l + 1))
            turn_parts(pe, ("mlr", l), "act", [(j * 128, MLG[:, j, :]) for j in range(2)])
            pe.wait_ge(s["msnorm"], l + 1)
            turn_parts(pe, ("mps", l), "dve", [(j * 32, MLR[:, j * 128:(j + 1) * 128]) for j in range(2)])
            ring.read(pe, ("mps", l))
            pe.wait_ge(s["mv_in"], 16 * NB * (l + 1))
            bank = ring.open(pe, ("msv", l), "act")
            for b in range(NB):
                for h in range(XH):
                    for j in range(2):
                        mm_ = T.matmul(bank[:, h * NB + b:h * NB + b + 1], MV8[:, b, j, h * 128:(h + 1) * 128],
                                       MPS[:, j, b * 4 + h:b * 4 + h + 1], start=(j == 0), stop=(j == 1))
            ring.close(mm_)

        def pe_experts(pe, l):
            m = moe[l]

            def turn_tokens(par, count):
                pe.wait_ge(m["gathered%d" % par], count)
                v = XE[:, par, :].rearrange("r (p k) -> r k p", k=KD)
                for half, name in ((0, "turned_a"), (1, "turned_b")):
                    for q in range(4):
                        mm_ = T.transpose(psum[:, 4 + half, q * 128:(q + 1) * 128], v[:, 4 * half + q, :], ident)
                    mm_.then_inc(m[name], 1)

            def down(j, t):
                pe.wait_ge(m["ht_ready"], t + 1)
                if not (isinstance(t, int) and t < 1):
                    pe.wait_ge(m["out_a"], t)
                    pe.wait_ge(m["out_b"], t)
                for half in range(2):
                    for q in range(2):
                        c0 = q * D + half * 512
                        mm_ = T.matmul(psum[:, 2 + half, :], HT[:, q, :], WE[:, j, 2, c0:c0 + 512],
                                       start=(q == 0), stop=(q == 1))
                mm_.then_inc(m["down_done"], 1)

            def step(g, j, first):
                t = 4 * g + j
                pe.wait_ge(m["w_in%d" % j], 48 * (g + 1))
                pe.wait_ge(m["xe_a"], t + 1)
                pe.wait_ge(m["xe_b"], t + 1)
                if not (first and j < 2):
                    pe.wait_ge(m["h_made"], t - 1)
                wv = WE[:, j, 0:2, :].rearrange("p m (k f) -> p k m f", k=KD)
                for k in range(KD):
                    mm_ = T.matmul(psum[:, j % 2, :].rearrange("p (m f) -> p m f", m=2), XET[:, j % 2, k, :],
                                   wv[:, k], start=(k == 0), stop=(k == KD - 1))
                mm_.then_inc(m["gu_done"], 1)
                if not (first and j == 0):
                    down((j - 1) % GRP, t - 1)
                turn_tokens((j + 1) % 2, 16 * (2 * g + (j + 1) // 2 + 1))
                pe.wait_ge(m["h_made"], t + 1)
                hv_ = HH.rearrange("s (p q) -> s q p", q=2)
                for q in range(2):
                    mm_ = T.transpose(psum[:, 6, q * 128:(q + 1) * 128], hv_[:, q, :], ident)
                mm_.then_inc(m["h_turned"], 1)

            pe.wait_ge(s["table_ready"], l + 1)
            groups = pe.value_load(NGI[0:1, 0:1], min_val=0, max_val=(MTILES - NE) // GRP) + NE // GRP
            turn_tokens(0, 16)
            for j in range(GRP):
                step(0, j, True)
            with pe.Fori(1, groups) as g:
                for j in range(GRP):
                    step(g, j, False)
            down(GRP - 1, 4 * groups - 1)

        @block.tensor
        def _(pe):
            pe.wait_ge(s_cst, 16)
            pe.wait_ge(s_x, 32)
            for i, (t0, n) in enumerate(TILES):
                turn_rows(pe, X[:n, i], ("xT", 0, i), ("act", "dve"), n)
            pe.wait_ge(s_mem, 16)
            for i in range(2):
                turn_rows(pe, MEMROW[:, i], ("memT", i), ("act", "dve"), 128)

            for l in range(DEPTH):
                for i in range(2):
                    for half in range(2):
                        ring.read(pe, ("memT", i, half))
                for name in ("km", "vm"):
                    w = chunk(pe, l, name)
                    for i in range(2):
                        product(pe, (l, name, i), "act" if name == "km" else "dve",
                                [(MT[:, k, i * 128:(i + 1) * 128], w[:, k, :]) for k in range(KD)], 128, XW)
                    mark_chunk(l, name)
                for i in range(2):
                    ring.read(pe, (l, "km", i))
                for hp in range(2):
                    turn_parts(pe, (l, "kmT", hp), "dve",
                               [(h * MEM + i * 128, MKROW[:, i, (2 * hp + h) * 128:(2 * hp + h + 1) * 128])
                                for h in range(2) for i in range(2)])
                for i in range(NT):
                    for half in range(2):
                        ring.read(pe, ("xT", l, i, half))

                if l == 0:
                    pe.wait_ge(s_l0, 16 * 8)
                    project_cols(pe, 0, "gi", GW, 0, "dve", 4)
                    project_cols(pe, 0, "gf", GW, 4, "dve", 4)
                    project_rows(pe, 0, "gs", GW, 4, "dve")
                    turn_parts(pe, (0, "cwT"), "act",
                               [(4 * k, CWR[:, k * 128:(k + 1) * 128]) for k in range(KD)]
                               + [(32 + 24 * k, SCR[:, k * 128:(k + 1) * 128]) for k in range(KD)])
                    for name in ("q", "k"):
                        w = chunk(pe, 0, name)
                        for c in range(4):
                            project_cols(pe, 0, name + str(c), w, c * 128, "dve")
                        project_sample(pe, 0, name + "s", w, Q4, "dve")
                        mark_chunk(0, name)
                    pe.wait_ge(s["dmend_done"], 1)
                    bank = ring.open(pe, (0, "gcol"), "dve")
                    for st in range(4):
                        T.transpose(bank[:, 4 * st:4 * st + 4], G["a"][:, st * 128:(st + 1) * 128], ident[:4, :4])
                    for st in range(4):
                        T.transpose(bank[:, 16 + 4 * st:20 + 4 * st], G["x"][:, st * 128:(st + 1) * 128],
                                    ident[:4, :4])
                    mm_ = T.matmul(bank[:, 32:36], C("ones", 4), dmend, start=True, stop=True)
                    ring.close(mm_)
                    for name in ("v", "o"):
                        w = chunk(pe, 0, name)
                        for i in range(NT):
                            project_rows(pe, 0, name, w, i, "act")
                        mark_chunk(0, name)
                else:
                    pe.wait_ge(s_l1, 16 * 5)
                    pe_dsa_projections(pe)
                if l == 0:
                    w = chunk(pe, 0, "qm")
                    for c in range(4):
                        project_cols(pe, 0, "qm" + str(c), w, c * 128, "act")
                    project_sample(pe, 0, "qms", w, Q4, "act")
                    mark_chunk(0, "qm")
                    pe_mlstm(pe)
                else:
                    pe_dsa(pe)
                stage_end(pe, "pe")
                pe_memory(pe, l)

                ring.read(pe, ("msv", l))
                if l == 0:
                    for i in range(NT):
                        ring.read(pe, (0, "tokT", i))
                else:
                    ring.read(pe, ("apv", AH - 1))
                    ring.read(pe, ("spv", NB - 1))
                for half in range(2):
                    w = chunk(pe, l, "wo%d" % half)
                    for i, (t0, n) in enumerate(TILES):
                        product(pe, (l, "y", half, i), "dve",
                                [(CT[:, c, t0:t0 + n], w[:, c, :]) for c in range(KD)], n, 512)
                    mark_chunk(l, "wo%d" % half)
                for i, (t0, n) in enumerate(TILES):
                    pe.wait_ge(s["x_norm"], 10 * l + i + 1)
                    turn_rows(pe, X[:n, i], ("x1T", l, i), ("act", "act"), n)
                stage_end(pe, "pe")

                pe.wait_ge(s["router_in"], 64 * (l + 1))
                for i in range(NT):
                    for half in range(2):
                        ring.read(pe, ("x1T", l, i, half))
                bank = ring.open(pe, (l, "router"), "dve")
                for i, (t0, n) in enumerate(TILES):
                    for k in range(KD):
                        mm_ = T.matmul(bank[:n, i * 36:(i + 1) * 36], XT[:, k, t0:t0 + n], WR[:, k, :],
                                       start=(k == 0), stop=(k == KD - 1))
                ring.close(mm_)
                pe.wait_ge(s["route_ready"], l + 1)
                bank = ring.open(pe, (l, "before"), "dve")
                for i, (t0, n) in enumerate(TILES):
                    for j in range(i):
                        T.matmul(bank[:n, i * NE:(i + 1) * NE], C("ones")[:, :n], rt["both"][:, j, :],
                                 start=(j == 0), stop=False)
                    T.matmul(bank[:n, i * NE:(i + 1) * NE], C("before", n)[:, :n], rt["both"][:n, i, :],
                             start=(i == 0), stop=True)
                for i, (t0, n) in enumerate(TILES):
                    mm_ = T.matmul(bank[:, NT * NE:(NT + 1) * NE], C("ones", n), rt["both"][:n, i, :],
                                   start=(i == 0), stop=(i == NT - 1))
                ring.close(mm_)
                for who in ("act", "dve"):
                    pe.wait_ge(ring.freed[who], ring.count[who])
                pe_experts(pe, l)
                stage_end(pe, "pe")
                if l == 0:
                    for i, (t0, n) in enumerate(TILES):
                        pe.wait_ge(s["x_norm"], 5 + i + 1)
                        turn_rows(pe, X[:n, i], ("xT", 1, i), ("act", "act"), n)

        A = nc.scalar

        def copy_turned(act, key, dst, n):
            bank = ring.full(act, key)
            ring.free(A.activation(dst, bank[:, 0:4 * n].rearrange("p (k t) -> p k t", k=4), ACT.Copy), key)

        def act_copy(act, key, dst, scale=1.0, rows=128, c0=0, n=None, view=None, func=ACT.Copy):
            bank = ring.full(act, key)[:rows, c0:(c0 + n) if n else 512]
            if view:
                bank = view(bank)
            ring.free(A.activation(dst, bank, func, scale=scale), key)

        def act_mlstm(act):
            cut8 = lambda v: v.rearrange("p (c b) -> p c b", b=NB)
            act.wait_ge(s["gates_lin"], 1)
            seq(act, "act", A.activation(G["e"], G["e"], ACT.Exp))
            A.activation(G["lf"], G["e"], ACT.Ln, bias=1.0).then_inc(s["gates_ln"], 1)
            act.wait_ge(s["sg_lin"], 1)
            seq(act, "act", A.activation(sg[:, 8:12], sg[:, 8:12], ACT.Exp))
            A.activation(sg[:, 12:16], sg[:, 8:12], ACT.Ln, bias=1.0).then_inc(s["sg_ln"], 1)
            bank = ring.full(act, (0, "cwT"))
            A.activation(CW, bank[:, 0:32].rearrange("p (k j) -> p k j", j=4), ACT.Copy)
            ring.free(A.activation(SCT, bank[:, 32:224].rearrange("p (k j) -> p k j", j=24), ACT.Copy), (0, "cwT"))
            for c in range(8):
                act.wait_ge(s["conv_done"], c + 1)
                if c >= 2:
                    act.wait_ge(s["silu_done"], c - 1)
                A.activation(TH[:, c % 2, :], QK[:, c, 0:SEQ], ACT.Tanh, scale=0.5).then_inc(s["tanh_done"], 1)
            act.wait_ge(s["sconv_done"], 1)
            A.activation(CVS[:, 2], CVS[:, 1], ACT.Tanh, scale=0.5).then_inc(s["stanh_done"], 1)
            act.wait_ge(s["exp_lin"], 1)
            A.activation(emC, mC, ACT.Exp, scale=-1.0)
            A.activation(wendC, wendC, ACT.Exp).then_inc(s["exp_col"], 1)
            for i, (t0, n) in enumerate(TILES):
                if i < 4:
                    act_copy(act, (0, "v", i), VA[:, i, :, 0:128], view=lambda v: v.rearrange("p (h d) -> p h d", h=MH))
                else:
                    act_copy(act, (0, "v", i), VS, rows=NB)
            for i, (t0, n) in enumerate(TILES):
                bank = ring.full(act, (0, "o", i))
                ring.free(A.activation(GO[:n, i, :], bank[:n, :], ACT.Tanh, scale=0.5), (0, "o", i))
            act_queries(act, 0)
            n = 0
            for h in range(MH):
                for st in range(4):
                    w = SEQ - st * 128
                    act.wait_ge(s["arg_done"], n + 1)
                    if n >= 2:
                        ring.read(act, ("score", (n - 2) // 4, (n - 2) % 4))
                    A.activation(DD[:, n % 2, 0:w], AR[:, n % 2, 0:w], ACT.Exp).then_inc(s["decay_done"], 1)
                    n += 1
                if h:
                    for i in range(4):
                        act_copy(act, ("num", h - 1, i), NUM[:, i * 4 + h - 1, 0:129], n=129)
            for i in range(4):
                act_copy(act, ("num", MH - 1, i), NUM[:, i * 4 + MH - 1, 0:129], n=129)
            stage_end(act, "act")
            act_copy(act, ("sq",), QKR[:, 0:MW], rows=NB)
            for j in range(2):
                act_copy(act, ("su", j), UR[:, j * 512:(j + 1) * 512], rows=NB)
            for j in range(2):
                act_copy(act, ("pu", j), UPR[:, j * 512:(j + 1) * 512], rows=3)
            act.wait_ge(s["sg_lin2"], 1)
            A.activation(sg[:, 20:32], sg[:, 20:32], ACT.Exp).then_inc(s["sg_exp"], 1)
            act_copy(act, ("newC",), CS, view=lambda v: v.rearrange("p (h d) -> p h d", h=MH))
            act_copy(act, ("newn",), NNR, rows=1)
            act.wait_ge(s["var_ready"], 1)
            A.activation(hs_, hv, ACT.Sqrt).then_inc(s["std_ready"], 1)
            act.wait_ge(s["urow"], 16)
            for i, (t0, n) in enumerate(TILES):
                act_copy(act, (0, "tokT", i), CT[:, 0:4, t0:t0 + n], n=4 * n,
                         view=lambda v, n=n: v.rearrange("p (c t) -> p c t", c=4))

        def act_queries(act, l):
            for c in range(4):
                act_copy(act, (l, "qm%d" % c), QMT[:, c, 0:SEQ], scale=float(XD) ** -0.5)
            act_copy(act, (l, "qms"), QMT[:, :, SEQ:TT], scale=float(XD) ** -0.5, n=32,
                     view=lambda v: v.rearrange("p (c b) -> p c b", b=NB))

        def act_dsa(act):
            cut8 = lambda v: v.rearrange("p (c b) -> p c b", b=NB)
            for c in range(4):
                act_copy(act, (1, "q%d" % c), AQT[:, c, 0:SEQ], scale=float(AD) ** -0.5)
            act_copy(act, (1, "qs"), AQT[:, :, SEQ:TT], scale=float(AD) ** -0.5, n=32, view=cut8)
            act_copy(act, (1, "ki"), KIT[:, 0:SEQ])
            act_copy(act, (1, "kis"), KIT[:, SEQ:TT], n=NB)
            act_copy(act, ("sq1",), R1["q"], rows=NB)
            act_copy(act, ("sqi1",), R1["qi"], rows=NB)
            act_copy(act, ("ski1",), r1ki, rows=NB, n=AD)
            act_copy(act, ("qis",), QIS, rows=64, n=64, view=lambda v: v.rearrange("p (g b) -> p g b", g=8))

            def products():
                for c in range(4):
                    act_copy(act, (1, "k%d" % c), AKT[:, c, 0:SEQ])
                    yield
                act_copy(act, (1, "ks"), AKT[:, :, SEQ:TT], n=32, view=cut8)
                yield
                for i in range(NT):
                    act_copy(act, (1, "v", i), VR[:, i, :] if i < 4 else R1["v"], rows=TILES[i][1])
                    yield
                for c in range(4):
                    act_copy(act, (1, "qm%d" % c), QMT[:, c, 0:SEQ], scale=float(XD) ** -0.5)
                    yield
                act_copy(act, (1, "qms"), QMT[:, :, SEQ:TT], scale=float(XD) ** -0.5, n=32, view=cut8)
                yield

            def keys(b):
                if b >= 2:
                    ring.full(act, ("sx", b - 2, 1))
                for half in range(2):
                    act_copy(act, ("kxT", b, half), KXT[0:64, b % 2, half * 512:(half + 1) * 512], rows=64)

            product_ = products()
            keys(0)
            for b in range(NB):
                for half in range(2):
                    if b:
                        ring.full(act, ("sw", b - 1, half))
                    bank = ring.full(act, ("sx", b, half))
                    ins = A.activation(S_RL[:, half, :], bank[:8, :], ACT.Relu, scale=float(AD) ** -0.5)
                    ring.free(ins, ("sx", b, half))
                if b + 1 < NB:
                    keys(b + 1)
                next(product_)
            for _ in product_:
                pass
            for i in range(4):
                act_copy(act, ("krow1", i), KROW[:, i, :])
            act_copy(act, ("sk1",), R1["k"], rows=NB)
            act_copy(act, ("kirow",), KIROW, n=4 * AD, view=lambda v: v.rearrange("p (i d) -> p i d", i=4))
            act_copy(act, ("rbt", 0), RBT[:, 0:512], rows=8)
            act_copy(act, ("rbt", 1), RBT[:, 512:640], rows=8, n=128)
            n = 0
            for i in range(1, 4):
                w = (i + 1) * 128
                for g in range(8):
                    if n >= 2:
                        act.wait_ge(s["scored"], n - 1)
                    bank = ring.full(act, ("ix", i, g))
                    ins = A.activation(RLU[:, n % 2, 0:w], bank[:, 0:w], ACT.Relu, scale=float(AD) ** -0.5)
                    ring.free(ins, ("ix", i, g))
                    n += 1
            for half in range(2):
                act_copy(act, ("lr", half), LR[:, half * 512:(half + 1) * 512], rows=64)
            act_copy(act, ("lnew",), LR[:, PAST:PAST + 1], rows=64, n=1)
            units = [(h, i) for h in range(AH) for i in range(4)]
            act.wait_ge(s["krow_out"], 64)

            def out_heads(h):
                p0 = (h % 2) * 64
                bank = ring.full(act, ("apv", h))
                ring.free(A.activation(CT[p0:p0 + 64, h // 2, 0:SEQ], bank[p0:p0 + 64, :], ACT.Copy), ("apv", h))

            def out_sample(b):
                bank = ring.full(act, ("spv", b))
                for half in range(2):
                    at = bank[half * 64:half * 64 + 64, half:half + 1]
                    src = bass.AP(at.tensor, at.offset, [at.ap[0], [10, 4]])
                    ins = A.activation(CT[half * 64:half * 64 + 64, 0:4, SEQ + b], src, ACT.Copy)
                ring.free(ins, ("spv", b))

            for n in range(len(units) + 2):
                if n < len(units):
                    h, i = units[n]
                    w = (i + 1) * 128
                    act.wait_ge(s["amax"], n + 1)
                    if n >= 2:
                        ring.full(act, ("apT",) + units[n - 2])
                    bank = ring.full(act, ("al", h, i))
                    ring.free(A.activation(PR[:, n % 2, 0:w], bank[:, 0:w], ACT.Exp, bias=anm[:, n:n + 1],
                                           accum_out=asm[:, n:n + 1]), ("al", h, i))
                if n >= 7 and (n - 3) % 4 == 0:
                    out_heads((n - 3) // 4 - 1)
                if n == SOFTMAX_AT:
                    act.wait_ge(s["smax"], 1)
                    A.activation(LR[:, 0:PAST + 1], LR[:, 0:PAST + 1], ACT.Exp, bias=sst[:, 0:1],
                                 accum_out=sst[:, 1:2]).then_inc(s["sexp"], 1)
                if n == SOFTMAX_AT + 2:
                    act_copy(act, ("psT",), PTS, view=lambda v: v.rearrange("p (j r) -> p j r", r=64))
                if n in VALUES_AT:
                    out_sample(VALUES_AT[n])
            out_heads(AH - 1)

        def act_memory(act, l):
            units = [(h, i) for h in range(XH) for i in range(4)]
            base = 16 * l
            act_copy(act, ("mqr", l), MQR, rows=NB)
            for n, (h, i) in enumerate(units):
                act.wait_ge(s["mmax"], base + n + 1)
                if n >= 2:
                    ring.full(act, ("mpT", l) + units[n - 2])
                bank = ring.full(act, ("ml", l, h, i))
                ring.free(A.activation(MP[:, n % 2, :], bank[:, 0:MEM], ACT.Exp, bias=mnm[:, n:n + 1],
                                       accum_out=msm[:, n:n + 1]), ("ml", l, h, i))
                if i == 3 and h >= 1:
                    act_copy(act, ("mpv", l, h - 1), CT[:, 4 + h - 1, 0:SEQ])
            act_copy(act, ("mpv", l, XH - 1), CT[:, 4 + XH - 1, 0:SEQ])
            act_copy(act, ("mlr", l), MLR, rows=32, n=MEM)
            act.wait_ge(s["msmax"], l + 1)
            A.activation(MLR, MLR, ACT.Exp, bias=mst[:, 0:1], accum_out=mst[:, 1:2]).then_inc(s["msexp"], 1)
            act_copy(act, ("msv", l), CT[:, 4:8, SEQ:TT], n=32, view=lambda v: v.rearrange("p (h b) -> p h b", b=NB))

        def act_experts(act, l):
            m = moe[l]

            def put_half(g, j, first):
                t = 4 * g + j
                act.wait_ge(m["down_done"], t)
                if not (first and j < 3):
                    act.wait_ge(m["put%d" % ((j - 1) % 2)], 16 * (2 * g + (j - 3) // 2 + 1))
                A.activation(OUT[:, (j - 1) % 2, 0:512], psum[:, 2, :], ACT.Copy).then_inc(m["out_a"], 1)

            def tokens(par, count):
                act.wait_ge(m["turned_a"], count)
                A.activation(XET[:, par, 0:4, :], psum[:, 4, :].rearrange("p (k t) -> p k t", k=4),
                             ACT.Copy).then_inc(m["xe_a"], 1)

            def step(g, j, first):
                t = 4 * g + j
                act.wait_ge(m["gu_done"], t + 1)
                if not (first and j < 2):
                    act.wait_ge(m["h_made"], t - 1)
                A.activation(SG[:, j % 2, :], psum[:, j % 2, 0:DE], ACT.Silu).then_inc(m["silu"], 1)
                if not (first and j == 0):
                    put_half(g, j, first)
                tokens((j + 1) % 2, t + 2)

            act.wait_ge(s["table_ready"], l + 1)
            groups = act.value_load(NGI[0:1, 0:1], min_val=0, max_val=(MTILES - NE) // GRP) + NE // GRP
            tokens(0, 1)
            for j in range(GRP):
                step(0, j, True)
            with act.Fori(1, groups) as g:
                for j in range(GRP):
                    step(g, j, False)
            put_half(groups, 0, False)

        @block.scalar
        def _(act):
            for i, (t0, n) in enumerate(TILES):
                copy_turned(act, ("xT", 0, i, 0), XT[:, 0:4, t0:t0 + n], n)
            for i in range(2):
                copy_turned(act, ("memT", i, 0), MT[:, 0:4, i * 128:(i + 1) * 128], 128)
            for l in range(DEPTH):
                for i in range(2):
                    act_copy(act, (l, "km", i), MKROW[:, i, :])
                if l == 0:
                    act_mlstm(act)
                else:
                    act_dsa(act)
                stage_end(act, "act")
                act_memory(act, l)
                act.wait_ge(s["lnstd"], 4 * l + 1)
                A.activation(std, vare, ACT.Sqrt).then_inc(s["lnstd"], 1)
                for i, (t0, n) in enumerate(TILES):
                    for half in range(2):
                        copy_turned(act, ("x1T", l, i, half), XT[:, 4 * half:4 * half + 4, t0:t0 + n], n)
                stage_end(act, "act")
                act.wait_ge(s["router_lin"], l + 1)
                A.activation(rg["e"], rg["c"], ACT.Exp).then_inc(s["router_exp"], 1)
                act.wait_ge(s["e2_lin"], l + 1)
                A.activation(rs["e2"], rs["d"], ACT.Exp).then_inc(s["e2_exp"], 1)
                act_experts(act, l)
                act.wait_ge(s["lnstd"], 4 * l + 3)
                A.activation(std, vare, ACT.Sqrt).then_inc(s["lnstd"], 1)
                stage_end(act, "act")
                if l == 0:
                    for i, (t0, n) in enumerate(TILES):
                        for half in range(2):
                            copy_turned(act, ("xT", 1, i, half), XT[:, 4 * half:4 * half + 4, t0:t0 + n], n)

        V = nc.vector

        def copy_turned_dve(dve, key, dst, n):
            bank = ring.full(dve, key)
            ring.free(V.tensor_copy(dst, bank[:, 0:4 * n].rearrange("p (k t) -> p k t", k=4)), key)

        def dve_copy(dve, key, dst, rows=128, n=512, c0=0, view=None):
            bank = ring.full(dve, key)[:rows, c0:c0 + n]
            if view:
                bank = view(bank)
            ring.free(V.tensor_copy(dst, bank), key)

        def heads(v, n=MH):
            return v.rearrange("p (h d) -> p h d", h=n)

        def dve_gates(dve):
            dve.wait_ge(s["gates_ln"], 1)
            V.memset(G["M"], 1.0)
            seq(dve, "dve", V.scalar_tensor_tensor(G["lf"], G["x"], 0.0, G["lf"], ALU.min, ALU.subtract))
            seq(dve, "dve", V.tensor_tensor_scan(G["B"], G["M"], G["lf"], 0.0, ALU.mult, ALU.add))
            seq(dve, "dve", V.tensor_tensor(G["a"], G["a"], G["B"], ALU.subtract))
            seq(dve, "dve", V.tensor_tensor_scan(G["M"], G["a"], G["a"], 0.0, ALU.max, ALU.max))
            seq(dve, "dve", V.tensor_tensor(G["x"], G["B"], G["M"], ALU.add))
            V.tensor_scalar(dmend, ident[:4, :4], G["M"][:, SEQ - 1:SEQ], None, ALU.mult).then_inc(s["dmend_done"], 1)
            dve.wait_ge(s["sg_ln"], 1)
            seq(dve, "dve", V.scalar_tensor_tensor(sg[:, 8:12], sg[:, 4:8], 0.0, sg[:, 12:16], ALU.min, ALU.subtract))
            seq(dve, "dve", V.tensor_tensor(sg[:, 12:16], sg[:, 8:12], sg[:, 44:48], ALU.add))
            seq(dve, "dve", V.tensor_tensor(sg[:, 16:20], sg[:, 12:16], sg[:, 0:4], ALU.max))
            V.tensor_tensor(sg[:, 20:24], sg[:, 0:4], sg[:, 16:20], ALU.subtract)
            V.tensor_tensor(sg[:, 24:28], sg[:, 12:16], sg[:, 16:20], ALU.subtract)
            V.tensor_scalar(sg[:, 28:32], sg[:, 16:20], -1.0, None, ALU.mult).then_inc(s["sg_lin2"], 1)

        def dve_mlstm(dve):
            dve.wait_ge(s_l0, 16 * 8)
            bank = ring.full(dve, (0, "gi"))
            ring.free(V.tensor_scalar(G["a"], bank[:4, :], GB[:4, 0:1], None, ALU.add), (0, "gi"))
            bank = ring.full(dve, (0, "gf"))
            ring.free(V.tensor_scalar(G["x"], bank[:4, :], GB[:4, 1:2], None, ALU.add), (0, "gf"))
            ring.read(dve, (0, "gf"))
            V.scalar_tensor_tensor(G["e"], G["x"], -1.0, G["x"], ALU.mult, ALU.min).then_inc(s["gates_lin"], 1)
            bank = ring.full(dve, (0, "gs", 4))
            ring.free(V.tensor_tensor(sg[:, 0:8], bank[:NB, 0:8], GB[:NB, 2:10], ALU.add), (0, "gs", 4))
            ring.read(dve, (0, "gs", 4))
            V.scalar_tensor_tensor(sg[:, 8:12], sg[:, 4:8], -1.0, sg[:, 4:8], ALU.mult, ALU.min).then_inc(s["sg_lin"], 1)
            ring.read(dve, (0, "cwT"))
            for half, name in enumerate(("q", "k")):
                for j in range(4):
                    c = 4 * half + j
                    bank = ring.full(dve, (0, name + str(j)))
                    seq(dve, "dve", V.tensor_scalar(QK[:, c, 0:SEQ], bank, CW[:, c, 3:4], None, ALU.mult))
                    for back in (1, 2, 3):
                        ins = V.scalar_tensor_tensor(QK[:, c, back:SEQ], bank[:, 0:SEQ - back],
                                                     CW[:, c, 3 - back:4 - back], QK[:, c, back:SEQ], ALU.mult, ALU.add)
                        if back < 3:
                            seq(dve, "dve", ins)
                    ins.then_inc(s["conv_done"], 1)
                    ring.free(V.tensor_copy(UTAIL[:, c, 0:3], bank[:, SEQ - 3:SEQ]), (0, name + str(j)))
                dve_copy(dve, (0, name + "s"), UST[:, 4 * half:4 * half + 4, :], n=32,
                         view=lambda v: v.rearrange("p (c b) -> p c b", b=NB))
                if half == 0:
                    dve_gates(dve)
            ring.read(dve, (0, "ks"))
            state = SCT.rearrange("p c (b j) -> p c b j", j=3)
            seq(dve, "dve", V.tensor_tensor(CVS[:, 1], UST, bc(CW[:, :, 3], 2, NB), ALU.mult))
            for j in range(3):
                seq(dve, "dve", V.tensor_tensor(CVS[:, 0], state[:, :, :, j], bc(CW[:, :, j], 2, NB), ALU.mult))
                ins = V.tensor_tensor(CVS[:, 1], CVS[:, 1], CVS[:, 0], ALU.add)
                if j < 2:
                    seq(dve, "dve", ins)
            ins.then_inc(s["sconv_done"], 1)
            dve_copy(dve, (0, "gcol"), gcol[:, 0:36], n=36)
            ring.read(dve, (0, "gcol"))
            V.tensor_tensor(wendC.rearrange("p (i h) -> p i h", h=4), aC.rearrange("p (i h) -> p i h", h=4),
                            bc(mendC, 1, 4), ALU.subtract).then_inc(s["exp_lin"], 1)
            dve.wait_ge(s["stanh_done"], 1)
            seq(dve, "dve", V.tensor_scalar(CVS[:, 2], CVS[:, 2], 0.5, 0.5, ALU.mult, ALU.add))
            V.tensor_tensor(QK[:, :, SEQ:TT], CVS[:, 1], CVS[:, 2], ALU.mult).then_inc(s["ssilu_done"], 1)
            units = [(h, st) for h in range(MH) for st in range(4)]
            ring.full(dve, (0, "qms"))
            dve.wait_ge(s["silu_done"], 8)

            def scores(n):
                h, st = units[n]
                w = SEQ - st * 128
                dve.wait_ge(s["decay_cut"], n + 1)
                if h >= 2 and st == 0:
                    ring.full(dve, ("num", h - 2, 3))
                bank = ring.full(dve, ("score", h, st))
                ring.free(V.scalar_tensor_tensor(PT[:, h % 2, st, 0:w], bank[:, 0:w], float(MD) ** -0.5,
                                                 DD[:, n % 2, 0:w], ALU.mult, ALU.mult), ("score", h, st))

            for n, (h, st) in enumerate(units):
                w = SEQ - st * 128
                if st == 0:
                    if n:
                        scores(n - 1)
                    dve_copy(dve, ("negm", h), TH[:, h % 2, :])
                    ring.read(dve, ("negm", h))
                if n >= 2:
                    dve.wait_ge(s["decay_done"], n - 1)
                V.tensor_scalar(AR[:, n % 2, 0:w], TH[:, h % 2, st * 128:SEQ], aC[:, st * 4 + h:st * 4 + h + 1], 0.0,
                                ALU.add, ALU.min).then_inc(s["arg_done"], 1)
                if st:
                    scores(n - 1)
            scores(len(units) - 1)
            ring.read(dve, ("num", MH - 1, 3))
            dve.wait_ge(s["exp_col"], 1)
            seq(dve, "dve", V.scalar_tensor_tensor(dn, NUM[:, :, 128], -1.0, NUM[:, :, 128], ALU.mult, ALU.max))
            seq(dve, "dve", V.tensor_tensor(dn, dn, emC, ALU.max))
            seq(dve, "dve", V.reciprocal(dn, dn))
            tv = TOK[:, 0:4, :].rearrange("p i (h d) -> p (i h) d", h=MH)
            V.tensor_tensor(tv, NUM[:, :, 0:128], bc(dn, 2, 128), ALU.mult)
            stage_end(dve, "dve")

            for st in range(4):
                bank = ring.full(dve, ("krow", st))
                for h in range(MH):
                    ins = V.tensor_scalar(KW[:, st, h * 128:(h + 1) * 128], bank[:, h * 128:(h + 1) * 128],
                                          wendC[:, st * 4 + h:st * 4 + h + 1], float(MD) ** -0.5, ALU.mult, ALU.mult)
                ring.free(ins, ("krow", st))
            bank = ring.full(dve, ("sk",))
            ring.free(V.tensor_scalar(QKR[:, MW:2 * MW], bank[:NB, :], float(MD) ** -0.5, None, ALU.mult), ("sk",))
            ring.read(dve, ("sk",))
            ring.read(dve, ("sq",))
            dve.wait_ge(s["sg_exp"], 1)
            dve.wait_ge(s["n_in"], 16)
            d_, wp_, em_ = sg[:, 20:24], sg[:, 24:28], sg[:, 28:32]
            qk_, qn_, den_, c_ = sg[:, 32:36], sg[:, 36:40], sg[:, 40:44], sg[:, 48:52]
            seq(dve, "dve", V.tensor_tensor(WPM, C("e84", NB).rearrange("p (b h) -> p b h", b=NB), bc(wp_, 1, NB), ALU.mult))
            seq(dve, "dve", V.tensor_tensor(heads(R["vd"]), heads(VS), bc(d_, 2, MD), ALU.mult))
            seq(dve, "dve", V.tensor_tensor(R["t"], QKR[:, 0:MW], QKR[:, MW:2 * MW], ALU.mult))
            seq(dve, "dve", V.tensor_reduce(qk_, heads(R["t"]), AX.X, ALU.add))
            seq(dve, "dve", V.tensor_tensor(R["t"], QKR[:, 0:MW], R["n"], ALU.mult))
            seq(dve, "dve", V.tensor_reduce(qn_, heads(R["t"]), AX.X, ALU.add))
            seq(dve, "dve", V.tensor_tensor(heads(R["n"]), heads(R["n"]), bc(wp_, 2, MD), ALU.mult))
            seq(dve, "dve", V.tensor_tensor(heads(R["t2"]), heads(QKR[:, MW:2 * MW]), bc(d_, 2, MD), ALU.mult))
            seq(dve, "dve", V.tensor_tensor(R["n"], R["n"], R["t2"], ALU.add))
            V.tensor_tensor(c_, qk_, d_, ALU.mult).then_inc(s["wp_ready"], 1)

            def mask(b):
                if b >= 2:
                    ring.full(dve, ("vk", b - 2))
                V.tensor_scalar(QMK[:, b % 2, :], QKR[:, 0:MW], ident[:NB, b:b + 1], None, ALU.mult)
                V.tensor_scalar(VMK[:, b % 2, :], R["vd"], ident[:NB, b:b + 1], None, ALU.mult).then_inc(s["masked"], 1)

            dve_copy(dve, ("wp",), WPB.rearrange("p b h -> p (b h)"), n=32)
            mask(0)
            mask(1)
            dve.wait_ge(s["c_in"], 16 * NB)
            ring.read(dve, ("wp",))
            for b in range(NB):
                bank = ring.full(dve, ("qb", b))
                ring.free(V.tensor_tensor(CTMP, CIN[:, b, :], bank, ALU.mult), ("qb", b))
                ring.read(dve, ("qb", b))
                ins = V.tensor_reduce(CQ[:, b, :], heads(CTMP), AX.X, ALU.add)
                if b == NB - 1:
                    ins.then_inc(s["cq_done"], 1)
                seq(dve, "dve", V.tensor_tensor(heads(CIN[:, b, :]), heads(CIN[:, b, :]), bc(WPB[:, b, :], 2, MD), ALU.mult))
                bank = ring.full(dve, ("vk", b))
                ring.free(V.tensor_tensor(CIN[:, b, :], CIN[:, b, :], bank, ALU.add), ("vk", b))
                if b + 2 < NB:
                    mask(b + 2)
            seq(dve, "dve", V.tensor_tensor(heads(R["t2"]), heads(VS), bc(c_, 2, MD), ALU.mult))
            bank = ring.full(dve, ("cqT",))
            ring.free(V.tensor_tensor(heads(R["t"]), heads(bank[:NB, :]), bc(wp_, 2, MD), ALU.mult), ("cqT",))
            ring.read(dve, ("cqT",))
            seq(dve, "dve", V.tensor_tensor(R["t"], R["t"], R["t2"], ALU.add))
            seq(dve, "dve", V.tensor_tensor(den_, wp_, qn_, ALU.mult))
            seq(dve, "dve", V.tensor_tensor(den_, den_, c_, ALU.add))
            seq(dve, "dve", V.scalar_tensor_tensor(den_, den_, -1.0, den_, ALU.mult, ALU.max))
            seq(dve, "dve", V.tensor_tensor(den_, den_, em_, ALU.max))
            seq(dve, "dve", V.reciprocal(den_, den_))
            seq(dve, "dve", V.tensor_tensor(heads(TOK[:NB, 4, :]), heads(R["t"]), bc(den_, 2, MD), ALU.mult))
            seq(dve, "dve", V.memset(MV, 1.0))
            for i, (t0, n) in enumerate(TILES):
                for h in range(MH):
                    ins = V.bn_stats(ST[:n, i * 4 + h, :], TOK[:n, i, h * 128:(h + 1) * 128])
            seq(dve, "dve", ins)
            for i, (t0, n) in enumerate(TILES):
                for h in range(MH):
                    ins = V.bn_aggr(MV[:n, i * 4 + h, :], ST[:n, i * 4 + h, :])
            seq(dve, "dve", ins)
            V.tensor_scalar(hv, MV[:, :, 1], EPS, None, ALU.add).then_inc(s["var_ready"], 1)
            dve.wait_ge(s["std_ready"], 1)
            seq(dve, "dve", V.reciprocal(hr, hs_))
            dve.wait_ge(s["go_ready"], NT)
            for rows_, v, g in ((128, tv, slice(0, 16)),
                                (NB, TOK[:NB, 4:5, :].rearrange("p i (h d) -> p (i h) d", h=MH), slice(16, 20))):
                seq(dve, "dve", V.tensor_tensor(v, v, bc(MV[:rows_, g, 0], 2, 128), ALU.subtract))
                seq(dve, "dve", V.tensor_tensor(v, v, bc(hr[:rows_, g], 2, 128), ALU.mult))
            V.tensor_tensor(TOK[:, 0:4, :], TOK[:, 0:4, :], GO[:, 0:4, :], ALU.mult)
            V.tensor_tensor(TOK[:NB, 4, :], TOK[:NB, 4, :], GO[:NB, 4, :], ALU.mult).then_inc(s["tok_ready"], 1)

        def dve_topk(dve, scores_, work, rounds):
            for r in range(rounds):
                src = scores_ if r == 0 else work
                seq(dve, "dve", V.max(m8[:src.shape[0]] if src.shape[0] == 128 else s8[:src.shape[0]], src))
                seq(dve, "dve", V.match_replace(work, m8[:src.shape[0]] if src.shape[0] == 128 else s8[:src.shape[0]],
                                                src, TAKEN))

        def dve_dsa(dve):
            cut8 = lambda v: v.rearrange("p (c b) -> p c b", b=NB)
            for c in range(4):
                dve_copy(dve, (1, "qi%d" % c), QIT[:, c, 0:SEQ])
            dve_copy(dve, (1, "qis"), QIT[:, :, SEQ:TT], n=32, view=cut8)
            for i, (t0, n) in reversed(list(enumerate(TILES))):
                bank = ring.full(dve, (1, "wi", i))
                ring.free(V.tensor_scalar(WIP[:, i, :] if i < 4 else r1wi, bank[:n, 0:8], float(8) ** -0.5, None,
                                          ALU.mult), (1, "wi", i))
            dve_copy(dve, ("wT",), WT, rows=NB, n=NB)
            ring.read(dve, ("wT",))
            V.tensor_tensor(WM, C("del88", NB).rearrange("p (b c) -> p b c", b=NB), bc(WT, 2, NB),
                            ALU.mult).then_inc(s["wm_ready"], 1)

            def mask(b):
                if b >= 2:
                    ring.full(dve, ("sqb", b - 2))
                V.tensor_scalar(S_QM[:, b % 2, :], R1["q"], ident[:NB, b:b + 1], None, ALU.mult).then_inc(s["sqm"], 1)

            ring.read(dve, ("sq1",))
            mask(0)
            mask(1)
            for b in range(NB):
                bank = ring.full(dve, ("sqb", b))
                for qd in range(4):
                    n = 4 * b + qd
                    dve.wait_ge(s["kv_in%d" % (n % 4)], 32 * (n // 4 + 1))
                    ins = V.tensor_tensor(KV[:, n % 4], KV[:, n % 4], bc(bank, 1, 2), ALU.mult)
                    if qd == 3:
                        ring.free(ins, ("sqb", b))
                        ring.read(dve, ("sqb", b))
                    else:
                        seq(dve, "dve", ins)
                    V.tensor_reduce(LG[:, 2 * qd:2 * qd + 2, b * 8:b * 8 + 8],
                                    KV[:, n % 4].rearrange("p j (h d) -> p j h d", h=8), AX.X,
                                    ALU.add).then_inc(s["kv_done"], 1)
                if b + 2 < NB:
                    mask(b + 2)
                for half in range(2):
                    bank = ring.full(dve, ("sw", b, half))
                    cols = slice(half * 512, (half + 1) * 512)
                    if b == 0:
                        ins = V.tensor_copy(S_SC[:, cols], bank[:NB, :])
                    else:
                        ring.read(dve, ("sw", b - 1, half))
                        ins = V.tensor_tensor(S_SC[:, cols], S_SC[:, cols], bank[:NB, :], ALU.add)
                    ring.free(ins, ("sw", b, half))
            ring.read(dve, ("sw", NB - 1, 1))
            ring.read(dve, ("ski1",))
            seq(dve, "dve", V.tensor_tensor(heads(S_T, 8), heads(R1["qi"], 8), bc(r1ki, 1, 8), ALU.mult))
            seq(dve, "dve", V.tensor_reduce(LN8, heads(S_T, 8), AX.X, ALU.add))
            seq(dve, "dve", V.tensor_scalar(LN8, LN8, float(AD) ** -0.5, 0.0, ALU.mult, ALU.max))
            seq(dve, "dve", V.tensor_tensor(LN8, LN8, r1wi, ALU.mult))
            seq(dve, "dve", V.tensor_reduce(S_SC[:, PAST:PAST + 1], LN8, AX.X, ALU.add))
            dve_topk(dve, S_SC[:, 0:PAST + 1], S_WK[:, 0:PAST + 1], TOPK_S // 8)
            V.tensor_scalar(S_WK[:, 0:PAST + 1], S_WK[:, 0:PAST + 1], -2.5e38, NEG, ALU.is_gt,
                            ALU.mult).then_inc(s["smask"], 1)
            ring.read(dve, ("sk1",))
            seq(dve, "dve", V.tensor_tensor(S_T, R1["q"], R1["k"], ALU.mult))
            seq(dve, "dve", V.tensor_reduce(LN8, heads(S_T, 8), AX.X, ALU.add))
            e8 = C("e8", NB).rearrange("p (b h) -> p b h", b=NB)
            V.tensor_tensor(LNM, e8, bc(LN8, 1, NB), ALU.mult).then_inc(s["lnew"], 1)
            V.tensor_copy(MASK[:, 0, 0:128], C("causal")).then_inc(s["mask_ready"], 1)
            for i in range(1, 4):
                w = (i + 1) * 128
                dve.wait_ge(s["cut"], i)
                dve_topk(dve, SC[:, i % 2, 0:w], SC[:, i % 2, 0:w], TOPK_P // 8)
                V.tensor_scalar(MASK[:, i, 0:w], SC[:, i % 2, 0:w], -2.5e38, NEG, ALU.is_gt,
                                ALU.mult).then_inc(s["mask_ready"], 1)
            units = [(h, i) for h in range(AH) for i in range(4)]
            ring.full(dve, (1, "qms"))
            for n in range(len(units) + 2):
                if n < len(units):
                    h, i = units[n]
                    bank = ring.full(dve, ("al", h, i))
                    V.tensor_reduce(anm[:, n:n + 1], bank[:, 0:(i + 1) * 128], AX.X, ALU.max,
                                    negate=True).then_inc(s["amax"], 1)
                if 1 <= n <= len(units):
                    h, i = units[n - 1]
                    w = (i + 1) * 128
                    ring.read(dve, ("al", h, i))
                    seq(dve, "dve", V.reciprocal(ars[:, n - 1:n], asm[:, n - 1:n]))
                    V.tensor_scalar(PR[:, (n - 1) % 2, 0:w], PR[:, (n - 1) % 2, 0:w], ars[:, n - 1:n], None,
                                    ALU.mult).then_inc(s["anorm"], 1)
                if n >= 2:
                    h, i = units[n - 2]
                    if h >= 2 and i == 0:
                        ring.full(dve, ("apv", h - 2))
                    dve_copy(dve, ("apT", h, i), PTA[:, h % 2, 0:i + 1, i * 128:(i + 1) * 128], n=(i + 1) * 128,
                             view=lambda v: v.rearrange("p (j t) -> p j t", t=128))
                if n == SOFTMAX_AT:
                    ring.read(dve, ("lnew",))
                    V.tensor_reduce(sst[:, 0:1], LR[:, 0:PAST + 1], AX.X, ALU.max, negate=True).then_inc(s["smax"], 1)
                    dve.wait_ge(s["sexp"], 1)
                    seq(dve, "dve", V.reciprocal(sst[:, 2:3], sst[:, 1:2]))
                    V.tensor_scalar(LR[:, 0:PAST + 1], LR[:, 0:PAST + 1], sst[:, 2:3], None,
                                    ALU.mult).then_inc(s["snorm"], 1)
                    dve.wait_ge(s["snorm"], 1)
                    V.tensor_scalar(PN, C("hsel", 64), LR[:, PAST:PAST + 1], None, ALU.mult).then_inc(s["pnew"], 1)
                if n == SOFTMAX_AT + 2:
                    dve_copy(dve, ("p8",), P8, rows=NB, n=8)
                    ring.read(dve, ("p8",))
                    V.tensor_tensor(PM8, e8, bc(P8, 1, NB), ALU.mult).then_inc(s["pm8"], 1)

        def dve_memory(dve, l):
            units = [(h, i) for h in range(XH) for i in range(4)]

            def mask(b):
                if b >= 2:
                    ring.full(dve, ("mqb", l, b - 2))
                V.tensor_scalar(MQM[:, b % 2, :], MQR, ident[:NB, b:b + 1], None, ALU.mult).then_inc(s["mqmask"], 1)

            for n in range(len(units) + 2):
                if n < len(units):
                    bank = ring.full(dve, ("ml", l) + units[n])
                    V.tensor_reduce(mnm[:, n:n + 1], bank[:, 0:MEM], AX.X, ALU.max, negate=True).then_inc(s["mmax"], 1)
                if 1 <= n <= len(units):
                    ring.read(dve, ("ml", l) + units[n - 1])
                    seq(dve, "dve", V.reciprocal(mrs[:, n - 1:n], msm[:, n - 1:n]))
                    V.tensor_scalar(MP[:, (n - 1) % 2, :], MP[:, (n - 1) % 2, :], mrs[:, n - 1:n], None,
                                    ALU.mult).then_inc(s["mnorm"], 1)
                if n >= 2:
                    h, i = units[n - 2]
                    if h >= 2 and i == 0:
                        ring.full(dve, ("mpv", l, h - 2))
                    dve_copy(dve, ("mpT", l, h, i), MPT[:, h % 2, :, i * 128:(i + 1) * 128], n=MEM,
                             view=lambda v: v.rearrange("p (j t) -> p j t", t=128))
            ring.read(dve, ("mqr", l))
            mask(0)
            mask(1)
            for b in range(NB):
                dve.wait_ge(s["mk_in%d" % (b % 2)], 16 * (4 * l + b // 2 + 1))
                bank = ring.full(dve, ("mqb", l, b))
                ring.free(V.tensor_tensor(MK2[:, b % 2], MK2[:, b % 2], bc(bank, 1, 2), ALU.mult), ("mqb", l, b))
                ring.read(dve, ("mqb", l, b))
                V.tensor_reduce(MLG[:, :, b * 4:b * 4 + 4], MK2[:, b % 2].rearrange("p j (h d) -> p j h d", h=XH),
                                AX.X, ALU.add).then_inc(s["mk_used"], 1)
                if b + 2 < NB:
                    mask(b + 2)
            ring.read(dve, ("mlr", l))
            V.tensor_reduce(mst[:, 0:1], MLR, AX.X, ALU.max, negate=True).then_inc(s["msmax"], 1)
            dve.wait_ge(s["msexp"], l + 1)
            seq(dve, "dve", V.reciprocal(mst[:, 2:3], mst[:, 1:2]))
            V.tensor_scalar(MLR, MLR, mst[:, 2:3], None, ALU.mult).then_inc(s["msnorm"], 1)
            dve_copy(dve, ("mps", l), MPS.rearrange("p j r -> p (j r)"), n=64)

        def dve_norm(dve, nth, gb):
            for i, (t0, n) in enumerate(TILES):
                V.bn_stats(stats[:n, 0], X[:n, i, 0:512])
                seq(dve, "dve", V.bn_stats(stats[:n, 1], X[:n, i, 512:1024]))
                seq(dve, "dve", V.bn_aggr(moments[:n, i, :], stats[:n].rearrange("p a b -> p (a b)")))
            V.tensor_scalar(vare, moments[:, :, 1], EPS, None, ALU.add).then_inc(s["lnstd"], 1)
            dve.wait_ge(s["lnstd"], 2 * nth + 2)
            seq(dve, "dve", V.reciprocal(rstd, std))
            for i, (t0, n) in enumerate(TILES):
                seq(dve, "dve", V.tensor_scalar(X[:n, i], X[:n, i], moments[:n, i, 0:1], rstd[:n, i:i + 1],
                                                ALU.subtract, ALU.mult))
                seq(dve, "dve", V.tensor_tensor(X[:n, i], X[:n, i], gb[:n, 0], ALU.mult))
                V.tensor_tensor(X[:n, i], X[:n, i], gb[:n, 1], ALU.add).then_inc(s["x_norm"], 1)

        def dve_route(dve, l):
            S = lambda ins: seq(dve, "dve", ins)
            S(V.memset(RL, 0.0))
            S(V.memset(rt["pos"], 0.0))
            dve.wait_ge(s["router_in"], 64 * (l + 1))
            bank = ring.full(dve, (l, "router"))
            V.tensor_tensor(RL[:, 0:4, :], bank[:, 0:144].rearrange("p (i e) -> p i e", e=36), bc(BR, 1, 4), ALU.add)
            ring.free(V.tensor_tensor(RL[:NB, 4, :], bank[:NB, 144:180], BR[:NB], ALU.add), (l, "router"))
            ring.read(dve, (l, "router"))
            GL, EL = RL[:, :, 0:NG], RL[:, :, NG:NG + NE]
            iota = bc(C("iota"), 1, NT)

            def first_max(logit, top_, eq, c, oh, n):
                S(V.tensor_tensor(eq, logit, bc(top_, 2, n), ALU.is_equal))
                S(V.scalar_tensor_tensor(c, eq, -64.0, iota[:, :, 0:n], ALU.mult, ALU.add))
                S(V.tensor_reduce(rs["mn"], c, AX.X, ALU.min))
                S(V.tensor_tensor(oh, c, bc(rs["mn"], 2, n), ALU.is_equal))

            S(V.tensor_reduce(rs["gm"], GL, AX.X, ALU.max))
            V.tensor_tensor(rg["c"], GL, bc(rs["gm"], 2, NG), ALU.subtract).then_inc(s["router_lin"], 1)
            dve.wait_ge(s["router_exp"], l + 1)
            S(V.tensor_reduce(rs["gw"], rg["e"], AX.X, ALU.add))
            S(V.reciprocal(rs["gw"], rs["gw"]))
            first_max(GL, rs["gm"], rg["eq"], rg["c"], rg["oh"], NG)
            S(V.tensor_scalar(rg["c"], rg["oh"], -1.0, -NEG, ALU.add, ALU.mult))
            S(V.tensor_tensor(rt["l2"].rearrange("p i (g e) -> p i g e", g=NG), EL.rearrange("p i (g e) -> p i g e", g=NG),
                              bc(rg["c"], 3, EPG), ALU.add))
            S(V.tensor_reduce(rs["m1"], rt["l2"], AX.X, ALU.max))
            first_max(rt["l2"], rs["m1"], rt["eq"], rt["c"], rt["oh1"], NE)
            S(V.tensor_scalar(rs["e"], rs["mn"], 64.0, None, ALU.add))
            S(V.scalar_tensor_tensor(rt["l3"], rt["oh1"], 3.0 * NEG, rt["l2"], ALU.mult, ALU.add))
            S(V.tensor_reduce(rs["m2"], rt["l3"], AX.X, ALU.max))
            V.tensor_tensor(rs["d"], rs["m2"], rs["m1"], ALU.subtract).then_inc(s["e2_lin"], 1)
            first_max(rt["l3"], rs["m2"], rt["eq"], rt["c"], rt["oh2"], NE)
            V.tensor_tensor(rt["both"], rt["oh1"], rt["oh2"], ALU.add).then_inc(s["route_ready"], 1)
            dve.wait_ge(s["e2_exp"], l + 1)
            S(V.tensor_scalar(rs["w1"], rs["e2"], 1.0, None, ALU.add))
            S(V.reciprocal(rs["w1"], rs["w1"]))
            S(V.tensor_tensor(rs["g1"], rs["gw"], rs["w1"], ALU.mult))
            S(V.tensor_tensor(rs["g2"], rs["g1"], rs["e2"], ALU.mult))

            bank = ring.full(dve, (l, "before"))
            V.tensor_copy(rt["pos"][:, 0:4, :], bank[:, 0:128].rearrange("p (i e) -> p i e", e=NE))
            V.tensor_copy(rt["pos"][:NB, 4, :], bank[:NB, 128:160])
            ring.free(V.tensor_copy(cnt, bank[:, 160:192]), (l, "before"))
            ring.read(dve, (l, "before"))
            S(V.tensor_scalar(over, cnt, 128.0, None, ALU.is_gt))
            for k in (2, 3, 4):
                S(V.scalar_tensor_tensor(over, cnt, 128.0 * k, over, ALU.is_gt, ALU.add))
            S(V.tensor_tensor_scan(incl, C("ones")[:, 0:NE], over, 0.0, ALU.mult, ALU.add))
            S(V.tensor_tensor(excl, incl, over, ALU.subtract))
            S(V.tensor_scalar(ngf[:, 0:1], incl[:, NE - 1:NE], 0.0, None, ALU.is_gt))
            S(V.scalar_tensor_tensor(ngf[:, 1:2], incl[:, NE - 1:NE], float(GRP), ngf[:, 0:1], ALU.is_gt, ALU.add))
            V.tensor_copy(NGI, ngf[:, 1:2])
            S(V.tensor_tensor(et1, bc(excl, 1, 8), bc(C("iota8"), 2, NE), ALU.is_le))
            S(V.tensor_tensor(et2, bc(incl, 1, 8), bc(C("iota8"), 2, NE), ALU.is_gt))
            S(V.tensor_tensor(et1, et1, et2, ALU.mult))
            S(V.tensor_tensor(et1, et1, bc(C("iota"), 1, 8), ALU.mult))
            S(V.tensor_reduce(et3, et1, AX.X, ALU.add))
            S(V.tensor_copy(ETI, et3))
            for r, oh in ((0, "oh1"), (1, "oh2")):
                if r:
                    S(V.tensor_scalar(rs["e"], rs["mn"], 64.0, None, ALU.add))
                S(V.tensor_tensor(rt["t"], rt[oh], rt["pos"], ALU.mult))
                S(V.tensor_reduce(rs["p"], rt["t"], AX.X, ALU.add))
                S(V.tensor_tensor(rt["t"], rt[oh], bc(excl, 1, NT), ALU.mult))
                S(V.tensor_reduce(rs["ot"], rt["t"], AX.X, ALU.add))
                S(V.tensor_scalar(rs["q"], rs["p"], 128.0, None, ALU.is_ge))
                for k in (2, 3, 4):
                    S(V.scalar_tensor_tensor(rs["q"], rs["p"], 128.0 * k, rs["q"], ALU.is_ge, ALU.add))
                S(V.tensor_tensor(rs["t"], rs["ot"], rs["q"], ALU.add))
                S(V.scalar_tensor_tensor(rs["t"], rs["t"], float(NE - 1), rs["e"], ALU.add, ALU.subtract))
                S(V.scalar_tensor_tensor(rs["t"], rs["q"], 0.0, rs["t"], ALU.is_gt, ALU.mult))
                S(V.tensor_tensor(rs["t"], rs["t"], rs["e"], ALU.add))
                S(V.scalar_tensor_tensor(rs["p"], rs["q"], -128.0, rs["p"], ALU.mult, ALU.add))
                S(V.scalar_tensor_tensor(rs["row"], rs["t"], 128.0, rs["p"], ALU.mult, ALU.add))
                S(V.scalar_tensor_tensor(rs["cell"], rs["p"], float(LW), rs["t"], ALU.mult, ALU.add))
                S(V.tensor_copy(ROWI[:, r, :], rs["row"]))
                S(V.tensor_copy(CELLI[:, r, :], rs["cell"]))
            V.tensor_copy(TOKI, C("tokid")).then_inc(s["table_ready"], 1)

        def dve_experts(dve, l):
            m = moe[l]

            def put_half(g, j, first):
                dve.wait_ge(m["down_done"], 4 * g + j)
                if not (first and j < 3):
                    dve.wait_ge(m["put%d" % ((j - 1) % 2)], 16 * (2 * g + (j - 3) // 2 + 1))
                V.tensor_copy(OUT[:, (j - 1) % 2, 512:1024], psum[:, 3, :]).then_inc(m["out_b"], 1)

            def tokens(par, count):
                dve.wait_ge(m["turned_b"], count)
                V.tensor_copy(XET[:, par, 4:8, :], psum[:, 5, :].rearrange("p (k t) -> p k t", k=4)).then_inc(m["xe_b"], 1)

            def step(g, j, first):
                t = 4 * g + j
                dve.wait_ge(m["silu"], t + 1)
                if not (first and j == 0):
                    dve.wait_ge(m["h_turned"], t)
                V.tensor_tensor(HH, SG[:, j % 2, :], psum[:, j % 2, DE:2 * DE], ALU.mult).then_inc(m["h_made"], 1)
                if not (first and j == 0):
                    put_half(g, j, first)
                tokens((j + 1) % 2, t + 2)
                dve.wait_ge(m["h_turned"], t + 1)
                V.tensor_copy(HT.rearrange("p q t -> p (q t)"), psum[:, 6, 0:256]).then_inc(m["ht_ready"], 1)

            groups = dve.value_load(NGI[0:1, 0:1], min_val=0, max_val=(MTILES - NE) // GRP) + NE // GRP
            tokens(0, 1)
            for j in range(GRP):
                step(0, j, True)
            with dve.Fori(1, groups) as g:
                for j in range(GRP):
                    step(g, j, False)
            put_half(groups, 0, False)
            return groups

        @block.vector
        def _(dve):
            seq(dve, "dve", V.memset(small, 1.0))
            for i, (t0, n) in enumerate(TILES):
                copy_turned_dve(dve, ("xT", 0, i, 1), XT[:, 4:8, t0:t0 + n], n)
            for i in range(2):
                copy_turned_dve(dve, ("memT", i, 1), MT[:, 4:8, i * 128:(i + 1) * 128], 128)
            for l in range(DEPTH):
                for i in range(2):
                    dve_copy(dve, (l, "vm", i), VM[:, i, :])
                for hp in range(2):
                    dve_copy(dve, (l, "kmT", hp), KMT[:, 2 * hp:2 * hp + 2, :].rearrange("p h s -> p (h s)"))
                if l == 0:
                    dve_mlstm(dve)
                else:
                    dve_dsa(dve)
                stage_end(dve, "dve")
                dve_memory(dve, l)
                for half in range(2):
                    for i, (t0, n) in enumerate(TILES):
                        bank = ring.full(dve, (l, "y", half, i))
                        cols = slice(half * 512, (half + 1) * 512)
                        ring.free(V.scalar_tensor_tensor(X[:n, i, cols], X[:n, i, cols], ALPHA, bank[:n, :],
                                                         ALU.mult, ALU.add), (l, "y", half, i))
                ring.read(dve, (l, "y", 1, NT - 1))
                dve.wait_ge(s_ln, 32 * (l + 1))
                dve_norm(dve, 2 * l, lng)
                stage_end(dve, "dve")
                dve_route(dve, l)
                groups = dve_experts(dve, l)
                dve.wait_ge(s["x1_out"], 16 * NT * (l + 1))
                dve.wait_ge(moe[l]["put0"], 32 * groups)
                dve.wait_ge(moe[l]["put1"], 32 * groups)
                V.tensor_copy(ngf[:, 0:1], ngf[:, 1:2]).then_inc(s["experts_out"], 1)
                for i, (t0, n) in enumerate(TILES):
                    ins = V.tensor_scalar(X[:n, i], X[:n, i], ALPHA, None, ALU.mult)
                seq(dve, "dve", ins)
                for i, (t0, n) in enumerate(TILES):
                    dve.wait_ge(s["y_in%d" % (i % 2)], 32 * ((3 if i % 2 == 0 else 2) * l + i // 2 + 1))
                    seq(dve, "dve", V.scalar_tensor_tensor(X[:n, i], YG[:n, i % 2, 0, :], rs["g1"][:n, i:i + 1],
                                                           X[:n, i], ALU.mult, ALU.add))
                    V.scalar_tensor_tensor(X[:n, i], YG[:n, i % 2, 1, :], rs["g2"][:n, i:i + 1], X[:n, i],
                                           ALU.mult, ALU.add).then_inc(s["y_used"], 1)
                dve.wait_ge(s["y_used"], NT * (l + 1))
                dve.wait_ge(s["lnf_in"], 32 * (l + 1))
                dve_norm(dve, 2 * l + 1, lnf)
                stage_end(dve, "dve")

        P = nc.gpsimd

        def store(pool, out, in_):
            stored[0] += 1
            pool.dma_start(out, in_).then_inc(s_st, 16)

        def pool_stage_end(pool):
            pool.wait_ge(s_st, 16 * stored[0])
            stage_end(pool, "pool")

        def pool_mlstm(pool):
            P.memset(VA[:, :, :, 128:130], 1.0).then_inc(s["vones"], 1)
            for c in range(8):
                pool.wait_ge(s["tanh_done"], c + 1)
                seq(pool, "pool", P.tensor_scalar(TH[:, c % 2, :], TH[:, c % 2, :], 0.5, 0.5, ALU.mult, ALU.add))
                P.tensor_tensor(QK[:, c, 0:SEQ], QK[:, c, 0:SEQ], TH[:, c % 2, :], ALU.mult).then_inc(s["silu_done"], 1)
            pool.wait_ge(s_l0, 16 * 8)
            for i, (t0, n) in enumerate(TILES):
                ring.read(pool, (0, "o", i))
                seq(pool, "pool", P.tensor_scalar(GO[:n, i], GO[:n, i], 0.5, 0.5, ALU.mult, ALU.add))
                P.tensor_tensor(GO[:n, i], GO[:n, i], NGB[:n], ALU.mult).then_inc(s["go_ready"], 1)
            for n in range(16):
                pool.wait_ge(s["decay_done"], n + 1)
                P.affine_select(out=DD[:, n % 2, 0:128], in_=DD[:, n % 2, 0:128], pattern=[[1, 128]],
                                compare_op=ALU.is_ge, fill=0.0, base=0, channel_multiplier=-1).then_inc(s["decay_cut"], 1)
            pool.wait_ge(s["dmend_done"], 1)
            store(pool, o["state_m_prompt"][0, 0].unsqueeze(1), G["x"][:, SEQ - 1:SEQ])
            pool_stage_end(pool)
            store(pool, o["state_m_sample"][0], sg[:, 16:20])
            for j in range(2):
                ring.read(pool, ("su", j))
            pool.dma_start(o["state_conv_sample"][0, :, 2, :], UR).then_inc(s["urow"], 16)
            store(pool, o["state_conv_sample"][0, :, 0:2, :], a["state_conv"][0, :, 1:3, :])
            for j in range(2):
                ring.read(pool, ("pu", j))
            store(pool, o["state_conv_prompt"][0, 0], UPR)
            ring.read(pool, ("newC",))
            store(pool, o["state_C_prompt"][0, 0].rearrange("h v k -> v h k"), CS)
            ring.read(pool, ("newn",))
            store(pool, o["state_n_prompt"][0].rearrange("b h k -> b (h k)"), NNR)
            pool.wait_ge(s["wp_ready"], 1)
            store(pool, o["state_n_sample"][0].rearrange("b h k -> b (h k)"), R["n"])
            for b in range(NB):
                ring.read(pool, ("vk", b))
                store(pool, o["state_C_sample"][0, b].rearrange("h v k -> v h k"), heads(CIN[:, b, :]))

        def pool_dsa(pool):
            for i in range(4):
                ring.read(pool, (1, "v", i))
                store(pool, o["new_v_prompt"][0, 0, i * 128:(i + 1) * 128].rearrange("t h d -> t (h d)"), VR[:, i, :])
            ring.read(pool, (1, "v", 4))
            store(pool, o["new_v_sample"][0, :, 0].rearrange("t h d -> t (h d)"), R1["v"])
            for i in range(4):
                ring.read(pool, ("krow1", i))
                pool.dma_start(o["new_k_prompt"][0, 0, i * 128:(i + 1) * 128].rearrange("t h d -> t (h d)"),
                               KROW[:, i, :]).then_inc(s["krow_out"], 16)
            ring.read(pool, ("sk1",))
            store(pool, o["new_k_sample"][0, :, 0].rearrange("t h d -> t (h d)"), R1["k"])
            ring.read(pool, ("kirow",))
            store(pool, o["new_kidx_prompt"][0, 0].rearrange("(i p) d -> p i d", p=128), KIROW)
            ring.read(pool, ("ski1",))
            store(pool, o["new_kidx_sample"][0, :, 0], r1ki)
            for j in range(2):
                ring.read(pool, ("rbt", j))
            pool.dma_start(scratch["bias"], RBT).then_inc(s["rbt_out"], 16)
            seq(pool, "pool", P.tensor_copy(RB64, bc(RB, 1, NB)))
            ring.read(pool, (1, "wi", 0))
            n = 0
            for i in range(1, 4):
                w, w0 = (i + 1) * 128, i * 128
                if i == 3:
                    pool.wait_ge(s["mask_ready"], 2)
                for g in range(8):
                    ring.read(pool, ("ix", i, g))
                    if g == 0:
                        ins = P.tensor_scalar(SC[:, i % 2, 0:w], RLU[:, n % 2, 0:w], WIP[:, i, g:g + 1], None, ALU.mult)
                    else:
                        seq(pool, "pool", P.tensor_scalar(RLU[:, n % 2, 0:w], RLU[:, n % 2, 0:w], WIP[:, i, g:g + 1],
                                                          None, ALU.mult))
                        pool.wait_ge(s["scored"], n)
                        ins = P.tensor_tensor(SC[:, i % 2, 0:w], SC[:, i % 2, 0:w], RLU[:, n % 2, 0:w], ALU.add)
                    ins.then_inc(s["scored"], 1)
                    n += 1
                pool.wait_ge(s["scored"], 8 * i)
                P.affine_select(out=SC[:, i % 2, w0:w], in_=SC[:, i % 2, w0:w], pattern=[[-1, 128]],
                                compare_op=ALU.is_ge, fill=NONE, base=0, channel_multiplier=1).then_inc(s["cut"], 1)

        def pool_experts(pool, l):
            m = moe[l]
            xd = scratch["x1_%d" % l]
            seq(pool, "pool", P.memset(LZ.bitcast(F32), 0.0))
            ids = scratch["ids_%d" % l]
            pool.dma_start(ids.rearrange("(p t) a -> p (t a)", t=LW), LZ).then_inc(s["zeroed"], 16)
            pool.wait_ge(s["table_ready"], l + 1)
            pool.wait_ge(s["zeroed"], 16 * (l + 1))
            for r in range(2):
                for i, (t0, n) in enumerate(TILES):
                    P.indirect_dma_start(ids, bass.IndirectOffsetOnAxis(ap=CELLI[:n, r, i:i + 1], axis=0),
                                         TOKI[:n, i:i + 1], None).then_inc(s["scattered"], 16)
            pool.wait_ge(s["scattered"], 16 * 2 * NT * (l + 1))
            pool.dma_start(LST, ids.rearrange("(p t) a -> p (t a)", t=LW)).then_inc(s["ids_in"], 16)
            pool.wait_ge(s["ids_in"], 16 * (l + 1))
            groups = pool.value_load(NGI[0:1, 0:1], min_val=0, max_val=(MTILES - NE) // GRP) + NE // GRP

            def pick(t, j):
                P.tensor_copy(IDX[:, j:j + 1], LST[:, bass.ds(t, 1)]).then_inc(m["picked"], 1)

            def fetch(t, j, first):
                pool.wait_ge(m["picked"], t + 1)
                if not (first and t < 2):
                    pool.wait_ge(m["turned_a"], t - 1)
                    pool.wait_ge(m["turned_b"], t - 1)
                pick(t + 1, (j + 1) % GRP)
                P.indirect_dma_start(XE[:, j % 2, :], None, xd, bass.IndirectOffsetOnAxis(ap=IDX[:, j:j + 1], axis=0)
                                     ).then_inc(m["gathered%d" % (j % 2)], 16)

            pick(0, 0)
            for t in range(GRP + 1):
                fetch(t, t % GRP, True)
            with pool.Fori(1, groups) as g:
                for j in range(1, GRP + 1):
                    fetch(4 * g + j, j % GRP, False)
            pool.wait_ge(s["experts_out"], l + 1)
            for i, (t0, n) in enumerate(TILES):
                if i >= 2:
                    pool.wait_ge(s["y_used"], NT * l + i - 1)
                for r in range(2):
                    P.indirect_dma_start(YG[:n, i % 2, r, :], None, scratch["y"],
                                         bass.IndirectOffsetOnAxis(ap=ROWI[:n, r, i:i + 1], axis=0)
                                         ).then_inc(s["y_in%d" % (i % 2)], 16)

        @block.gpsimd
        def _(pool):
            pool.wait_ge(s_x, 32)
            for t in range(NE, MTILES, 4):
                store(pool, scratch["y"][t * 128:(t + 4) * 128, :].rearrange("(i p) d -> p i d", p=128), X[:, 0:4, :])
            for l in range(DEPTH):
                for i in range(2):
                    ring.read(pool, (l, "km", i))
                    store(pool, o["mem_k_prompt"][l, 0, i * 128:(i + 1) * 128].rearrange("s h d -> s (h d)"),
                          MKROW[:, i, :])
                    ring.read(pool, (l, "vm", i))
                    store(pool, o["mem_v_prompt"][l, 0, i * 128:(i + 1) * 128].rearrange("s h d -> s (h d)"),
                          VM[:, i, :])
                if l == 0:
                    pool_mlstm(pool)
                else:
                    pool_dsa(pool)
                pool_stage_end(pool)
                for i, (t0, n) in enumerate(TILES):
                    pool.wait_ge(s["x_norm"], 10 * l + i + 1)
                    pool.dma_start(scratch["x1_%d" % l][t0:t0 + n, :], X[:n, i]).then_inc(s["x1_out"], 16)
                pool.wait_ge(s["x1_out"], 16 * NT * (l + 1))
                pool_stage_end(pool)
                pool_experts(pool, l)
                if l == DEPTH - 1:
                    for i, (t0, n) in enumerate(TILES):
                        pool.wait_ge(s["x_norm"], 10 * l + 5 + i + 1)
                        if i < 4:
                            store(pool, o["y_prompt"][0, t0:t0 + n, :], X[:n, i])
                        else:
                            store(pool, o["y_sample"][:, 0, :], X[:n, i])
                pool_stage_end(pool)

        def sync_small0(sp):
            w = a["w_in_mlstm"][0]
            sp.dma_start(GW, w[:, 2048:2056].rearrange("(p k) n -> p k n", k=KD)).then_inc(s_l0, 16)
            sp.dma_start(CWR, a["conv_mlstm"][0]).then_inc(s_l0, 16)
            sp.dma_start(SCR, a["state_conv"][0].rearrange("b j c -> (b j) c")).then_inc(s_l0, 16)
            g = a["b_gates_mlstm"][0]
            sp.dma_start(GB[:4, 0:1], g[0:4].unsqueeze(1)).then_inc(s_l0, 16)
            sp.dma_start(GB[:4, 1:2], g[4:8].unsqueeze(1)).then_inc(s_l0, 16)
            sp.dma_start(GB[:NB, 2:10], g.partition_broadcast(NB)).then_inc(s_l0, 16)
            sp.dma_start(NGB, a["norm_mlstm"][0].partition_broadcast(128)).then_inc(s_l0, 16)
            sp.dma_start(sg[:, 44:48], a["state_m"][0]).then_inc(s_l0, 16)

        def sync_chunk(sp, l, name):
            i = chunk_no[(l, name)]
            if i >= 2:
                sp.wait_ge(ring.filled, chunk_last[i - 2])
            sp.dma_start(WS[:, i % 2], chunks[i][2]).then_inc(chunk_in[i % 2], 16)

        def sync_norm(sp, l):
            for q, n in enumerate(("ln_mix_g", "ln_mix_b")):
                sp.dma_start(lng[:, q, :], a[n][l].partition_broadcast(128)).then_inc(s_ln, 16)

        def sync_dsa(sp):
            def page(n):
                return sp.value_load(PTB[0:1, n:n + 1], min_val=0, max_val=NPOOL - 1)

            def index_keys(b):
                if b >= 2:
                    ring.full(sp, ("kxT", b - 2, 1))
                for j in range(NPG):
                    sp.dma_start(KIX[:, b % 2, j, :],
                                 a["cache_kidx"][0, bass.ds(page(b * NPG + j), 1)].rearrange("a r d -> (a r) d")
                                 ).then_inc(s["kix_in%d" % (b % 2)], 16)

            def pages(cache, at, dst, arrived):
                for j in range(2):
                    sp.dma_start(dst[:, j, :], cache[0, bass.ds(page(at + j), 1)].rearrange("a r h d -> (a r) (h d)")
                                 ).then_inc(arrived, 16)

            def keys(b):
                for q in range(4):
                    n = 4 * b + q
                    if b >= 1:
                        sp.wait_ge(s["kv_done"], n - 3)
                    pages(a["cache_k"], 2 * n, KV[:, q], s["kv_in%d" % q])

            def values(b):
                for q in range(4):
                    if b == 0 and q == 0:
                        sp.wait_ge(ring.filled, chunk_last[chunk_no[(1, "qm")]])
                    if b >= 1:
                        if q < 3:
                            sp.wait_ge(s["v_used"], 3 * (b - 1) + q + 1)
                        else:
                            ring.full(sp, ("spv", b - 1))
                    pages(a["cache_v"], 8 * b + 2 * q, VV[:, q], s["v_in%d" % q])

            def bias(h):
                if h >= 2:
                    ring.full(sp, ("al", h - 2, 3))
                v = scratch["bias"][h, 0:512]
                sp.dma_start(HK[:, h % 2, :], bass.AP(v.tensor, v.offset, [[1, 128], [1, 512]])
                             ).then_inc(s["hk_in%d" % (h % 2)], 16)

            for name in ("vm", "q", "qi"):
                sync_chunk(sp, 1, name)
            sp.wait_ge(s_l1, 16 * 5)
            index_keys(0)
            keys(0)
            index_keys(1)
            sync_chunk(sp, 1, "k")
            sync_chunk(sp, 1, "v")
            for b in range(1, NB):
                if b + 1 < NB:
                    index_keys(b + 1)
                keys(b)
                if b == 6:
                    sync_chunk(sp, 1, "qm")
            sync_chunk(sp, 1, "wo0")
            values(0)
            sp.wait_ge(s["rbt_out"], 16)
            sp.dma_start(OHS, a["tables"][:, 0:PAST + 2]).then_inc(s["ohs_in"], 16)
            sp.wait_ge(s["kv_done"], 4 * NB)
            steps = sorted([(4 * h - 4, bias, h) for h in range(AH)] + [(3 * b + 6, values, b) for b in range(1, NB)],
                           key=lambda v: v[0])
            for _, load, n in steps:
                load(n)
            ring.full(sp, ("p8",))
            sync_norm(sp, 1)
            ring.full(sp, ("spv", NB - 1))
            sync_chunk(sp, 1, "wo1")

        def sync_memory(sp, l):
            def keys(b):
                if b >= 2:
                    sp.wait_ge(s["mk_used"], NB * l + b - 1)
                sp.dma_start(MK2[:, b % 2], a["cache_mem_k"][l, b].rearrange("(j p) h d -> p j (h d)", p=128)
                             ).then_inc(s["mk_in%d" % (b % 2)], 16)

            keys(0)
            keys(1)
            for b in range(NB):
                sp.dma_start(MV8[:, b], a["cache_mem_v"][l, b].rearrange("(j p) h d -> p j (h d)", p=128)
                             ).then_inc(s["mv_in"], 16)
            for b in range(2, NB):
                keys(b)

        def sync_experts(sp, l):
            m = moe[l]
            up, gate, dn_ = (a[n][l] for n in ("w_exp_up", "w_exp_gate", "w_exp_down"))

            def load(j, e):
                def pick(w):
                    return w[e] if isinstance(e, int) else w[bass.ds(e, 1)].rearrange("a r n -> (a r) n")
                for q, (w, k) in enumerate(((gate, KD), (up, KD), (dn_, 2))):
                    sp.dma_start(WE[:, j, q, :], pick(w).rearrange("(p k) n -> p (k n)", k=k)
                                 ).then_inc(m["w_in%d" % j], 16)

            def put(g, j):
                t = 4 * g + j
                sp.wait_ge(m["out_a"], t + 1)
                sp.wait_ge(m["out_b"], t + 1)
                yd = scratch["y"]
                dst = yd[t * 128:(t + 1) * 128, :] if isinstance(t, int) else yd[bass.ds(t * 128, 128), :]
                sp.dma_start(dst, OUT[:, j % 2, :]).then_inc(m["put%d" % (j % 2)], 16)

            for j in range(GRP):
                load(j, j)
            with sp.Fori(0, NE // GRP - 1) as g:
                for j in range(GRP):
                    sp.wait_ge(m["down_done"], 4 * g + j + 1)
                    load(j, 4 * g + j + GRP)
                    put(g, j)
            sp.wait_ge(s["table_ready"], l + 1)
            groups = sp.value_load(NGI[0:1, 0:1], min_val=0, max_val=(MTILES - NE) // GRP) + NE // GRP
            for j in range(GRP - 1):
                put(NE // GRP - 1, j)
            with sp.If(groups > NE // GRP):
                with sp.Fori(NE // GRP, groups) as g:
                    for j in range(GRP):
                        sp.wait_ge(m["down_done"], 4 * g + j - GRP + 1)
                        load(j, sp.value_load(ETI[0:1, bass.ds(4 * g + j - NE, 1)], min_val=0, max_val=NE - 1))
                    put(g - 1, GRP - 1)
                    for j in range(GRP - 1):
                        put(g, j)
            put(groups - 1, GRP - 1)

        @block.sync
        def _(sp):
            sp.dma_start(cst, a["constants"]).then_inc(s_cst, 16)
            sp.dma_start(X[:, 0:4, :], a["x_prompt"][0].rearrange("(i p) d -> p i d", p=128)).then_inc(s_x, 16)
            sp.dma_start(X[:NB, 4, :], a["x_sample"][:, 0, :]).then_inc(s_x, 16)
            sp.dma_start(MEMROW, a["mem_prompt"][0].rearrange("(i p) d -> p i d", p=128)).then_inc(s_mem, 16)
            nst = 0
            for l in range(DEPTH):
                sync_chunk(sp, l, "km")
                if l == 0:
                    sync_small0(sp)
                else:
                    w = a["w_in_dsa"][0].rearrange("(p k) n -> p k n", k=KD)
                    sp.dma_start(KW1[:, :, 0:64], w[:, :, 2048:2112]).then_inc(s_l1, 16)
                    sp.dma_start(KW1[:, :, 64:136], w[:, :, 2048:2120]).then_inc(s_l1, 16)
                    sp.dma_start(OHP, a["tables"][:, PAST + 2:PAST + 642]).then_inc(s_l1, 16)
                    sp.dma_start(RB, a["rel_bias"]).then_inc(s_l1, 16)
                    sp.dma_start(PTB, a["page_table"].rearrange("b n -> (b n)").unsqueeze(0)).then_inc(s_l1, 16)
                if l == 0:
                    for name in ("vm", "q", "k", "v", "o", "qm"):
                        sync_chunk(sp, l, name)
                    ring.full(sp, ("memT", 1, 1))
                    sync_norm(sp, l)
                if l == 0:
                    sp.wait_ge(stage_done, 4)
                    sp.dma_start(R["n"], a["state_n"][0].rearrange("b h k -> b (h k)")).then_inc(s["n_in"], 16)
                    for b in range(NB):
                        sp.dma_start(heads(CIN[:, b, :]), a["state_C"][0, b].rearrange("h v k -> v h k")
                                     ).then_inc(s["c_in"], 16)
                    nst = 2
                else:
                    sync_dsa(sp)
                    nst = 5
                if l == 0:
                    for name in ("wo0", "wo1"):
                        sync_chunk(sp, l, name)
                sp.wait_ge(stage_done, 4 * nst)
                sync_memory(sp, l)
                sp.wait_ge(stage_done, 4 * (nst + 1))
                wr = WR
                sp.dma_start(wr[:, :, 0:NG], a["w_router_group"][l].rearrange("(p k) n -> p k n", k=KD)).then_inc(s["router_in"], 16)
                sp.dma_start(wr[:, :, NG:36], a["w_router_expert"][l].rearrange("(p k) n -> p k n", k=KD)).then_inc(s["router_in"], 16)
                sp.dma_start(BR[:, 0:NG], a["b_router_group"][l].partition_broadcast(128)).then_inc(s["router_in"], 16)
                sp.dma_start(BR[:, NG:36], a["b_router_expert"][l].partition_broadcast(128)).then_inc(s["router_in"], 16)
                for q, n in enumerate(("ln_ffn_g", "ln_ffn_b")):
                    sp.dma_start(lnf[:, q, :], a[n][l].partition_broadcast(128)).then_inc(s["lnf_in"], 16)
                sync_experts(sp, l)
                sp.wait_ge(stage_done, 4 * (nst + 2))


INS = ["x_prompt", "x_sample", "cache_k", "cache_v", "cache_kidx", "state_C", "state_n", "state_m", "state_conv",
       "cache_mem_k", "cache_mem_v", "page_table", "mem_prompt", "w_in_mlstm", "b_gates_mlstm", "conv_mlstm",
       "norm_mlstm", "w_in_dsa", "rel_bias", "w_mem_kv", "w_out", "ln_mix_g", "ln_mix_b", "ln_ffn_g", "ln_ffn_b",
       "w_router_group", "b_router_group", "w_router_expert", "b_router_expert", "w_exp_up", "w_exp_gate",
       "w_exp_down"]
OUTS = [("y_prompt", (1, SEQ, D)), ("y_sample", (NB, 1, D)),
        ("new_k_prompt", (1, 1, SEQ, AH, AD)), ("new_v_prompt", (1, 1, SEQ, AH, AD)),
        ("new_kidx_prompt", (1, 1, SEQ, AD)),
        ("new_k_sample", (1, NB, 1, AH, AD)), ("new_v_sample", (1, NB, 1, AH, AD)),
        ("new_kidx_sample", (1, NB, 1, AD)),
        ("state_C_prompt", (1, 1, MH, MD, MD)), ("state_n_prompt", (1, 1, MH, MD)), ("state_m_prompt", (1, 1, MH)),
        ("state_conv_prompt", (1, 1, 3, 2 * MW)),
        ("state_C_sample", (1, NB, MH, MD, MD)), ("state_n_sample", (1, NB, MH, MD)), ("state_m_sample", (1, NB, MH)),
        ("state_conv_sample", (1, NB, 3, 2 * MW)),
        ("mem_k_prompt", (DEPTH, 1, MEM, XH, XD)), ("mem_v_prompt", (DEPTH, 1, MEM, XH, XD))]


def kernel(**inputs):
    import numpy as np
    import concourse.bacc as bacc
    from concourse.bass_utils import run_bass_kernel_spmd

    nc = bacc.Bacc("TRN2", target_bir_lowering=False, num_devices=1)
    arrays, a, o, scratch = {}, {}, {}, {}
    table, buckets = constants()
    named = {n: np.ascontiguousarray(inputs[n]) for n in INS}
    named["constants"], named["tables"] = table, buckets
    for name, v in named.items():
        arrays[f"in_{name}"] = v
        a[name] = nc.dram_tensor(f"in_{name}", v.shape, mybir.dt.from_np(v.dtype), kind="ExternalInput").ap()
    for name, shape in OUTS:
        o[name] = nc.dram_tensor(f"out_{name}", shape, F32, kind="ExternalOutput").ap()
    scratch["bias"] = nc.dram_tensor("bias_table", (AH, 640), F32, kind="Internal").ap()
    for l in range(DEPTH):
        scratch["x1_%d" % l] = nc.dram_tensor("x1_%d" % l, (TT, D), F32, kind="Internal").ap()
        scratch["ids_%d" % l] = nc.dram_tensor("token_ids_%d" % l, (128 * LW, 1), U32, kind="Internal").ap()
    scratch["y"] = nc.dram_tensor("expert_out", (MTILES * 128, D), F32, kind="Internal").ap()
    build(nc, a, o, scratch)
    r = run_bass_kernel_spmd(nc, [arrays], core_ids=[0])
    return tuple(r.results[0][f"out_{name}"] for name, _ in OUTS)
```

```python
from contextlib import ExitStack

import concourse.bass as bass
from concourse import mybir

ALU = mybir.AluOpType
ACT = mybir.ActivationFunctionType
AX = mybir.AxisListType
F32 = mybir.dt.float32
I32 = mybir.dt.int32
U32 = mybir.dt.uint32

D = 1024
KD = D // 128
SEQ = 512
NB = 8
TT = SEQ + NB
TILES = [(0, 128), (128, 128), (256, 128), (384, 128), (512, NB)]
NT = len(TILES)
DEPTH = 2
MH, MD, MW = 4, 128, 512
AH, AD, AW = 8, 64, 512
MEM, XH, XD, XW = 256, 4, 128, 512
PAST, PAGE = 1024, 128
NPG = PAST // PAGE
TOPK_P = min(256, SEQ // 4)
TOPK_S = min(256, (PAST + 1) // 4)
NG, EPG, NE, DE = 4, 8, 32, 256
ALPHA = float((2 * DEPTH) ** 0.25)
EPS = 1e-5
NEG = -1e30
NONE = -2e38
TAKEN = -3e38
MTILES = NE + 8
LW = MTILES + 4
GRP = 4


CST = [("ident", 128), ("flip", 128), ("causal", 128), ("ones", 128), ("before", 128), ("del88", 64),
       ("iota", NE), ("e8", 64), ("e84", 32), ("seln", 4 * 128), ("hsel", 8), ("e64", 8), ("tokid", NT),
       ("iota8", 8), ("h32", 4), ("e32", 8)]


def offsets(parts):
    out, at = {}, 0
    for name, n in parts:
        out[name] = (at, n)
        at += n
    return out, at


def constants():
    import math
    import numpy as np
    off, width = offsets(CST)
    c = np.zeros((128, width), np.float32)
    p = np.arange(128)[:, None]

    def put(name, value):
        a, n = off[name]
        c[:value.shape[0], a:a + n] = value

    j = np.arange(128)[None, :]
    put("ident", (p == j) * 1.0)
    put("flip", (p + j == 127) * 1.0)
    put("causal", np.where(j > p, NEG, 0.0))
    put("ones", np.ones((128, 128)))
    put("before", (p < j) * 1.0)
    put("del88", np.tile(np.eye(8).reshape(1, 64), (128, 1)))
    put("iota", np.tile(np.arange(NE)[None], (128, 1)))
    put("e8", (np.arange(8)[:, None] == np.arange(64)[None] // 8) * 1.0)
    put("e84", (np.arange(8)[:, None] == np.arange(32)[None] // 4) * 1.0)
    put("seln", -np.repeat(np.eye(4), 128, axis=1))
    put("hsel", (np.arange(64)[:, None] % 8 == np.arange(8)[None]) * 1.0)
    put("e64", (np.arange(64)[:, None] // 8 == np.arange(8)[None]) * 1.0)
    put("tokid", 128.0 * np.arange(NT)[None] + p)
    put("iota8", np.tile(np.arange(8)[None], (128, 1)))
    put("h32", (np.arange(32)[:, None] % 4 == np.arange(4)[None]) * 1.0)
    put("e32", (np.arange(32)[:, None] // 4 == np.arange(8)[None]) * 1.0)

    def bucket(dist):
        d = np.maximum(dist, 0)
        far = 16 + (np.log(np.maximum(d, 1).astype(np.float32) / np.float32(16))
                    / np.float32(math.log(8)) * np.float32(16)).astype(np.int32)
        return np.where(d < 16, d, np.minimum(far, 31))

    b = np.arange(32)[:, None]
    t = np.concatenate([
        bucket(PAST - np.arange(PAST))[None] == b,
        np.tile(b == 0, (1, 2)),
        bucket(SEQ - 1 - np.arange(640))[None] == b,
    ], axis=1).astype(np.float32)
    return c, t


class Region:

    def __init__(self, tensor, start, end):
        self.tensor, self.at, self.end = tensor, start, end

    def take(self, *dims, rows=128, dtype=F32):
        n = 1
        for d in dims:
            n *= d
        assert self.at + n <= self.end, (self.at, n, self.end)
        v = self.tensor[:rows, self.at:self.at + n]
        self.at += n
        if dtype != F32:
            v = v.bitcast(dtype)
        if len(dims) == 2:
            v = v.rearrange("p (a b) -> p a b", b=dims[1])
        if len(dims) == 3:
            v = v.rearrange("p (a b c) -> p a b c", b=dims[1], c=dims[2])
        if len(dims) == 4:
            v = v.rearrange("p (a b c d) -> p a b c d", b=dims[1], c=dims[2], d=dims[3])
        return v

    def overlay(self):
        return Region(self.tensor, self.at, self.end)


class PsumRing:

    def __init__(self, ps, filled, freed):
        self.ps, self.filled, self.freed = ps, filled, freed
        self.uses, self.at, self.count, self.done = [], {}, {"act": 0, "dve": 0}, {"act": 0, "dve": 0}

    def open(self, pe, key, reader):
        n = len(self.uses)
        if n >= 8:
            who, k = self.uses[n - 8]
            pe.wait_ge(self.freed[who], k)
        self.count[reader] += 1
        assert key not in self.at, key
        self.at[key] = (n, reader, self.count[reader])
        self.uses.append((reader, self.count[reader]))
        return self.ps[:, n % 8, :]

    def close(self, mm):
        mm.then_inc(self.filled, 1)

    def full(self, eng, key):
        n, _, _ = self.at[key]
        eng.wait_ge(self.filled, n + 1)
        return self.ps[:, n % 8, :]

    def free(self, ins, key):
        _, who, k = self.at[key]
        self.done[who] += 1
        assert self.done[who] == k, (key, who, k, self.done[who])
        ins.then_inc(self.freed[who], 1)

    def read(self, eng, key):
        _, who, k = self.at[key]
        eng.wait_ge(self.freed[who], k)


def bc(ap, axis, n):
    v = ap.unsqueeze(axis)
    shape = list(v.shape)
    shape[axis] = n
    return v.broadcast_to(shape)


def build(nc, a, o, scratch):
    with ExitStack() as ctx:
        def sem(name):
            return ctx.enter_context(nc.semaphore(name))

        psum = ctx.enter_context(nc.psum_tensor("psum", [128, 8, 512], F32))
        WIDTH = 53184
        mem = ctx.enter_context(nc.sbuf_tensor("mem", [128, WIDTH], F32))

        top = Region(mem, 0, WIDTH)
        coff, cwidth = offsets(CST)
        cst = top.take(cwidth)

        def C(name, rows=128):
            at, n = coff[name]
            return cst[:rows, at:at + n]

        ident = C("ident")
        X = top.take(NT, D)
        XT = top.take(KD, TT)
        MT = top.take(KD, MEM)
        small = top.take(48)
        stats = small[:, 0:12].rearrange("p (a b) -> p a b", b=6)
        moments = small[:, 12:22].rearrange("p (a b) -> p a b", b=2)
        rstd, vare, std, shift = small[:, 24:29], small[:, 30:35], small[:, 36:41], small[:, 42:47]

        mix = top.overlay()
        WS = mix.take(2, KD, 512)
        ct_at = mix.at
        CT = mix.take(KD, TT)
        KMT = mix.take(XH, MEM)
        MKROW = mix.take(2, XW)
        VM = mix.take(2, XW)
        QMT = mix.take(XH, TT)
        ln_at = mix.at
        lng = mix.take(2, D)
        ln_end = mix.at = mix.at + 8
        MEMROW = lng
        tok = mix.overlay()
        xt_reuse = Region(mem, cwidth + NT * D, cwidth + NT * D + KD * TT)
        ct_reuse = Region(mem, ct_at, ct_at + KD * TT)

        m0 = tok.overlay()
        QK = m0.take(KD, TT)
        VA = m0.take(4, MH, 130)
        GO = m0.take(NT, MW)
        TOK = m0.take(NT, MW)
        GW = m0.take(KD, 8)
        CW = m0.take(KD, 4)
        SCT = m0.take(KD, 24)
        UST = m0.take(KD, NB)
        CVS = m0.take(3, KD, NB)
        UTAIL = m0.take(KD, 4)
        GB = m0.take(16)
        NGB = m0.take(MW)
        VS = m0.take(MW, rows=NB)
        gcol = m0.take(96)
        aC, mC, mendC = gcol[:, 0:16], gcol[:, 16:32], gcol[:, 32:36]
        emC, wendC, dn = gcol[:, 36:52], gcol[:, 52:68], gcol[:, 68:84]
        dmend = gcol[:4, 84:88]
        ST = m0.take(20, 6)
        MV = m0.take(20, 2)
        hv, hs_, hr = m0.take(20), m0.take(20), m0.take(20)
        sg = m0.take(200, rows=NB)
        m0s = m0.overlay()
        TH = m0.take(2, SEQ)
        G = {n: m0.take(SEQ, rows=4) for n in ("x", "e", "lf", "B", "a", "M")}
        cr = ct_reuse.overlay()
        CWR = cr.take(D, rows=4)
        SCR = cr.take(D, rows=24)
        cr = ct_reuse.overlay()
        NUM = cr.take(16, 130)
        AR = cr.take(2, SEQ)
        DD = cr.take(2, SEQ)
        PT = xt_reuse.overlay().take(2, 4, SEQ)
        CIN = xt_reuse.overlay().take(NB, MW)
        cr = ct_reuse.overlay()
        QKR = cr.take(D, rows=NB)
        UR = cr.take(D, rows=NB)
        QMK = cr.take(2, MW, rows=NB)
        VMK = cr.take(2, MW, rows=NB)
        KW = m0s.take(4, MW)
        CS = m0s.take(MH, MD)
        R = {n: m0s.take(MW, rows=NB) for n in ("vd", "n", "t", "t2")}
        CTMP = m0s.take(MW)
        NNR = m0s.take(MW, rows=1)
        UPR = m0s.take(D, rows=3)
        CQ = m0s.take(NB, MH)
        WPB = m0s.take(NB, MH)
        WPM = m0s.take(NB, MH, rows=NB)

        m1 = tok.overlay()
        R1 = {n: m1.take(AW, rows=NB) for n in ("q", "k", "v", "qi")}
        r1ki = m1.take(AD, rows=NB)
        r1t = m1.take(AW, rows=NB)
        r1wi = m1.take(AH, rows=NB)
        RB = m1.take(AH, rows=32)
        RB64 = m1.take(NB, AH, rows=32)
        WIP = m1.take(4, AH)
        PTB = m1.take(NB * NPG, rows=1, dtype=I32)
        m1a = m1.overlay()
        kw_at = m1a.at
        KW1 = m1a.take(KD, 136)
        AQT = m1a.take(4, TT)
        AKT = m1a.take(4, TT)
        QIT = m1a.take(4, TT)
        KIT = m1a.take(TT)
        VR = m1a.take(4, AW)
        table_at = m1a.at
        OHP = m1a.take(640, rows=32)
        RBT = m1a.take(640, rows=8)
        ring_at = m1a.at
        MASK = m1a.take(4, SEQ)
        HK = m1a.take(2, SEQ)
        PR = m1a.take(2, SEQ)
        SC1, SC2 = m1a.take(2 * 128), m1a.take(3 * 128)
        relu_at = m1a.at
        RLU = m1a.take(2, SEQ)
        KROW = ct_reuse.overlay().take(4, AW)
        KIROW = m1a.take(4, AD)
        m8 = m1a.take(8)
        anm, asm, ars = m1a.take(32), m1a.take(32), m1a.take(32)
        QIS = m1a.take(8, 8, rows=64)
        WT = m1a.take(8, rows=NB)
        WM = m1a.take(8, 8, rows=NB)
        LN8 = m1a.take(8, rows=NB)
        LNM = m1a.take(8, 8, rows=NB)
        PN = m1a.take(8, rows=64)
        P8 = m1a.take(8, rows=NB)
        PM8 = m1a.take(8, 8, rows=NB)
        s8 = m1a.take(8)
        sst = m1a.take(8, rows=64)
        OWN = Region(mem, relu_at, mem.shape[1]).take(2, AW, rows=8)
        PTA = xt_reuse.overlay().take(2, 4, SEQ)
        KV = Region(mem, ring_at, relu_at).take(4, 2, AW)
        S_RL = Region(mem, relu_at, mem.shape[1]).take(2, 512, rows=NB)
        OHS = Region(mem, table_at, ring_at).take(PAST + 2, rows=32)
        S_WK = Region(mem, kw_at, kw_at + KD * 136).take(PAST + 2, rows=NB)
        ln_reuse = Region(mem, ln_at, ln_end)
        S_SC = ln_reuse.take(PAST + 2, rows=NB)
        LR = ln_reuse.overlay().take(PAST + 1, rows=64)
        KIX = ln_reuse.take(2, NPG, AD)
        mt_reuse = Region(mem, cwidth + NT * D + KD * TT, cwidth + NT * D + KD * TT + KD * MEM)
        S_QM = mt_reuse.take(2, AW, rows=NB)
        LG = mt_reuse.take(NPG, 64)
        PTS = mt_reuse.take(NPG, 64)
        KXT = Region(mem, ct_at + 4 * TT, ct_at + 8 * TT).take(2, PAST)
        SC = {1: SC1, 2: SC2, 3: Region(mem, ct_at + 4 * TT, ct_at + 8 * TT).take(SEQ)}
        S_T = r1t
        VV = WS[:, 1].rearrange("p (n j) c -> p n j c", j=2)

        mm = tok.overlay()
        MP = mm.take(2, MEM)
        MPT = mm.take(2, 2, SEQ)
        MK2 = mm.take(2, 2, XW)
        MV8 = mm.take(NB, 2, XW)
        MQR = mm.take(XW, rows=NB)
        MQM = mm.take(2, XW, rows=NB)
        MLG = mm.take(2, 32)
        MLR = mm.take(MEM, rows=32)
        MPM = mm.take(NB, 2, 32)
        MOWN = mm.take(XW, rows=32)
        mnm, msm, mrs = mm.take(16), mm.take(16), mm.take(16)
        mst = mm.take(4, rows=32)

        mo = top.overlay()
        we_at = mo.at
        WE = mo.take(GRP, 3, 2 * D)
        XE = mo.take(2, D)
        XET = mo.take(2, KD, 128)
        SG = mo.take(2, DE)
        HH = mo.take(DE)
        HT = mo.take(2, 128)
        OUT = mo.take(2, D)
        early = Region(mem, WIDTH - 36 * KD - 36 - 2 * D, WIDTH)
        assert mm.at <= early.at
        WR = early.take(KD, 36)
        BR = early.take(36)
        RL = mo.take(NT, 36)
        rt = {n: mo.take(NT, NE) for n in ("l2", "eq", "c", "oh1", "oh2", "l3", "both", "pos", "t")}
        rg = {n: mo.take(NT, NG) for n in ("e", "eq", "c", "oh")}
        rs = {n: mo.take(NT) for n in ("gm", "gw", "m1", "m2", "d", "e2", "w1", "mn", "g1", "g2")}
        cnt, over, incl, excl = mo.take(NE), mo.take(NE), mo.take(NE), mo.take(NE)
        et1, et2, et3 = mo.take(8, NE), mo.take(8, NE), mo.take(8)
        ngf = mo.take(2)
        r2 = {n: mo.take(2 * NT) for n in ("e", "p", "q", "ot", "t", "row", "cell")}
        ROWI = mo.take(2, NT, dtype=U32)
        CELLI = mo.take(2, NT, dtype=U32)
        TOKI = mo.take(NT, dtype=U32)
        ETI = mo.take(8, dtype=I32)
        NGI = mo.take(1, dtype=I32)
        LZ = mo.take(LW, dtype=U32)
        LST = mo.take(LW, dtype=U32)
        IDX = mo.take(GRP, dtype=U32)
        assert mo.at <= WIDTH - 36 * KD - 36 - 2 * D
        lnf = early.take(2, D)
        yg_at = we_at + 2 * 3 * 2 * D
        YG = Region(mem, yg_at, yg_at + 2 * NT * D).take(NT, 2, D)

        NPOOL = a["cache_k"].shape[1]

        ring = PsumRing(psum, sem("bank_filled"), {"act": sem("bank_freed_act"), "dve": sem("bank_freed_dve")})
        order = {e: sem(f"{e}_order") for e in ("act", "dve", "pool")}
        at_order = {"act": 0, "dve": 0, "pool": 0}
        stage_done = sem("stage_done")
        n_stage = {}

        def seq(eng, name, ins):
            at_order[name] += 1
            ins.then_inc(order[name], 1)
            eng.wait_ge(order[name], at_order[name])

        def stage_end(eng, name):
            n_stage[name] = n_stage.get(name, 0) + 1
            eng.drain().then_inc(stage_done, 1)
            eng.wait_ge(stage_done, 4 * n_stage[name])

        s_cst, s_x, s_mem = sem("constants_in"), sem("x_in"), sem("mem_in")
        s_l0, s_l1, s_ln = sem("layer0_small_in"), sem("layer1_small_in"), sem("ln_mix_in")
        s_st = sem("stored")
        stored = [0]
        s = {n: sem(n) for n in (
            "gates_lin", "gates_ln", "dmend_done", "conv_done", "tanh_done", "silu_done", "sconv_done",
            "stanh_done", "ssilu_done", "vones", "exp_lin", "exp_col", "go_ready", "arg_done", "decay_done",
            "decay_cut", "sg_lin", "sg_ln", "sg_lin2", "sg_exp", "c_in", "n_in", "masked", "cq_done", "wp_ready",
            "var_ready", "std_ready", "tok_ready", "sample_ready", "head_scale", "head_norm", "urow", "mmax", "mnorm", "mk_in0", "mk_in1", "mv_in", "mqmask",
            "mk_used", "msmax", "msexp", "msnorm", "scored", "cut", "mask_ready", "rbt_out", "hk_in0", "hk_in1",
            "amax", "anorm", "lnvar", "lnstd", "lnscale", "lnx", "gained", "x_norm", "x1_out", "kix_in0", "kix_in1", "v_in0", "v_in1", "v_in2", "v_in3", "v_used", "kv_in0", "kv_in1", "kv_in2", "kv_in3",
            "kv_done", "wm_ready", "smask", "sqm", "lnew", "smax", "sexp", "snorm", "pnew", "pm8", "krow_out", "experts_out",
            "ohs_in", "router_in", "lnf_in", "router_lin", "router_exp", "e2_lin", "e2_exp", "route_ready",
            "table_ready", "zeroed", "scattered", "ids_in", "y_in0", "y_in1", "y_in2", "y_in3", "y_in4", "cells_ready")}
        moe = [{n: sem(f"{n}_{l}") for n in (
            "w_in0", "w_in1", "w_in2", "w_in3", "gathered0", "gathered1", "turned_a", "turned_b", "xe_a", "xe_b",
            "gu_done", "silu", "h_made", "h_turned", "ht_ready", "down_done", "out_a", "out_b", "put0", "put1",
            "picked")}
            for l in range(DEPTH)]

        def w_cols(w, c0):
            return w[:, c0:c0 + 512].rearrange("(p k) n -> p k n", k=KD)

        def w_rows(w, c0):
            return w[:, c0:c0 + 512].rearrange("(k p) n -> p k n", p=128)

        chunks = []
        for l in range(DEPTH):
            kv = a["w_mem_kv"][l]
            chunks += [(l, "km", w_cols(kv, 0)), (l, "vm", w_cols(kv, XW))]
            w = a["w_in_mlstm"][0] if l == 0 else a["w_in_dsa"][0]
            names = [("q", 0), ("k", 512), ("v", 1024), ("o", 1536), ("qm", 2056)] if l == 0 else \
                    [("q", 0), ("qi", 1536), ("k", 512), ("v", 1024), ("qm", 2120)]
            chunks += [(l, n, w_cols(w, c)) for n, c in names]
            chunks += [(l, "wo0", w_rows(a["w_out"][l], 0)), (l, "wo1", w_rows(a["w_out"][l], 512))]
        chunk_no = {(l, n): i for i, (l, n, _) in enumerate(chunks)}
        chunk_last = {}
        chunk_in = [sem("chunk_in0"), sem("chunk_in1")]

        def chunk(pe, l, name):
            i = chunk_no[(l, name)]
            pe.wait_ge(chunk_in[i % 2], 16 * (i // 2 + 1))
            return WS[:, i % 2]

        def mark_chunk(l, name):
            chunk_last[chunk_no[(l, name)]] = len(ring.uses)

        Q4 = [(c * 128, 128) for c in range(4)]
        HALF = TT // 2
        SOFTMAX_AT = 2
        PRODUCT_AT = (0, 1, 3, 5, 7)
        SCORES = [(i, g) for i in range(1, 4) for g in range(8)]
        SCORE_STEP = 3
        VALUES_AT = {3 * b + 9: b for b in range(NB)}
        block = ctx.enter_context(nc.Block())

        T = nc.tensor

        def turn_rows(pe, src, key, readers, n):
            v = src.rearrange("r (p k) -> r k p", k=KD)
            for half in range(2):
                bank = ring.open(pe, key + (half,), readers[half])
                for j in range(4):
                    mm_ = T.transpose(bank[:, j * n:j * n + n], v[:, 4 * half + j, :], ident[:n, :n])
                ring.close(mm_)

        def product(pe, key, reader, terms, rows, ncol, at=0):
            bank = ring.open(pe, key, reader)
            for k, (lhs, rhs) in enumerate(terms):
                mm_ = T.matmul(bank[:rows, at:at + ncol], lhs, rhs, start=(k == 0), stop=(k == len(terms) - 1))
            ring.close(mm_)

        def project_cols(pe, l, name, w, c0, reader, ncol=128):
            product(pe, (l, name), reader,
                    [(w[:, k, c0:c0 + ncol], XT[:, k, 0:SEQ]) for k in range(KD)], ncol, SEQ)

        def project_all(pe, l, name, w, c0, reader):
            for half in range(2):
                product(pe, (l, name, half), reader,
                        [(w[:, k, c0:c0 + 128], XT[:, k, half * HALF:(half + 1) * HALF]) for k in range(KD)], 128, HALF)

        def project_sample(pe, l, name, w, parts, reader):
            bank = ring.open(pe, (l, name), reader)
            for j, (c0, ncol) in enumerate(parts):
                for k in range(KD):
                    mm_ = T.matmul(bank[:ncol, j * NB:j * NB + NB], w[:, k, c0:c0 + ncol], XT[:, k, SEQ:TT],
                                   start=(k == 0), stop=(k == KD - 1))
            ring.close(mm_)

        def project_rows(pe, l, name, w, i, reader):
            t0, n = TILES[i]
            product(pe, (l, name, i), reader,
                    [(XT[:, k, t0:t0 + n], w[:, k, :]) for k in range(KD)], n, w.shape[2])

        def turn_parts(pe, key, reader, parts):
            bank = ring.open(pe, key, reader)
            for at, src in parts:
                p, n = src.shape
                mm_ = T.transpose(bank[:n, at:at + p], src, ident[:p, :p])
            ring.close(mm_)

        def pe_mlstm(pe):
            def nums(h):
                for i in range(4):
                    bank = ring.open(pe, ("num", h, i), "act")
                    for st in range(i + 1):
                        if i == 0:
                            ring.read(pe, ("score", h, 3))
                        mm_ = T.matmul(bank[:, 0:129], PT[:, h % 2, st, (i - st) * 128:(i - st + 1) * 128],
                                       VA[:, st, h, 0:129], start=(st == 0), stop=(st == i))
                    ring.close(mm_)

            pe.wait_ge(s["silu_done"], 8)
            pe.wait_ge(s["vones"], 1)
            for i in range(4):
                ring.read(pe, (0, "v", i))
            for h in range(MH):
                product(pe, ("negm", h), "dve", [(C("seln", 4)[:, h * 128:(h + 1) * 128], G["M"])], 128, SEQ)
                for st in range(4):
                    product(pe, ("score", h, st), "dve",
                            [(QK[:, 4 + h, st * 128:(st + 1) * 128], QK[:, h, st * 128:SEQ])], 128, SEQ - st * 128)
                if h:
                    nums(h - 1)
            nums(MH - 1)
            stage_end(pe, "pe")
            for st in range(4):
                turn_parts(pe, ("krow", st), "dve", [(h * 128, QK[:, 4 + h, st * 128:(st + 1) * 128]) for h in range(MH)])
            pe.wait_ge(s["ssilu_done"], 1)
            turn_parts(pe, ("sq",), "act", [(h * 128, QK[:, h, SEQ:TT]) for h in range(MH)])
            turn_parts(pe, ("sk",), "dve", [(h * 128, QK[:, 4 + h, SEQ:TT]) for h in range(MH)])
            for j in range(2):
                turn_parts(pe, ("su", j), "act", [(c * 128, UST[:, 4 * j + c, :]) for c in range(4)])
            for j in range(2):
                turn_parts(pe, ("pu", j), "act", [(c * 128, UTAIL[:, 4 * j + c, 0:3]) for c in range(4)])
            ring.read(pe, ("krow", 3))
            bank = ring.open(pe, ("newC",), "act")
            for h in range(MH):
                for st in range(4):
                    mm_ = T.matmul(bank[:, h * 128:(h + 1) * 128], VA[:, st, h, 0:128], KW[:, st, h * 128:(h + 1) * 128],
                                   start=(st == 0), stop=(st == 3))
            ring.close(mm_)
            product(pe, ("newn",), "act", [(C("ones")[:, 0:1], KW[:, st, :]) for st in range(4)], 1, MW)
            pe.wait_ge(s["wp_ready"], 1)
            product(pe, ("wp",), "dve", [(C("ones", NB), WPM.rearrange("p b h -> p (b h)"))], 128, 32)
            for b in range(NB):
                pe.wait_ge(s["masked"], b + 1)
                product(pe, ("qb", b), "dve", [(C("ones", NB), QMK[:, b % 2, :])], 128, MW)
                bank = ring.open(pe, ("vk", b), "dve")
                for h in range(MH):
                    mm_ = T.matmul(bank[:, h * 128:(h + 1) * 128], VMK[:, b % 2, h * 128:(h + 1) * 128],
                                   QKR[:, MW + h * 128:MW + (h + 1) * 128], start=True, stop=True)
                ring.close(mm_)
            pe.wait_ge(s["cq_done"], 1)
            turn_parts(pe, ("cqT",), "dve", [(h * 128, CQ[:, :, h]) for h in range(MH)])
            for i, (t0, n) in enumerate(TILES):
                if i < 4:
                    pe.wait_ge(s["tok_ready"], i + 1)
                else:
                    pe.wait_ge(s["sample_ready"], 1)
                turn_parts(pe, (0, "tokT", i), "act", [(c * n, TOK[:n, i, c * 128:(c + 1) * 128]) for c in range(4)])

        def pe_dsa_projections(pe):
            w = chunk(pe, 1, "q")
            for c in range(4):
                project_all(pe, 1, "q" + str(c), w, c * 128, "act")
            mark_chunk(1, "q")
            ring.read(pe, (1, "q3", 1))
            turn_parts(pe, ("sq1",), "act", [(c * 128, AQT[:, c, SEQ:TT]) for c in range(4)])

            def query(b):
                pe.wait_ge(s["sqm"], b + 1)
                product(pe, ("sqb", b), "dve", [(C("ones", NB), S_QM[:, b % 2, :])], 128, AW)

            w = chunk(pe, 1, "qi")
            for c in range(4):
                project_all(pe, 1, "qi" + str(c), w, c * 128, "dve")
                query(c)
            mark_chunk(1, "qi")
            project_all(pe, 1, "ki", KW1, 0, "act")
            for i in reversed(range(NT)):
                project_rows(pe, 1, "wi", KW1[:, :, 128:136], i, "dve")
            ring.read(pe, (1, "qi3", 1))
            turn_parts(pe, ("sqi1",), "act", [(c * 128, QIT[:, c, SEQ:TT]) for c in range(4)])
            ring.read(pe, (1, "ki", 1))
            turn_parts(pe, ("ski1",), "act", [(0, KIT[0:AD, SEQ:TT])])
            ring.read(pe, ("sqi1",))
            turn_parts(pe, ("qis",), "act", [(g * 8, R1["qi"][:, g * 64:(g + 1) * 64]) for g in range(8)])
            ring.read(pe, (1, "wi", 4))
            turn_parts(pe, ("wT",), "dve", [(0, r1wi)])

            def products():
                w = chunk(pe, 1, "k")
                for c in range(4):
                    project_all(pe, 1, "k" + str(c), w, c * 128, "act")
                    if c == 3:
                        mark_chunk(1, "k")
                    yield
                w = chunk(pe, 1, "v")
                for i in range(NT):
                    project_rows(pe, 1, "v", w, i, "act")
                    if i == NT - 1:
                        mark_chunk(1, "v")
                    yield
                w = chunk(pe, 1, "qm")
                for c in range(4):
                    project_all(pe, 1, "qm" + str(c), w, c * 128, "act")
                    if c == 3:
                        mark_chunk(1, "qm")
                    yield
                yield "end"

            def keys(b):
                pe.wait_ge(s["kix_in%d" % (b % 2)], 16 * NPG * (b // 2 + 1))
                for half in range(2):
                    turn_parts(pe, ("kxT", b, half), "act",
                               [(j * 128, KIX[:, b % 2, half * 4 + j, :]) for j in range(4)])

            product_ = products()
            keys(0)
            ring.read(pe, ("qis",))
            for b in range(NB):
                if b < 4:
                    query(b + 4)
                for half in range(2):
                    ring.read(pe, ("kxT", b, half))
                    product(pe, ("sx", b, half), "act",
                            [(QIS[:, :, b], KXT[0:64, b % 2, half * 512:(half + 1) * 512])], 8, 512)
                if b + 1 < NB:
                    keys(b + 1)
                if b in PRODUCT_AT:
                    next(product_)
                pe.wait_ge(s["wm_ready"], 1)
                for half in range(2):
                    ring.read(pe, ("sx", b, half))
                    product(pe, ("sw", b, half), "dve", [(WM[:, b, :], S_RL[:, half, :])], 8, 512)
            for n, (i, g) in enumerate(SCORES):
                if n % SCORE_STEP == 0:
                    next(product_)
                w, p0 = (i + 1) * 128, (g % 2) * 64
                product(pe, ("ix", i, g), "act",
                        [(QIT[p0:p0 + 64, g // 2, i * 128:(i + 1) * 128], KIT[p0:p0 + 64, 0:w])], 128, w)
            assert next(product_, None) == "end"

        def pe_dsa(pe):
            ring.read(pe, (1, "k3", 1))
            for i in range(4):
                turn_parts(pe, ("krow1", i), "act", [(c * 128, AKT[:, c, i * 128:(i + 1) * 128]) for c in range(4)])
            turn_parts(pe, ("sk1",), "act", [(c * 128, AKT[:, c, SEQ:TT]) for c in range(4)])
            turn_parts(pe, ("kirow",), "act", [(i * AD, KIT[0:AD, i * 128:(i + 1) * 128]) for i in range(4)])
            for j, (c0, n) in enumerate(((0, 512), (512, 128))):
                product(pe, ("rbt", j), "act", [(RB, OHP[:, c0:c0 + n])], 8, n)
            pe.wait_ge(s["smask"], 1)
            pe.wait_ge(s["ohs_in"], 16)
            for half in range(2):
                bank = ring.open(pe, ("lr", half), "act")
                cols = slice(half * 512, (half + 1) * 512)
                T.matmul(bank[:64, :], RB64.rearrange("p b h -> p (b h)"), OHS[:, cols], start=True, stop=False,
                         skip_group_check=True)
                T.matmul(bank[:64, :], C("e8", NB), S_WK[:, cols], start=False, stop=False, skip_group_check=True)
                for j in range(4):
                    mm_ = T.matmul(bank[:64, j * 128:(j + 1) * 128], LG[:, half * 4 + j, :], ident, start=False,
                                   stop=(j == 3), skip_group_check=True)
                ring.close(mm_)
            pe.wait_ge(s["lnew"], 1)
            product(pe, ("lnew",), "act", [
                (LNM.rearrange("p b h -> p (b h)"), C("ones", NB)[:, 0:1]),
                (C("e8", NB), S_WK[:, PAST:PAST + 1]),
                (RB64.rearrange("p b h -> p (b h)"), OHS[:, PAST:PAST + 1])], 64, 1)
            for i in range(NT):
                ring.read(pe, (1, "v", i))
            units = [(h, i) for h in range(AH) for i in range(4)]

            def logits(n):
                h, i = units[n]
                p0, w = (h % 2) * 64, (i + 1) * 128
                if i == 0:
                    pe.wait_ge(s["hk_in%d" % (h % 2)], 16 * (h // 2 + 1))
                if h == 0:
                    pe.wait_ge(s["mask_ready"], i + 1)
                x0 = 384 - i * 128
                product(pe, ("al", h, i), "act",
                        [(AQT[p0:p0 + 64, h // 2, i * 128:(i + 1) * 128], AKT[p0:p0 + 64, h // 2, 0:w]),
                         (C("flip"), HK[:, h % 2, x0:x0 + w]),
                         (ident, MASK[:, i, 0:w])], 128, w)

            def turn(n):
                h, i = units[n]
                pe.wait_ge(s["anorm"], n + 1)
                turn_parts(pe, ("apT", h, i), "dve",
                           [(j * 128, PR[:, n % 2, j * 128:(j + 1) * 128]) for j in range(i + 1)])

            def values(h):
                for i in range(4):
                    ring.read(pe, ("apT", h, i))
                bank = ring.open(pe, ("apv", h), "act")
                c0 = (h // 2) * 128
                for j in range(4):
                    mm_ = T.matmul(bank[:, j * 128:SEQ], VR[:, j, c0:c0 + 128], PTA[:, h % 2, j, j * 128:SEQ],
                                   start=(j == 0), stop=(j == 3))
                ring.close(mm_)

            def sample_values(b):
                if b == 0:
                    ring.read(pe, ("psT",))
                    pe.wait_ge(s["pm8"], 1)
                bank = ring.open(pe, ("spv", b), "dve")
                T.matmul(bank[:8, :], PM8[:, b, :], R1["v"], start=True, stop=False)
                for qd in range(4):
                    pe.wait_ge(s["v_in%d" % qd], 32 * (b + 1))
                    for j in range(2):
                        mm_ = T.matmul(bank[:8, :], PTS[:, 2 * qd + j, b * 8:b * 8 + 8], VV[:, qd, j, :], start=False,
                                       stop=(qd == 3 and j == 1))
                    if qd < 3:
                        mm_.then_inc(s["v_used"], 1)
                ring.close(mm_)

            def sample_columns(b):
                ring.read(pe, ("spv", b))
                bank = ring.open(pe, ("spc", b), "act")
                for c in range(4):
                    mm_ = T.matmul(bank[:, c:c + 1], OWN[:, b % 2, c * 128:(c + 1) * 128], C("ones", 8)[:, 0:1],
                                   start=True, stop=True)
                ring.close(mm_)

            for n in range(len(units) + 2):
                if n < len(units):
                    logits(n)
                if n >= 2:
                    turn(n - 2)
                if n >= 7 and (n - 3) % 4 == 0:
                    values((n - 3) // 4 - 1)
                if n == SOFTMAX_AT + 2:
                    pe.wait_ge(s["snorm"], 1)
                    turn_parts(pe, ("psT",), "act", [(j * 64, LR[:, j * 128:(j + 1) * 128]) for j in range(NPG)])
                    pe.wait_ge(s["pnew"], 1)
                    product(pe, ("p8",), "dve", [(C("e64", 64), PN)], 8, 8)
                if n in VALUES_AT:
                    sample_values(VALUES_AT[n])
                if n - 1 in VALUES_AT:
                    sample_columns(VALUES_AT[n - 1])
            values(AH - 1)

        def pe_memory(pe, l):
            units = [(h, i) for h in range(XH) for i in range(4)]
            base = 16 * l
            ring.read(pe, (l, "qm3", 1))
            turn_parts(pe, ("mqr", l), "act", [(c * 128, QMT[:, c, SEQ:TT]) for c in range(4)])

            def values(h):
                for i in range(4):
                    ring.read(pe, ("mpT", l, h, i))
                product(pe, ("mpv", l, h), "act",
                        [(VM[:, j, h * 128:(h + 1) * 128], MPT[:, h % 2, j, :]) for j in range(2)], 128, SEQ)

            for n in range(len(units) + 2):
                if n < len(units):
                    h, i = units[n]
                    product(pe, ("ml", l, h, i), "act", [(QMT[:, h, i * 128:(i + 1) * 128], KMT[:, h, :])], 128, MEM)
                if n >= 2:
                    h, i = units[n - 2]
                    pe.wait_ge(s["mnorm"], base + n - 1)
                    turn_parts(pe, ("mpT", l, h, i), "dve",
                               [(j * 128, MP[:, n % 2, j * 128:(j + 1) * 128]) for j in range(2)])
                    if n % 2 == 0 and n // 2 - 1 < NB:
                        b = n // 2 - 1
                        pe.wait_ge(s["mqmask"], NB * l + b + 1)
                        product(pe, ("mqb", l, b), "dve", [(C("ones", NB), MQM[:, b % 2, :])], 128, XW)
                if n >= 7 and (n - 3) % 4 == 0:
                    values((n - 3) // 4 - 1)
            values(XH - 1)
            pe.wait_ge(s["mk_used"], NB * (l + 1))
            turn_parts(pe, ("mlr", l), "act", [(j * 128, MLG[:, j, :]) for j in range(2)])
            pe.wait_ge(s["msnorm"], l + 1)
            turn_parts(pe, ("mps", l), "dve", [(j * 32, MLR[:, j * 128:(j + 1) * 128]) for j in range(2)])
            ring.read(pe, ("mps", l))
            pe.wait_ge(s["mv_in"], 16 * NB * (l + 1))
            bank = ring.open(pe, ("msv", l), "dve")
            for b in range(NB):
                for j in range(2):
                    mm_ = T.matmul(bank[:32, :], MPM[:, b, j, :], MV8[:, b, j, :], start=(b == 0 and j == 0),
                                   stop=(b == NB - 1 and j == 1))
            ring.close(mm_)
            ring.read(pe, ("msv", l))
            bank = ring.open(pe, ("msc", l), "act")
            for h in range(XH):
                mm_ = T.matmul(bank[:, h * NB:(h + 1) * NB], MOWN[:, h * 128:(h + 1) * 128], C("e32", 32),
                               start=True, stop=True)
            ring.close(mm_)

        def pe_experts(pe, l):
            m = moe[l]

            def turn_tokens(par, count):
                pe.wait_ge(m["gathered%d" % par], count)
                v = XE[:, par, :].rearrange("r (p k) -> r k p", k=KD)
                for half, name in ((0, "turned_a"), (1, "turned_b")):
                    for q in range(4):
                        mm_ = T.transpose(psum[:, 4 + half, q * 128:(q + 1) * 128], v[:, 4 * half + q, :], ident)
                    mm_.then_inc(m[name], 1)

            def down(j, t):
                pe.wait_ge(m["ht_ready"], t + 1)
                if not (isinstance(t, int) and t < 1):
                    pe.wait_ge(m["out_a"], t)
                    pe.wait_ge(m["out_b"], t)
                for half in range(2):
                    for q in range(2):
                        c0 = q * D + half * 512
                        mm_ = T.matmul(psum[:, 2 + half, :], HT[:, q, :], WE[:, j, 2, c0:c0 + 512],
                                       start=(q == 0), stop=(q == 1))
                mm_.then_inc(m["down_done"], 1)

            def step(g, j, first):
                t = 4 * g + j
                pe.wait_ge(m["w_in%d" % j], 48 * (g + 1))
                pe.wait_ge(m["xe_a"], t + 1)
                pe.wait_ge(m["xe_b"], t + 1)
                if not (first and j < 2):
                    pe.wait_ge(m["h_made"], t - 1)
                wv = WE[:, j, 0:2, :].rearrange("p m (k f) -> p k m f", k=KD)
                for k in range(KD):
                    mm_ = T.matmul(psum[:, j % 2, :].rearrange("p (m f) -> p m f", m=2), XET[:, j % 2, k, :],
                                   wv[:, k], start=(k == 0), stop=(k == KD - 1))
                mm_.then_inc(m["gu_done"], 1)
                turn_tokens((j + 1) % 2, 16 * (2 * g + (j + 1) // 2 + 1))
                if not (first and j == 0):
                    down((j - 1) % GRP, t - 1)
                pe.wait_ge(m["h_made"], t + 1)
                hv_ = HH.rearrange("s (p q) -> s q p", q=2)
                for q in range(2):
                    mm_ = T.transpose(psum[:, 6, q * 128:(q + 1) * 128], hv_[:, q, :], ident)
                mm_.then_inc(m["h_turned"], 1)

            pe.wait_ge(s["table_ready"], l + 1)
            groups = pe.value_load(NGI[0:1, 0:1], min_val=0, max_val=(MTILES - NE) // GRP) + NE // GRP
            turn_tokens(0, 16)
            for j in range(GRP):
                step(0, j, True)
            with pe.Fori(1, groups) as g:
                for j in range(GRP):
                    step(g, j, False)
            down(GRP - 1, 4 * groups - 1)

        @block.tensor
        def _(pe):
            pe.wait_ge(s_cst, 16)
            pe.wait_ge(s_x, 32)
            for i, (t0, n) in enumerate(TILES):
                turn_rows(pe, X[:n, i], ("xT", 0, i), ("act", "dve"), n)
            pe.wait_ge(s_mem, 16)
            for i in range(2):
                turn_rows(pe, MEMROW[:, i], ("memT", i), ("act", "dve"), 128)

            for l in range(DEPTH):
                for i in range(2):
                    for half in range(2):
                        ring.read(pe, ("memT", i, half))
                for name in ("km", "vm"):
                    w = chunk(pe, l, name)
                    for i in range(2):
                        product(pe, (l, name, i), "act" if name == "km" else "dve",
                                [(MT[:, k, i * 128:(i + 1) * 128], w[:, k, :]) for k in range(KD)], 128, XW)
                    mark_chunk(l, name)
                for i in range(2):
                    ring.read(pe, (l, "km", i))
                for hp in range(2):
                    turn_parts(pe, (l, "kmT", hp), "dve",
                               [(h * MEM + i * 128, MKROW[:, i, (2 * hp + h) * 128:(2 * hp + h + 1) * 128])
                                for h in range(2) for i in range(2)])
                for i in range(NT):
                    for half in range(2):
                        ring.read(pe, ("xT", l, i, half))

                if l == 0:
                    pe.wait_ge(s_l0, 16 * 8)
                    project_cols(pe, 0, "gi", GW, 0, "dve", 4)
                    project_cols(pe, 0, "gf", GW, 4, "dve", 4)
                    project_rows(pe, 0, "gs", GW, 4, "dve")
                    turn_parts(pe, (0, "cwT"), "act",
                               [(4 * k, CWR[:, k * 128:(k + 1) * 128]) for k in range(KD)]
                               + [(32 + 24 * k, SCR[:, k * 128:(k + 1) * 128]) for k in range(KD)])
                    for name in ("q", "k"):
                        w = chunk(pe, 0, name)
                        for c in range(4):
                            project_cols(pe, 0, name + str(c), w, c * 128, "dve")
                        project_sample(pe, 0, name + "s", w, Q4, "dve")
                        mark_chunk(0, name)
                    pe.wait_ge(s["dmend_done"], 1)
                    bank = ring.open(pe, (0, "gcol"), "dve")
                    for st in range(4):
                        T.transpose(bank[:, 4 * st:4 * st + 4], G["a"][:, st * 128:(st + 1) * 128], ident[:4, :4])
                    for st in range(4):
                        T.transpose(bank[:, 16 + 4 * st:20 + 4 * st], G["x"][:, st * 128:(st + 1) * 128],
                                    ident[:4, :4])
                    mm_ = T.matmul(bank[:, 32:36], C("ones", 4), dmend, start=True, stop=True)
                    ring.close(mm_)
                    for name in ("v", "o"):
                        w = chunk(pe, 0, name)
                        for i in range(NT):
                            project_rows(pe, 0, name, w, i, "act")
                        mark_chunk(0, name)
                else:
                    pe.wait_ge(s_l1, 16 * 5)
                    pe_dsa_projections(pe)
                if l == 0:
                    w = chunk(pe, 0, "qm")
                    for c in range(4):
                        project_all(pe, 0, "qm" + str(c), w, c * 128, "act")
                    mark_chunk(0, "qm")
                    pe_mlstm(pe)
                else:
                    pe_dsa(pe)
                stage_end(pe, "pe")
                pe_memory(pe, l)

                ring.read(pe, ("msc", l))
                if l == 0:
                    for i in range(NT):
                        ring.read(pe, (0, "tokT", i))
                else:
                    ring.read(pe, ("apv", AH - 1))
                    ring.read(pe, ("spc", NB - 1))
                def turn_x1(i):
                    pe.wait_ge(s["x_norm"], 10 * l + i + 1)
                    turn_rows(pe, X[:TILES[i][1], i], ("x1T", l, i), ("act", "act"), TILES[i][1])

                def router(name, tiles):
                    ring.read(pe, ("x1T", l, tiles[-1], 1))
                    bank = ring.open(pe, (l, name), "dve")
                    for i in tiles:
                        t0, n = TILES[i]
                        for k in range(KD):
                            mm_ = T.matmul(bank[:n, i * 36:(i + 1) * 36], XT[:, k, t0:t0 + n], WR[:, k, :],
                                           start=(k == 0), stop=(k == KD - 1))
                    ring.close(mm_)

                for i in range(NT + 3):
                    if i < NT:
                        t0, n = TILES[i]
                        for half in range(2):
                            w = chunk(pe, l, "wo%d" % half)
                            product(pe, (l, "y", half, i), "dve",
                                    [(CT[:, c, t0:t0 + n], w[:, c, :]) for c in range(KD)], n, 512)
                            if i == NT - 1:
                                mark_chunk(l, "wo%d" % half)
                    if i == NT + 2:
                        pe.wait_ge(s["router_in"], 64 * (l + 1))
                        router("router0", [0, 1, 2, 3])
                    if i >= 3:
                        turn_x1(i - 3)
                router("router1", [4])
                stage_end(pe, "pe")

                pe.wait_ge(s["route_ready"], l + 1)
                bank = ring.open(pe, (l, "before"), "dve")
                for i, (t0, n) in enumerate(TILES):
                    for j in range(i):
                        T.matmul(bank[:n, i * NE:(i + 1) * NE], C("ones")[:, :n], rt["both"][:, j, :],
                                 start=(j == 0), stop=False)
                    T.matmul(bank[:n, i * NE:(i + 1) * NE], C("before", n)[:, :n], rt["both"][:n, i, :],
                             start=(i == 0), stop=True)
                for i, (t0, n) in enumerate(TILES):
                    mm_ = T.matmul(bank[:, NT * NE:(NT + 1) * NE], C("ones", n), rt["both"][:n, i, :],
                                   start=(i == 0), stop=(i == NT - 1))
                ring.close(mm_)
                for who in ("act", "dve"):
                    pe.wait_ge(ring.freed[who], ring.count[who])
                pe_experts(pe, l)
                if l == 0:
                    for i, (t0, n) in enumerate(TILES):
                        pe.wait_ge(s["x_norm"], 5 + i + 1)
                        turn_rows(pe, X[:n, i], ("xT", 1, i), ("act", "act"), n)
                stage_end(pe, "pe")

        A = nc.scalar

        def copy_turned(act, key, dst, n):
            bank = ring.full(act, key)
            ring.free(A.activation(dst, bank[:, 0:4 * n].rearrange("p (k t) -> p k t", k=4), ACT.Copy), key)

        def act_copy(act, key, dst, scale=1.0, rows=128, c0=0, n=None, view=None, func=ACT.Copy):
            bank = ring.full(act, key)[:rows, c0:(c0 + n) if n else 512]
            if view:
                bank = view(bank)
            ring.free(A.activation(dst, bank, func, scale=scale), key)

        def act_mlstm(act):
            act.wait_ge(s["gates_lin"], 1)
            seq(act, "act", A.activation(G["e"], G["e"], ACT.Exp))
            A.activation(G["lf"], G["e"], ACT.Ln, bias=1.0).then_inc(s["gates_ln"], 1)
            act.wait_ge(s["sg_lin"], 1)
            seq(act, "act", A.activation(sg[:, 8:12], sg[:, 8:12], ACT.Exp))
            A.activation(sg[:, 12:16], sg[:, 8:12], ACT.Ln, bias=1.0).then_inc(s["sg_ln"], 1)
            bank = ring.full(act, (0, "cwT"))
            A.activation(CW, bank[:, 0:32].rearrange("p (k j) -> p k j", j=4), ACT.Copy)
            ring.free(A.activation(SCT, bank[:, 32:224].rearrange("p (k j) -> p k j", j=24), ACT.Copy), (0, "cwT"))
            for c in range(8):
                act.wait_ge(s["conv_done"], c + 1)
                if c >= 2:
                    act.wait_ge(s["silu_done"], c - 1)
                A.activation(TH[:, c % 2, :], QK[:, c, 0:SEQ], ACT.Tanh, scale=0.5).then_inc(s["tanh_done"], 1)
            act.wait_ge(s["sconv_done"], 1)
            A.activation(CVS[:, 2], CVS[:, 1], ACT.Tanh, scale=0.5).then_inc(s["stanh_done"], 1)
            act.wait_ge(s["exp_lin"], 1)
            A.activation(emC, mC, ACT.Exp, scale=-1.0)
            A.activation(wendC, wendC, ACT.Exp).then_inc(s["exp_col"], 1)
            for i, (t0, n) in enumerate(TILES):
                if i < 4:
                    act_copy(act, (0, "v", i), VA[:, i, :, 0:128], view=lambda v: v.rearrange("p (h d) -> p h d", h=MH))
                else:
                    act_copy(act, (0, "v", i), VS, rows=NB)
            for i, (t0, n) in enumerate(TILES):
                bank = ring.full(act, (0, "o", i))
                ring.free(A.activation(GO[:n, i, :], bank[:n, :], ACT.Tanh, scale=0.5), (0, "o", i))
            act_queries(act, 0)
            n = 0
            for h in range(MH):
                for st in range(4):
                    w = SEQ - st * 128
                    act.wait_ge(s["arg_done"], n + 1)
                    if n >= 2:
                        ring.read(act, ("score", (n - 2) // 4, (n - 2) % 4))
                    A.activation(DD[:, n % 2, 0:w], AR[:, n % 2, 0:w], ACT.Exp).then_inc(s["decay_done"], 1)
                    n += 1
                if h:
                    for i in range(4):
                        act_copy(act, ("num", h - 1, i), NUM[:, i * 4 + h - 1, 0:129], n=129)
            for i in range(4):
                act_copy(act, ("num", MH - 1, i), NUM[:, i * 4 + MH - 1, 0:129], n=129)
            stage_end(act, "act")
            act_copy(act, ("sq",), QKR[:, 0:MW], rows=NB)
            for j in range(2):
                act_copy(act, ("su", j), UR[:, j * 512:(j + 1) * 512], rows=NB)
            for j in range(2):
                act_copy(act, ("pu", j), UPR[:, j * 512:(j + 1) * 512], rows=3)
            act.wait_ge(s["sg_lin2"], 1)
            A.activation(sg[:, 20:32], sg[:, 20:32], ACT.Exp).then_inc(s["sg_exp"], 1)
            act.wait_ge(s["var_ready"], 1)
            A.activation(hs_[:, 0:16], hv[:, 0:16], ACT.Sqrt).then_inc(s["std_ready"], 1)
            act.wait_ge(s["head_scale"], 1)
            for i in range(4):
                for h in range(MH):
                    g = 4 * i + h
                    v = TOK[:, i, h * MD:(h + 1) * MD]
                    ins = A.activation(v, v, ACT.Identity, scale=hr[:, g:g + 1], bias=hv[:, g:g + 1])
                ins.then_inc(s["head_norm"], 1)
            act_copy(act, ("newC",), CS, view=lambda v: v.rearrange("p (h d) -> p h d", h=MH))
            act_copy(act, ("newn",), NNR, rows=1)
            act.wait_ge(s["wp_ready"], 1)
            for b in range(NB):
                if b >= 2:
                    ring.full(act, ("vk", b - 2))
                only = ident[:NB, b:b + 1]
                A.activation(QMK[:, b % 2, :], QKR[:, 0:MW], ACT.Copy, scale=only)
                A.activation(VMK[:, b % 2, :], R["vd"], ACT.Copy, scale=only).then_inc(s["masked"], 1)
            act.wait_ge(s["var_ready"], 2)
            A.activation(hs_[:, 16:20], hv[:, 16:20], ACT.Sqrt).then_inc(s["std_ready"], 1)
            act.wait_ge(s["urow"], 16)
            for i, (t0, n) in enumerate(TILES):
                act_copy(act, (0, "tokT", i), CT[:, 0:4, t0:t0 + n], n=4 * n,
                         view=lambda v, n=n: v.rearrange("p (c t) -> p c t", c=4))

        def copy_all(act, l, name, dst, scale=1.0):
            for half in range(2):
                act_copy(act, (l, name, half), dst[:, half * HALF:(half + 1) * HALF], scale=scale, n=HALF)

        def act_queries(act, l):
            for c in range(4):
                copy_all(act, l, "qm%d" % c, QMT[:, c, :], float(XD) ** -0.5)

        def act_dsa(act):
            for c in range(4):
                copy_all(act, 1, "q%d" % c, AQT[:, c, :], float(AD) ** -0.5)
            act_copy(act, ("sq1",), R1["q"], rows=NB)
            copy_all(act, 1, "ki", KIT)
            act_copy(act, ("sqi1",), R1["qi"], rows=NB)
            act_copy(act, ("ski1",), r1ki, rows=NB, n=AD)
            act_copy(act, ("qis",), QIS, rows=64, n=64, view=lambda v: v.rearrange("p (g b) -> p g b", g=8))

            def products():
                for c in range(4):
                    copy_all(act, 1, "k%d" % c, AKT[:, c, :])
                    yield
                for i in range(NT):
                    act_copy(act, (1, "v", i), VR[:, i, :] if i < 4 else R1["v"], rows=TILES[i][1])
                    yield
                for c in range(4):
                    copy_all(act, 1, "qm%d" % c, QMT[:, c, :], float(XD) ** -0.5)
                    yield

            def keys(b):
                if b >= 2:
                    ring.full(act, ("sx", b - 2, 1))
                for half in range(2):
                    act_copy(act, ("kxT", b, half), KXT[0:64, b % 2, half * 512:(half + 1) * 512], rows=64)

            product_ = products()
            keys(0)
            for b in range(NB):
                for half in range(2):
                    if b:
                        ring.full(act, ("sw", b - 1, half))
                    bank = ring.full(act, ("sx", b, half))
                    ins = A.activation(S_RL[:, half, :], bank[:8, :], ACT.Relu, scale=float(AD) ** -0.5)
                    ring.free(ins, ("sx", b, half))
                if b + 1 < NB:
                    keys(b + 1)
                if b in PRODUCT_AT:
                    next(product_)
            for n, (i, g) in enumerate(SCORES):
                if n % SCORE_STEP == 0:
                    next(product_)
                w = (i + 1) * 128
                if n >= 2:
                    act.wait_ge(s["scored"], n - 1)
                bank = ring.full(act, ("ix", i, g))
                ins = A.activation(RLU[:, n % 2, 0:w], bank[:, 0:w], ACT.Relu, scale=float(AD) ** -0.5)
                ring.free(ins, ("ix", i, g))
            for i in range(4):
                act_copy(act, ("krow1", i), KROW[:, i, :])
            act_copy(act, ("sk1",), R1["k"], rows=NB)
            act_copy(act, ("kirow",), KIROW, n=4 * AD, view=lambda v: v.rearrange("p (i d) -> p i d", i=4))
            act_copy(act, ("rbt", 0), RBT[:, 0:512], rows=8)
            act_copy(act, ("rbt", 1), RBT[:, 512:640], rows=8, n=128)
            for half in range(2):
                act_copy(act, ("lr", half), LR[:, half * 512:(half + 1) * 512], rows=64)
            act_copy(act, ("lnew",), LR[:, PAST:PAST + 1], rows=64, n=1)
            units = [(h, i) for h in range(AH) for i in range(4)]
            act.wait_ge(s["krow_out"], 64)

            def out_heads(h):
                p0 = (h % 2) * 64
                bank = ring.full(act, ("apv", h))
                ring.free(A.activation(CT[p0:p0 + 64, h // 2, 0:SEQ], bank[p0:p0 + 64, :], ACT.Copy), ("apv", h))

            def out_sample(b):
                act_copy(act, ("spc", b), CT[:, 0:4, SEQ + b], n=4)

            for n in range(len(units) + 2):
                if n < len(units):
                    h, i = units[n]
                    w = (i + 1) * 128
                    act.wait_ge(s["amax"], n + 1)
                    if n >= 2:
                        ring.full(act, ("apT",) + units[n - 2])
                    bank = ring.full(act, ("al", h, i))
                    ring.free(A.activation(PR[:, n % 2, 0:w], bank[:, 0:w], ACT.Exp, bias=anm[:, n:n + 1],
                                           accum_out=asm[:, n:n + 1]), ("al", h, i))
                if n >= 7 and (n - 3) % 4 == 0:
                    out_heads((n - 3) // 4 - 1)
                if n == SOFTMAX_AT:
                    act.wait_ge(s["smax"], 1)
                    A.activation(LR[:, 0:PAST + 1], LR[:, 0:PAST + 1], ACT.Exp, bias=sst[:, 0:1],
                                 accum_out=sst[:, 1:2]).then_inc(s["sexp"], 1)
                if n == SOFTMAX_AT + 2:
                    act_copy(act, ("psT",), PTS, view=lambda v: v.rearrange("p (j r) -> p j r", r=64))
                if n - 1 in VALUES_AT:
                    out_sample(VALUES_AT[n - 1])
            out_heads(AH - 1)

        def act_norm(act, nth, i):
            n = TILES[i][1]
            act.wait_ge(s["lnvar"], NT * nth + i + 1)
            A.activation(std[:, i:i + 1], vare[:, i:i + 1], ACT.Sqrt).then_inc(s["lnstd"], 1)
            act.wait_ge(s["lnscale"], NT * nth + i + 1)
            A.activation(X[:n, i], X[:n, i], ACT.Identity, scale=rstd[:n, i:i + 1],
                         bias=shift[:n, i:i + 1]).then_inc(s["lnx"], 1)

        def act_memory(act, l):
            units = [(h, i) for h in range(XH) for i in range(4)]
            base = 16 * l
            act_copy(act, ("mqr", l), MQR, rows=NB)
            for n, (h, i) in enumerate(units):
                act.wait_ge(s["mmax"], base + n + 1)
                if n >= 2:
                    ring.full(act, ("mpT", l) + units[n - 2])
                bank = ring.full(act, ("ml", l, h, i))
                ring.free(A.activation(MP[:, n % 2, :], bank[:, 0:MEM], ACT.Exp, bias=mnm[:, n:n + 1],
                                       accum_out=msm[:, n:n + 1]), ("ml", l, h, i))
                if i == 3 and h >= 1:
                    act_copy(act, ("mpv", l, h - 1), CT[:, 4 + h - 1, 0:SEQ])
            act_copy(act, ("mpv", l, XH - 1), CT[:, 4 + XH - 1, 0:SEQ])
            act_copy(act, ("mlr", l), MLR, rows=32, n=MEM)
            act.wait_ge(s["msmax"], l + 1)
            A.activation(MLR, MLR, ACT.Exp, bias=mst[:, 0:1], accum_out=mst[:, 1:2]).then_inc(s["msexp"], 1)
            act_copy(act, ("msc", l), CT[:, 4:8, SEQ:TT], n=32, view=lambda v: v.rearrange("p (h b) -> p h b", b=NB))

        def act_experts(act, l):
            m = moe[l]

            def put_half(g, j, first):
                t = 4 * g + j
                act.wait_ge(m["down_done"], t)
                if not (first and j < 3):
                    act.wait_ge(m["put%d" % ((j - 1) % 2)], 16 * (2 * g + (j - 3) // 2 + 1))
                A.activation(OUT[:, (j - 1) % 2, 0:512], psum[:, 2, :], ACT.Copy).then_inc(m["out_a"], 1)

            def tokens(par, count):
                act.wait_ge(m["turned_a"], count)
                A.activation(XET[:, par, 0:4, :], psum[:, 4, :].rearrange("p (k t) -> p k t", k=4),
                             ACT.Copy).then_inc(m["xe_a"], 1)

            def step(g, j, first):
                t = 4 * g + j
                act.wait_ge(m["gu_done"], t + 1)
                if not (first and j < 2):
                    act.wait_ge(m["h_made"], t - 1)
                A.activation(SG[:, j % 2, :], psum[:, j % 2, 0:DE], ACT.Silu).then_inc(m["silu"], 1)
                tokens((j + 1) % 2, t + 2)
                if not (first and j == 0):
                    put_half(g, j, first)

            act.wait_ge(s["table_ready"], l + 1)
            groups = act.value_load(NGI[0:1, 0:1], min_val=0, max_val=(MTILES - NE) // GRP) + NE // GRP
            tokens(0, 1)
            for j in range(GRP):
                step(0, j, True)
            with act.Fori(1, groups) as g:
                for j in range(GRP):
                    step(g, j, False)
            put_half(groups, 0, False)

        @block.scalar
        def _(act):
            for i, (t0, n) in enumerate(TILES):
                copy_turned(act, ("xT", 0, i, 0), XT[:, 0:4, t0:t0 + n], n)
            for i in range(2):
                copy_turned(act, ("memT", i, 0), MT[:, 0:4, i * 128:(i + 1) * 128], 128)
            for l in range(DEPTH):
                for i in range(2):
                    act_copy(act, (l, "km", i), MKROW[:, i, :])
                if l == 0:
                    act_mlstm(act)
                else:
                    act_dsa(act)
                stage_end(act, "act")
                act_memory(act, l)
                for i in range(NT + 3):
                    if i < NT:
                        act_norm(act, 2 * l, i)
                    if i >= 3:
                        t0, n = TILES[i - 3]
                        for half in range(2):
                            copy_turned(act, ("x1T", l, i - 3, half), XT[:, 4 * half:4 * half + 4, t0:t0 + n], n)
                stage_end(act, "act")
                act.wait_ge(s["router_lin"], l + 1)
                A.activation(rg["e"], rg["c"], ACT.Exp).then_inc(s["router_exp"], 1)
                act.wait_ge(s["e2_lin"], l + 1)
                A.activation(rs["e2"], rs["d"], ACT.Exp).then_inc(s["e2_exp"], 1)
                act_experts(act, l)
                for i in range(NT + 1):
                    if i < NT:
                        act_norm(act, 2 * l + 1, i)
                    if i >= 1 and l == 0:
                        t0, n = TILES[i - 1]
                        for half in range(2):
                            copy_turned(act, ("xT", 1, i - 1, half), XT[:, 4 * half:4 * half + 4, t0:t0 + n], n)
                stage_end(act, "act")

        V = nc.vector

        def copy_turned_dve(dve, key, dst, n):
            bank = ring.full(dve, key)
            ring.free(V.tensor_copy(dst, bank[:, 0:4 * n].rearrange("p (k t) -> p k t", k=4)), key)

        def dve_copy(dve, key, dst, rows=128, n=512, c0=0, view=None):
            bank = ring.full(dve, key)[:rows, c0:c0 + n]
            if view:
                bank = view(bank)
            ring.free(V.tensor_copy(dst, bank), key)

        def heads(v, n=MH):
            return v.rearrange("p (h d) -> p h d", h=n)

        def dve_gates(dve):
            dve.wait_ge(s["gates_ln"], 1)
            V.memset(G["M"], 1.0)
            seq(dve, "dve", V.scalar_tensor_tensor(G["lf"], G["x"], 0.0, G["lf"], ALU.min, ALU.subtract))
            seq(dve, "dve", V.tensor_tensor_scan(G["B"], G["M"], G["lf"], 0.0, ALU.mult, ALU.add))
            seq(dve, "dve", V.tensor_tensor(G["a"], G["a"], G["B"], ALU.subtract))
            seq(dve, "dve", V.tensor_tensor_scan(G["M"], G["a"], G["a"], 0.0, ALU.max, ALU.max))
            seq(dve, "dve", V.tensor_tensor(G["x"], G["B"], G["M"], ALU.add))
            V.tensor_scalar(dmend, ident[:4, :4], G["M"][:, SEQ - 1:SEQ], None, ALU.mult).then_inc(s["dmend_done"], 1)
            dve.wait_ge(s["sg_ln"], 1)
            seq(dve, "dve", V.scalar_tensor_tensor(sg[:, 8:12], sg[:, 4:8], 0.0, sg[:, 12:16], ALU.min, ALU.subtract))
            seq(dve, "dve", V.tensor_tensor(sg[:, 12:16], sg[:, 8:12], sg[:, 44:48], ALU.add))
            seq(dve, "dve", V.tensor_tensor(sg[:, 16:20], sg[:, 12:16], sg[:, 0:4], ALU.max))
            V.tensor_tensor(sg[:, 20:24], sg[:, 0:4], sg[:, 16:20], ALU.subtract)
            V.tensor_tensor(sg[:, 24:28], sg[:, 12:16], sg[:, 16:20], ALU.subtract)
            V.tensor_scalar(sg[:, 28:32], sg[:, 16:20], -1.0, None, ALU.mult).then_inc(s["sg_lin2"], 1)

        def dve_mlstm(dve):
            dve.wait_ge(s_l0, 16 * 8)
            bank = ring.full(dve, (0, "gi"))
            ring.free(V.tensor_scalar(G["a"], bank[:4, :], GB[:4, 0:1], None, ALU.add), (0, "gi"))
            bank = ring.full(dve, (0, "gf"))
            ring.free(V.tensor_scalar(G["x"], bank[:4, :], GB[:4, 1:2], None, ALU.add), (0, "gf"))
            ring.read(dve, (0, "gf"))
            V.scalar_tensor_tensor(G["e"], G["x"], -1.0, G["x"], ALU.mult, ALU.min).then_inc(s["gates_lin"], 1)
            bank = ring.full(dve, (0, "gs", 4))
            ring.free(V.tensor_tensor(sg[:, 0:8], bank[:NB, 0:8], GB[:NB, 2:10], ALU.add), (0, "gs", 4))
            ring.read(dve, (0, "gs", 4))
            V.scalar_tensor_tensor(sg[:, 8:12], sg[:, 4:8], -1.0, sg[:, 4:8], ALU.mult, ALU.min).then_inc(s["sg_lin"], 1)
            ring.read(dve, (0, "cwT"))
            for half, name in enumerate(("q", "k")):
                for j in range(4):
                    c = 4 * half + j
                    bank = ring.full(dve, (0, name + str(j)))
                    seq(dve, "dve", V.tensor_scalar(QK[:, c, 0:SEQ], bank, CW[:, c, 3:4], None, ALU.mult))
                    for back in (1, 2, 3):
                        ins = V.scalar_tensor_tensor(QK[:, c, back:SEQ], bank[:, 0:SEQ - back],
                                                     CW[:, c, 3 - back:4 - back], QK[:, c, back:SEQ], ALU.mult, ALU.add)
                        if back < 3:
                            seq(dve, "dve", ins)
                    ins.then_inc(s["conv_done"], 1)
                    ring.free(V.tensor_copy(UTAIL[:, c, 0:3], bank[:, SEQ - 3:SEQ]), (0, name + str(j)))
                dve_copy(dve, (0, name + "s"), UST[:, 4 * half:4 * half + 4, :], n=32,
                         view=lambda v: v.rearrange("p (c b) -> p c b", b=NB))
                if half == 0:
                    dve_gates(dve)
            ring.read(dve, (0, "ks"))
            state = SCT.rearrange("p c (b j) -> p c b j", j=3)
            seq(dve, "dve", V.tensor_tensor(CVS[:, 1], UST, bc(CW[:, :, 3], 2, NB), ALU.mult))
            for j in range(3):
                seq(dve, "dve", V.tensor_tensor(CVS[:, 0], state[:, :, :, j], bc(CW[:, :, j], 2, NB), ALU.mult))
                ins = V.tensor_tensor(CVS[:, 1], CVS[:, 1], CVS[:, 0], ALU.add)
                if j < 2:
                    seq(dve, "dve", ins)
            ins.then_inc(s["sconv_done"], 1)
            dve_copy(dve, (0, "gcol"), gcol[:, 0:36], n=36)
            ring.read(dve, (0, "gcol"))
            V.tensor_tensor(wendC.rearrange("p (i h) -> p i h", h=4), aC.rearrange("p (i h) -> p i h", h=4),
                            bc(mendC, 1, 4), ALU.subtract).then_inc(s["exp_lin"], 1)
            dve.wait_ge(s["stanh_done"], 1)
            seq(dve, "dve", V.tensor_scalar(CVS[:, 2], CVS[:, 2], 0.5, 0.5, ALU.mult, ALU.add))
            V.tensor_tensor(QK[:, :, SEQ:TT], CVS[:, 1], CVS[:, 2], ALU.mult).then_inc(s["ssilu_done"], 1)
            units = [(h, st) for h in range(MH) for st in range(4)]
            ring.full(dve, (0, "qm3", 1))
            dve.wait_ge(s["silu_done"], 8)

            def scores(n):
                h, st = units[n]
                w = SEQ - st * 128
                dve.wait_ge(s["decay_cut"], n + 1)
                if h >= 2 and st == 0:
                    ring.full(dve, ("num", h - 2, 3))
                bank = ring.full(dve, ("score", h, st))
                ring.free(V.scalar_tensor_tensor(PT[:, h % 2, st, 0:w], bank[:, 0:w], float(MD) ** -0.5,
                                                 DD[:, n % 2, 0:w], ALU.mult, ALU.mult), ("score", h, st))

            for n, (h, st) in enumerate(units):
                w = SEQ - st * 128
                if st == 0:
                    if n:
                        scores(n - 1)
                    dve_copy(dve, ("negm", h), TH[:, h % 2, :])
                    ring.read(dve, ("negm", h))
                if n >= 2:
                    dve.wait_ge(s["decay_done"], n - 1)
                V.tensor_scalar(AR[:, n % 2, 0:w], TH[:, h % 2, st * 128:SEQ], aC[:, st * 4 + h:st * 4 + h + 1], 0.0,
                                ALU.add, ALU.min).then_inc(s["arg_done"], 1)
                if st:
                    scores(n - 1)
            scores(len(units) - 1)
            ring.read(dve, ("num", MH - 1, 3))
            dve.wait_ge(s["exp_col"], 1)
            seq(dve, "dve", V.scalar_tensor_tensor(dn, NUM[:, :, 128], -1.0, NUM[:, :, 128], ALU.mult, ALU.max))
            seq(dve, "dve", V.tensor_tensor(dn, dn, emC, ALU.max))
            seq(dve, "dve", V.reciprocal(dn, dn))
            tv = TOK[:, 0:4, :].rearrange("p i (h d) -> p (i h) d", h=MH)
            V.tensor_tensor(tv, NUM[:, :, 0:128], bc(dn, 2, 128), ALU.mult)
            stage_end(dve, "dve")

            seq(dve, "dve", V.memset(MV, 1.0))
            for g in range(16):
                ins = V.bn_stats(ST[:, g, :], TOK[:, g // 4, (g % 4) * MD:(g % 4 + 1) * MD])
            seq(dve, "dve", ins)
            for g in range(16):
                ins = V.bn_aggr(MV[:, g, :], ST[:, g, :])
            seq(dve, "dve", ins)
            V.tensor_scalar(hv[:, 0:16], MV[:, 0:16, 1], EPS, None, ALU.add).then_inc(s["var_ready"], 1)
            for st in range(4):
                bank = ring.full(dve, ("krow", st))
                for h in range(MH):
                    ins = V.tensor_scalar(KW[:, st, h * 128:(h + 1) * 128], bank[:, h * 128:(h + 1) * 128],
                                          wendC[:, st * 4 + h:st * 4 + h + 1], float(MD) ** -0.5, ALU.mult, ALU.mult)
                ring.free(ins, ("krow", st))
            dve.wait_ge(s["std_ready"], 1)
            seq(dve, "dve", V.reciprocal(hr[:, 0:16], hs_[:, 0:16]))
            V.scalar_tensor_tensor(hv[:, 0:16], MV[:, 0:16, 0], -1.0, hr[:, 0:16], ALU.mult,
                                   ALU.mult).then_inc(s["head_scale"], 1)
            bank = ring.full(dve, ("sk",))
            ring.free(V.tensor_scalar(QKR[:, MW:2 * MW], bank[:NB, :], float(MD) ** -0.5, None, ALU.mult), ("sk",))
            ring.read(dve, ("sk",))
            ring.read(dve, ("sq",))
            dve.wait_ge(s["sg_exp"], 1)
            dve.wait_ge(s["n_in"], 16)
            d_, wp_, em_ = sg[:, 20:24], sg[:, 24:28], sg[:, 28:32]
            qk_, qn_, den_, c_ = sg[:, 32:36], sg[:, 36:40], sg[:, 40:44], sg[:, 48:52]
            seq(dve, "dve", V.tensor_tensor(WPM, C("e84", NB).rearrange("p (b h) -> p b h", b=NB), bc(wp_, 1, NB), ALU.mult))
            seq(dve, "dve", V.tensor_tensor(heads(R["vd"]), heads(VS), bc(d_, 2, MD), ALU.mult))
            seq(dve, "dve", V.tensor_tensor(R["t"], QKR[:, 0:MW], QKR[:, MW:2 * MW], ALU.mult))
            seq(dve, "dve", V.tensor_reduce(qk_, heads(R["t"]), AX.X, ALU.add))
            seq(dve, "dve", V.tensor_tensor(R["t"], QKR[:, 0:MW], R["n"], ALU.mult))
            seq(dve, "dve", V.tensor_reduce(qn_, heads(R["t"]), AX.X, ALU.add))
            seq(dve, "dve", V.tensor_tensor(heads(R["n"]), heads(R["n"]), bc(wp_, 2, MD), ALU.mult))
            seq(dve, "dve", V.tensor_tensor(heads(R["t2"]), heads(QKR[:, MW:2 * MW]), bc(d_, 2, MD), ALU.mult))
            seq(dve, "dve", V.tensor_tensor(R["n"], R["n"], R["t2"], ALU.add))
            V.tensor_tensor(c_, qk_, d_, ALU.mult).then_inc(s["wp_ready"], 1)

            dve_copy(dve, ("wp",), WPB.rearrange("p b h -> p (b h)"), n=32)
            dve.wait_ge(s["c_in"], 16 * NB)
            ring.read(dve, ("wp",))
            for b in range(NB):
                bank = ring.full(dve, ("qb", b))
                ring.free(V.tensor_tensor(CTMP, CIN[:, b, :], bank, ALU.mult), ("qb", b))
                ring.read(dve, ("qb", b))
                ins = V.tensor_reduce(CQ[:, b, :], heads(CTMP), AX.X, ALU.add)
                if b == NB - 1:
                    ins.then_inc(s["cq_done"], 1)
                seq(dve, "dve", V.tensor_tensor(heads(CIN[:, b, :]), heads(CIN[:, b, :]), bc(WPB[:, b, :], 2, MD), ALU.mult))
                bank = ring.full(dve, ("vk", b))
                ring.free(V.tensor_tensor(CIN[:, b, :], CIN[:, b, :], bank, ALU.add), ("vk", b))
            seq(dve, "dve", V.tensor_tensor(heads(R["t2"]), heads(VS), bc(c_, 2, MD), ALU.mult))
            bank = ring.full(dve, ("cqT",))
            ring.free(V.tensor_tensor(heads(R["t"]), heads(bank[:NB, :]), bc(wp_, 2, MD), ALU.mult), ("cqT",))
            ring.read(dve, ("cqT",))
            seq(dve, "dve", V.tensor_tensor(R["t"], R["t"], R["t2"], ALU.add))
            seq(dve, "dve", V.tensor_tensor(den_, wp_, qn_, ALU.mult))
            seq(dve, "dve", V.tensor_tensor(den_, den_, c_, ALU.add))
            seq(dve, "dve", V.scalar_tensor_tensor(den_, den_, -1.0, den_, ALU.mult, ALU.max))
            seq(dve, "dve", V.tensor_tensor(den_, den_, em_, ALU.max))
            seq(dve, "dve", V.reciprocal(den_, den_))
            seq(dve, "dve", V.tensor_tensor(heads(TOK[:NB, 4, :]), heads(R["t"]), bc(den_, 2, MD), ALU.mult))
            for h in range(MH):
                ins = V.bn_stats(ST[:NB, 16 + h, :], TOK[:NB, 4, h * MD:(h + 1) * MD])
            seq(dve, "dve", ins)
            for h in range(MH):
                ins = V.bn_aggr(MV[:NB, 16 + h, :], ST[:NB, 16 + h, :])
            seq(dve, "dve", ins)
            V.tensor_scalar(hv[:, 16:20], MV[:, 16:20, 1], EPS, None, ALU.add).then_inc(s["var_ready"], 1)
            dve.wait_ge(s["std_ready"], 2)
            seq(dve, "dve", V.reciprocal(hr[:, 16:20], hs_[:, 16:20]))
            dve.wait_ge(s["go_ready"], NT)
            v = heads(TOK[:NB, 4, :])
            seq(dve, "dve", V.tensor_tensor(v, v, bc(MV[:NB, 16:20, 0], 2, MD), ALU.subtract))
            seq(dve, "dve", V.tensor_tensor(v, v, bc(hr[:NB, 16:20], 2, MD), ALU.mult))
            V.tensor_tensor(TOK[:NB, 4, :], TOK[:NB, 4, :], GO[:NB, 4, :], ALU.mult).then_inc(s["sample_ready"], 1)

        def dve_topk(dve, scores_, work, rounds):
            for r in range(rounds):
                src = scores_ if r == 0 else work
                seq(dve, "dve", V.max(m8[:src.shape[0]] if src.shape[0] == 128 else s8[:src.shape[0]], src))
                seq(dve, "dve", V.match_replace(work, m8[:src.shape[0]] if src.shape[0] == 128 else s8[:src.shape[0]],
                                                src, TAKEN))

        def dve_dsa(dve):
            def mask(b):
                if b >= 2:
                    ring.full(dve, ("sqb", b - 2))
                V.tensor_scalar(S_QM[:, b % 2, :], R1["q"], ident[:NB, b:b + 1], None, ALU.mult).then_inc(s["sqm"], 1)

            def keys(b):
                bank = ring.full(dve, ("sqb", b))
                for qd in range(4):
                    n = 4 * b + qd
                    dve.wait_ge(s["kv_in%d" % (n % 4)], 32 * (n // 4 + 1))
                    ins = V.tensor_tensor(KV[:, n % 4], KV[:, n % 4], bc(bank, 1, 2), ALU.mult)
                    if qd == 3:
                        ring.free(ins, ("sqb", b))
                        ring.read(dve, ("sqb", b))
                    else:
                        seq(dve, "dve", ins)
                    V.tensor_reduce(LG[:, 2 * qd:2 * qd + 2, b * 8:b * 8 + 8],
                                    KV[:, n % 4].rearrange("p j (h d) -> p j h d", h=8), AX.X,
                                    ALU.add).then_inc(s["kv_done"], 1)
                if b + 2 < NB:
                    mask(b + 2)

            ring.read(dve, ("sq1",))
            mask(0)
            mask(1)
            for c in range(4):
                for half in range(2):
                    dve_copy(dve, (1, "qi%d" % c, half), QIT[:, c, half * HALF:(half + 1) * HALF], n=HALF)
                keys(c)
            for i, (t0, n) in reversed(list(enumerate(TILES))):
                bank = ring.full(dve, (1, "wi", i))
                ring.free(V.tensor_scalar(WIP[:, i, :] if i < 4 else r1wi, bank[:n, 0:8], float(8) ** -0.5, None,
                                          ALU.mult), (1, "wi", i))
            dve_copy(dve, ("wT",), WT, rows=NB, n=NB)
            ring.read(dve, ("wT",))
            V.tensor_tensor(WM, C("del88", NB).rearrange("p (b c) -> p b c", b=NB), bc(WT, 2, NB),
                            ALU.mult).then_inc(s["wm_ready"], 1)
            for b in range(NB):
                if b < 4:
                    keys(b + 4)
                for half in range(2):
                    bank = ring.full(dve, ("sw", b, half))
                    cols = slice(half * 512, (half + 1) * 512)
                    if b == 0:
                        ins = V.tensor_copy(S_SC[:, cols], bank[:NB, :])
                    else:
                        ring.read(dve, ("sw", b - 1, half))
                        ins = V.tensor_tensor(S_SC[:, cols], S_SC[:, cols], bank[:NB, :], ALU.add)
                    ring.free(ins, ("sw", b, half))
            ring.read(dve, ("sw", NB - 1, 1))
            ring.read(dve, ("ski1",))
            seq(dve, "dve", V.tensor_tensor(heads(S_T, 8), heads(R1["qi"], 8), bc(r1ki, 1, 8), ALU.mult))
            seq(dve, "dve", V.tensor_reduce(LN8, heads(S_T, 8), AX.X, ALU.add))
            seq(dve, "dve", V.tensor_scalar(LN8, LN8, float(AD) ** -0.5, 0.0, ALU.mult, ALU.max))
            seq(dve, "dve", V.tensor_tensor(LN8, LN8, r1wi, ALU.mult))
            seq(dve, "dve", V.tensor_reduce(S_SC[:, PAST:PAST + 1], LN8, AX.X, ALU.add))
            dve_topk(dve, S_SC[:, 0:PAST + 1], S_WK[:, 0:PAST + 1], TOPK_S // 8)
            V.tensor_scalar(S_WK[:, 0:PAST + 1], S_WK[:, 0:PAST + 1], -2.5e38, NEG, ALU.is_gt,
                            ALU.mult).then_inc(s["smask"], 1)
            ring.read(dve, ("sk1",))
            seq(dve, "dve", V.tensor_tensor(S_T, R1["q"], R1["k"], ALU.mult))
            seq(dve, "dve", V.tensor_reduce(LN8, heads(S_T, 8), AX.X, ALU.add))
            e8 = C("e8", NB).rearrange("p (b h) -> p b h", b=NB)
            V.tensor_tensor(LNM, e8, bc(LN8, 1, NB), ALU.mult).then_inc(s["lnew"], 1)
            V.tensor_copy(MASK[:, 0, 0:128], C("causal")).then_inc(s["mask_ready"], 1)
            for i in range(1, 4):
                w = (i + 1) * 128
                dve.wait_ge(s["cut"], i)
                dve_topk(dve, SC[i][:, 0:w], SC[i][:, 0:w], TOPK_P // 8)
                V.tensor_scalar(MASK[:, i, 0:w], SC[i][:, 0:w], -2.5e38, NEG, ALU.is_gt,
                                ALU.mult).then_inc(s["mask_ready"], 1)
            units = [(h, i) for h in range(AH) for i in range(4)]
            ring.full(dve, (1, "qm3", 1))
            for n in range(len(units) + 2):
                if n < len(units):
                    h, i = units[n]
                    bank = ring.full(dve, ("al", h, i))
                    V.tensor_reduce(anm[:, n:n + 1], bank[:, 0:(i + 1) * 128], AX.X, ALU.max,
                                    negate=True).then_inc(s["amax"], 1)
                if 1 <= n <= len(units):
                    h, i = units[n - 1]
                    w = (i + 1) * 128
                    ring.read(dve, ("al", h, i))
                    seq(dve, "dve", V.reciprocal(ars[:, n - 1:n], asm[:, n - 1:n]))
                    V.tensor_scalar(PR[:, (n - 1) % 2, 0:w], PR[:, (n - 1) % 2, 0:w], ars[:, n - 1:n], None,
                                    ALU.mult).then_inc(s["anorm"], 1)
                if n >= 2:
                    h, i = units[n - 2]
                    if h >= 2 and i == 0:
                        ring.full(dve, ("apv", h - 2))
                    dve_copy(dve, ("apT", h, i), PTA[:, h % 2, 0:i + 1, i * 128:(i + 1) * 128], n=(i + 1) * 128,
                             view=lambda v: v.rearrange("p (j t) -> p j t", t=128))
                if n == SOFTMAX_AT:
                    ring.read(dve, ("lnew",))
                    V.tensor_reduce(sst[:, 0:1], LR[:, 0:PAST + 1], AX.X, ALU.max, negate=True).then_inc(s["smax"], 1)
                    dve.wait_ge(s["sexp"], 1)
                    seq(dve, "dve", V.reciprocal(sst[:, 2:3], sst[:, 1:2]))
                    V.tensor_scalar(LR[:, 0:PAST + 1], LR[:, 0:PAST + 1], sst[:, 2:3], None,
                                    ALU.mult).then_inc(s["snorm"], 1)
                    dve.wait_ge(s["snorm"], 1)
                    V.tensor_scalar(PN, C("hsel", 64), LR[:, PAST:PAST + 1], None, ALU.mult).then_inc(s["pnew"], 1)
                if n == SOFTMAX_AT + 2:
                    dve_copy(dve, ("p8",), P8, rows=NB, n=8)
                    ring.read(dve, ("p8",))
                    V.tensor_tensor(PM8, e8, bc(P8, 1, NB), ALU.mult).then_inc(s["pm8"], 1)
                if n in VALUES_AT:
                    b = VALUES_AT[n]
                    if b >= 2:
                        ring.full(dve, ("spc", b - 2))
                    bank = ring.full(dve, ("spv", b))
                    ring.free(V.tensor_tensor(heads(OWN[:, b % 2, :], 8), heads(bank[:8, :], 8),
                                              bc(C("ident", 8)[:, 0:8], 2, AD), ALU.mult), ("spv", b))

        def dve_memory(dve, l):
            units = [(h, i) for h in range(XH) for i in range(4)]

            def mask(b):
                if b >= 2:
                    ring.full(dve, ("mqb", l, b - 2))
                V.tensor_scalar(MQM[:, b % 2, :], MQR, ident[:NB, b:b + 1], None, ALU.mult).then_inc(s["mqmask"], 1)

            V.memset(MPM, 0.0)
            ring.read(dve, ("mqr", l))
            mask(0)
            mask(1)

            def keys(b):
                dve.wait_ge(s["mk_in%d" % (b % 2)], 16 * (4 * l + b // 2 + 1))
                bank = ring.full(dve, ("mqb", l, b))
                ring.free(V.tensor_tensor(MK2[:, b % 2], MK2[:, b % 2], bc(bank, 1, 2), ALU.mult), ("mqb", l, b))
                ring.read(dve, ("mqb", l, b))
                V.tensor_reduce(MLG[:, :, b * 4:b * 4 + 4], MK2[:, b % 2].rearrange("p j (h d) -> p j h d", h=XH),
                                AX.X, ALU.add).then_inc(s["mk_used"], 1)
                if b + 2 < NB:
                    mask(b + 2)

            for n in range(len(units) + 2):
                if n < len(units):
                    bank = ring.full(dve, ("ml", l) + units[n])
                    V.tensor_reduce(mnm[:, n:n + 1], bank[:, 0:MEM], AX.X, ALU.max, negate=True).then_inc(s["mmax"], 1)
                if 1 <= n <= len(units):
                    ring.read(dve, ("ml", l) + units[n - 1])
                    seq(dve, "dve", V.reciprocal(mrs[:, n - 1:n], msm[:, n - 1:n]))
                    V.tensor_scalar(MP[:, (n - 1) % 2, :], MP[:, (n - 1) % 2, :], mrs[:, n - 1:n], None,
                                    ALU.mult).then_inc(s["mnorm"], 1)
                if n >= 2:
                    h, i = units[n - 2]
                    if h >= 2 and i == 0:
                        ring.full(dve, ("mpv", l, h - 2))
                    dve_copy(dve, ("mpT", l, h, i), MPT[:, h % 2, :, i * 128:(i + 1) * 128], n=MEM,
                             view=lambda v: v.rearrange("p (j t) -> p j t", t=128))
                    if n % 2 == 0 and n // 2 - 1 < NB:
                        keys(n // 2 - 1)
            ring.read(dve, ("mlr", l))
            V.tensor_reduce(mst[:, 0:1], MLR, AX.X, ALU.max, negate=True).then_inc(s["msmax"], 1)
            dve.wait_ge(s["msexp"], l + 1)
            seq(dve, "dve", V.reciprocal(mst[:, 2:3], mst[:, 1:2]))
            V.tensor_scalar(MLR, MLR, mst[:, 2:3], None, ALU.mult).then_inc(s["msnorm"], 1)
            at = MPM[:, 0:1, 0:1, 0:1]
            diagonal = bass.AP(at.tensor, at.offset, [at.ap[0], [2 * 32 + XH, NB], [32, 2], [1, XH]])
            bank = ring.full(dve, ("mps", l))
            ring.free(V.tensor_copy(diagonal, bank[:, 0:64].rearrange("p (j b h) -> p b j h", j=2, b=NB)), ("mps", l))
            bank = ring.full(dve, ("msv", l))
            ring.free(V.tensor_tensor(heads(MOWN), heads(bank[:32, :]), bc(C("h32", 32), 2, XD), ALU.mult), ("msv", l))

        def dve_norm_stats(dve, nth, i):
            n = TILES[i][1]
            V.bn_stats(stats[:n, 0], X[:n, i, 0:512])
            seq(dve, "dve", V.bn_stats(stats[:n, 1], X[:n, i, 512:1024]))
            seq(dve, "dve", V.bn_aggr(moments[:n, i, :], stats[:n].rearrange("p a b -> p (a b)")))
            V.tensor_scalar(vare[:, i:i + 1], moments[:, i, 1:2], EPS, None, ALU.add).then_inc(s["lnvar"], 1)

        def dve_norm_bias(dve, nth, i, gb):
            n = TILES[i][1]
            dve.wait_ge(s["gained"], NT * nth + i + 1)
            V.tensor_tensor(X[:n, i], X[:n, i], gb[:n, 1], ALU.add).then_inc(s["x_norm"], 1)

        def dve_norm_scale(dve, nth, i):
            dve.wait_ge(s["lnstd"], NT * nth + i + 1)
            seq(dve, "dve", V.reciprocal(rstd[:, i:i + 1], std[:, i:i + 1]))
            V.scalar_tensor_tensor(shift[:, i:i + 1], moments[:, i, 0:1], -1.0, rstd[:, i:i + 1], ALU.mult,
                                   ALU.mult).then_inc(s["lnscale"], 1)

        def dve_route(dve, l):
            S = lambda ins: seq(dve, "dve", ins)
            S(V.memset(RL, 0.0))
            S(V.memset(rt["pos"], 0.0))
            dve.wait_ge(s["router_in"], 64 * (l + 1))
            bank = ring.full(dve, (l, "router0"))
            ring.free(V.tensor_tensor(RL[:, 0:4, :], bank[:, 0:144].rearrange("p (i e) -> p i e", e=36), bc(BR, 1, 4),
                                      ALU.add), (l, "router0"))
            bank = ring.full(dve, (l, "router1"))
            ring.free(V.tensor_tensor(RL[:NB, 4, :], bank[:NB, 144:180], BR[:NB], ALU.add), (l, "router1"))
            ring.read(dve, (l, "router1"))
            GL, EL = RL[:, :, 0:NG], RL[:, :, NG:NG + NE]
            iota = bc(C("iota"), 1, NT)

            def first_max(logit, top_, eq, c, oh, n):
                S(V.tensor_tensor(eq, logit, bc(top_, 2, n), ALU.is_equal))
                S(V.scalar_tensor_tensor(c, eq, -64.0, iota[:, :, 0:n], ALU.mult, ALU.add))
                S(V.tensor_reduce(rs["mn"], c, AX.X, ALU.min))
                S(V.tensor_tensor(oh, c, bc(rs["mn"], 2, n), ALU.is_equal))

            S(V.tensor_reduce(rs["gm"], GL, AX.X, ALU.max))
            V.tensor_tensor(rg["c"], GL, bc(rs["gm"], 2, NG), ALU.subtract).then_inc(s["router_lin"], 1)
            dve.wait_ge(s["router_exp"], l + 1)
            S(V.tensor_reduce(rs["gw"], rg["e"], AX.X, ALU.add))
            S(V.reciprocal(rs["gw"], rs["gw"]))
            first_max(GL, rs["gm"], rg["eq"], rg["c"], rg["oh"], NG)
            S(V.tensor_scalar(rg["c"], rg["oh"], -1.0, -NEG, ALU.add, ALU.mult))
            S(V.tensor_tensor(rt["l2"].rearrange("p i (g e) -> p i g e", g=NG), EL.rearrange("p i (g e) -> p i g e", g=NG),
                              bc(rg["c"], 3, EPG), ALU.add))
            S(V.tensor_reduce(rs["m1"], rt["l2"], AX.X, ALU.max))
            first_max(rt["l2"], rs["m1"], rt["eq"], rt["c"], rt["oh1"], NE)
            S(V.tensor_scalar(r2["e"][:, 0:NT], rs["mn"], 64.0, None, ALU.add))
            S(V.scalar_tensor_tensor(rt["l3"], rt["oh1"], 3.0 * NEG, rt["l2"], ALU.mult, ALU.add))
            S(V.tensor_reduce(rs["m2"], rt["l3"], AX.X, ALU.max))
            V.tensor_tensor(rs["d"], rs["m2"], rs["m1"], ALU.subtract).then_inc(s["e2_lin"], 1)
            first_max(rt["l3"], rs["m2"], rt["eq"], rt["c"], rt["oh2"], NE)
            V.tensor_tensor(rt["both"], rt["oh1"], rt["oh2"], ALU.add).then_inc(s["route_ready"], 1)
            V.tensor_copy(TOKI, C("tokid"))
            S(V.tensor_scalar(r2["e"][:, NT:2 * NT], rs["mn"], 64.0, None, ALU.add))
            dve.wait_ge(s["e2_exp"], l + 1)
            S(V.tensor_scalar(rs["w1"], rs["e2"], 1.0, None, ALU.add))
            S(V.reciprocal(rs["w1"], rs["w1"]))
            S(V.tensor_tensor(rs["g1"], rs["gw"], rs["w1"], ALU.mult))
            S(V.tensor_tensor(rs["g2"], rs["g1"], rs["e2"], ALU.mult))

            bank = ring.full(dve, (l, "before"))
            V.tensor_copy(rt["pos"][:, 0:4, :], bank[:, 0:128].rearrange("p (i e) -> p i e", e=NE))
            V.tensor_copy(rt["pos"][:NB, 4, :], bank[:NB, 128:160])
            ring.free(V.tensor_copy(cnt, bank[:, 160:192]), (l, "before"))
            ring.read(dve, (l, "before"))
            S(V.tensor_scalar(over, cnt, 128.0, None, ALU.is_gt))
            for k in (2, 3, 4):
                S(V.scalar_tensor_tensor(over, cnt, 128.0 * k, over, ALU.is_gt, ALU.add))
            S(V.tensor_tensor_scan(incl, C("ones")[:, 0:NE], over, 0.0, ALU.mult, ALU.add))
            S(V.tensor_tensor(excl, incl, over, ALU.subtract))
            for r, oh in ((0, "oh1"), (1, "oh2")):
                cols = slice(r * NT, (r + 1) * NT)
                S(V.tensor_tensor(rt["t"], rt[oh], rt["pos"], ALU.mult))
                V.tensor_reduce(r2["p"][:, cols], rt["t"], AX.X, ALU.add)
                S(V.tensor_tensor(rt["l3"], rt[oh], bc(excl, 1, NT), ALU.mult))
                S(V.tensor_reduce(r2["ot"][:, cols], rt["l3"], AX.X, ALU.add))
            S(V.tensor_scalar(r2["q"], r2["p"], 128.0, None, ALU.is_ge))
            for k in (2, 3, 4):
                S(V.scalar_tensor_tensor(r2["q"], r2["p"], 128.0 * k, r2["q"], ALU.is_ge, ALU.add))
            S(V.tensor_tensor(r2["t"], r2["ot"], r2["q"], ALU.add))
            S(V.scalar_tensor_tensor(r2["t"], r2["t"], float(NE - 1), r2["e"], ALU.add, ALU.subtract))
            S(V.scalar_tensor_tensor(r2["t"], r2["q"], 0.0, r2["t"], ALU.is_gt, ALU.mult))
            S(V.tensor_tensor(r2["t"], r2["t"], r2["e"], ALU.add))
            S(V.scalar_tensor_tensor(r2["p"], r2["q"], -128.0, r2["p"], ALU.mult, ALU.add))
            S(V.scalar_tensor_tensor(r2["cell"], r2["p"], float(LW), r2["t"], ALU.mult, ALU.add))
            V.tensor_copy(CELLI.rearrange("p r i -> p (r i)"), r2["cell"]).then_inc(s["cells_ready"], 1)
            S(V.scalar_tensor_tensor(r2["row"], r2["t"], 128.0, r2["p"], ALU.mult, ALU.add))
            V.tensor_copy(ROWI.rearrange("p r i -> p (r i)"), r2["row"])
            S(V.tensor_scalar(ngf[:, 0:1], incl[:, NE - 1:NE], 0.0, None, ALU.is_gt))
            S(V.scalar_tensor_tensor(ngf[:, 1:2], incl[:, NE - 1:NE], float(GRP), ngf[:, 0:1], ALU.is_gt, ALU.add))
            V.tensor_copy(NGI, ngf[:, 1:2])
            S(V.tensor_tensor(et1, bc(excl, 1, 8), bc(C("iota8"), 2, NE), ALU.is_le))
            S(V.tensor_tensor(et2, bc(incl, 1, 8), bc(C("iota8"), 2, NE), ALU.is_gt))
            S(V.tensor_tensor(et1, et1, et2, ALU.mult))
            S(V.tensor_tensor(et1, et1, bc(C("iota"), 1, 8), ALU.mult))
            S(V.tensor_reduce(et3, et1, AX.X, ALU.add))
            V.tensor_copy(ETI, et3).then_inc(s["table_ready"], 1)

        def dve_experts(dve, l):
            m = moe[l]

            def put_half(g, j, first):
                dve.wait_ge(m["down_done"], 4 * g + j)
                if not (first and j < 3):
                    dve.wait_ge(m["put%d" % ((j - 1) % 2)], 16 * (2 * g + (j - 3) // 2 + 1))
                V.tensor_copy(OUT[:, (j - 1) % 2, 512:1024], psum[:, 3, :]).then_inc(m["out_b"], 1)

            def tokens(par, count):
                dve.wait_ge(m["turned_b"], count)
                V.tensor_copy(XET[:, par, 4:8, :], psum[:, 5, :].rearrange("p (k t) -> p k t", k=4)).then_inc(m["xe_b"], 1)

            def step(g, j, first):
                t = 4 * g + j
                dve.wait_ge(m["silu"], t + 1)
                if not (first and j == 0):
                    dve.wait_ge(m["h_turned"], t)
                V.tensor_tensor(HH, SG[:, j % 2, :], psum[:, j % 2, DE:2 * DE], ALU.mult).then_inc(m["h_made"], 1)
                tokens((j + 1) % 2, t + 2)
                if not (first and j == 0):
                    put_half(g, j, first)
                dve.wait_ge(m["h_turned"], t + 1)
                V.tensor_copy(HT.rearrange("p q t -> p (q t)"), psum[:, 6, 0:256]).then_inc(m["ht_ready"], 1)

            dve.wait_ge(s["x1_out"], 16 * NT * (l + 1))
            for i, (t0, n) in enumerate(TILES):
                V.tensor_scalar(X[:n, i], X[:n, i], ALPHA, None, ALU.mult)
            groups = dve.value_load(NGI[0:1, 0:1], min_val=0, max_val=(MTILES - NE) // GRP) + NE // GRP
            tokens(0, 1)
            for j in range(GRP):
                step(0, j, True)
            with dve.Fori(1, groups) as g:
                for j in range(GRP):
                    step(g, j, False)
            put_half(groups, 0, False)
            return groups

        @block.vector
        def _(dve):
            seq(dve, "dve", V.memset(small, 1.0))
            for i, (t0, n) in enumerate(TILES):
                copy_turned_dve(dve, ("xT", 0, i, 1), XT[:, 4:8, t0:t0 + n], n)
            for i in range(2):
                copy_turned_dve(dve, ("memT", i, 1), MT[:, 4:8, i * 128:(i + 1) * 128], 128)
            for l in range(DEPTH):
                for i in range(2):
                    dve_copy(dve, (l, "vm", i), VM[:, i, :])
                for hp in range(2):
                    dve_copy(dve, (l, "kmT", hp), KMT[:, 2 * hp:2 * hp + 2, :].rearrange("p h s -> p (h s)"))
                if l == 0:
                    dve_mlstm(dve)
                else:
                    dve_dsa(dve)
                stage_end(dve, "dve")
                dve_memory(dve, l)
                dve.wait_ge(s_ln, 32 * (l + 1))
                for i in range(NT + 2):
                    if i < NT:
                        n = TILES[i][1]
                        for half in range(2):
                            bank = ring.full(dve, (l, "y", half, i))
                            cols = slice(half * 512, (half + 1) * 512)
                            ring.free(V.scalar_tensor_tensor(X[:n, i, cols], X[:n, i, cols], ALPHA, bank[:n, :],
                                                             ALU.mult, ALU.add), (l, "y", half, i))
                        ring.read(dve, (l, "y", 1, i))
                        dve_norm_stats(dve, 2 * l, i)
                    if 1 <= i <= NT:
                        dve_norm_scale(dve, 2 * l, i - 1)
                    if i >= 2:
                        dve_norm_bias(dve, 2 * l, i - 2, lng)
                stage_end(dve, "dve")
                dve_route(dve, l)
                groups = dve_experts(dve, l)
                dve.wait_ge(moe[l]["put0"], 32 * groups)
                dve.wait_ge(moe[l]["put1"], 32 * groups)
                V.tensor_copy(ngf[:, 0:1], ngf[:, 1:2]).then_inc(s["experts_out"], 1)
                dve.wait_ge(s["lnf_in"], 32 * (l + 1))
                for i in range(NT + 2):
                    if i < NT:
                        n = TILES[i][1]
                        dve.wait_ge(s["y_in%d" % i], 32 * (l + 1))
                        seq(dve, "dve", V.scalar_tensor_tensor(X[:n, i], YG[:n, i, 0, :], rs["g1"][:n, i:i + 1],
                                                               X[:n, i], ALU.mult, ALU.add))
                        seq(dve, "dve", V.scalar_tensor_tensor(X[:n, i], YG[:n, i, 1, :], rs["g2"][:n, i:i + 1],
                                                               X[:n, i], ALU.mult, ALU.add))
                        dve_norm_stats(dve, 2 * l + 1, i)
                    if 1 <= i <= NT:
                        dve_norm_scale(dve, 2 * l + 1, i - 1)
                    if i >= 2:
                        dve_norm_bias(dve, 2 * l + 1, i - 2, lnf)
                stage_end(dve, "dve")

        P = nc.gpsimd

        def store(pool, out, in_):
            stored[0] += 1
            pool.dma_start(out, in_).then_inc(s_st, 16)

        def pool_stage_end(pool):
            pool.wait_ge(s_st, 16 * stored[0])
            stage_end(pool, "pool")

        def pool_norm(pool, nth, i, gb):
            n = TILES[i][1]
            pool.wait_ge(s["lnx"], NT * nth + i + 1)
            P.tensor_tensor(X[:n, i], X[:n, i], gb[:n, 0], ALU.mult).then_inc(s["gained"], 1)

        def pool_mlstm(pool):
            P.memset(VA[:, :, :, 128:130], 1.0).then_inc(s["vones"], 1)
            for c in range(8):
                pool.wait_ge(s["tanh_done"], c + 1)
                seq(pool, "pool", P.tensor_scalar(TH[:, c % 2, :], TH[:, c % 2, :], 0.5, 0.5, ALU.mult, ALU.add))
                P.tensor_tensor(QK[:, c, 0:SEQ], QK[:, c, 0:SEQ], TH[:, c % 2, :], ALU.mult).then_inc(s["silu_done"], 1)
            pool.wait_ge(s_x, 32)
            for t in range(NE, MTILES, 4):
                store(pool, scratch["y"][t * 128:(t + 4) * 128, :].rearrange("(i p) d -> p i d", p=128), X[:, 0:4, :])
            pool.wait_ge(s_l0, 16 * 8)
            for i, (t0, n) in enumerate(TILES):
                ring.read(pool, (0, "o", i))
                seq(pool, "pool", P.tensor_scalar(GO[:n, i], GO[:n, i], 0.5, 0.5, ALU.mult, ALU.add))
                P.tensor_tensor(GO[:n, i], GO[:n, i], NGB[:n], ALU.mult).then_inc(s["go_ready"], 1)
            for n in range(16):
                pool.wait_ge(s["decay_done"], n + 1)
                P.affine_select(out=DD[:, n % 2, 0:128], in_=DD[:, n % 2, 0:128], pattern=[[1, 128]],
                                compare_op=ALU.is_ge, fill=0.0, base=0, channel_multiplier=-1).then_inc(s["decay_cut"], 1)
            pool.wait_ge(s["dmend_done"], 1)
            store(pool, o["state_m_prompt"][0, 0].unsqueeze(1), G["x"][:, SEQ - 1:SEQ])
            pool_stage_end(pool)
            store(pool, o["state_m_sample"][0], sg[:, 16:20])
            for j in range(2):
                ring.read(pool, ("su", j))
            pool.dma_start(o["state_conv_sample"][0, :, 2, :], UR).then_inc(s["urow"], 16)
            store(pool, o["state_conv_sample"][0, :, 0:2, :], a["state_conv"][0, :, 1:3, :])
            for j in range(2):
                ring.read(pool, ("pu", j))
            store(pool, o["state_conv_prompt"][0, 0], UPR)
            ring.read(pool, ("newC",))
            store(pool, o["state_C_prompt"][0, 0].rearrange("h v k -> v h k"), CS)
            ring.read(pool, ("newn",))
            store(pool, o["state_n_prompt"][0].rearrange("b h k -> b (h k)"), NNR)
            pool.wait_ge(s["wp_ready"], 1)
            store(pool, o["state_n_sample"][0].rearrange("b h k -> b (h k)"), R["n"])
            for b in range(NB):
                if b < 4:
                    pool.wait_ge(s["head_norm"], b + 1)
                    P.tensor_tensor(TOK[:, b, :], TOK[:, b, :], GO[:, b, :], ALU.mult).then_inc(s["tok_ready"], 1)
                ring.read(pool, ("vk", b))
                store(pool, o["state_C_sample"][0, b].rearrange("h v k -> v h k"), heads(CIN[:, b, :]))

        def pool_dsa(pool):
            pool.wait_ge(s_l1, 16 * 5)
            seq(pool, "pool", P.tensor_copy(RB64, bc(RB, 1, NB)))
            ring.read(pool, (1, "wi", 0))
            n = 0
            for i in range(1, 4):
                w, w0 = (i + 1) * 128, i * 128
                for g in range(8):
                    ring.read(pool, ("ix", i, g))
                    if g == 0:
                        ins = P.tensor_scalar(SC[i][:, 0:w], RLU[:, n % 2, 0:w], WIP[:, i, g:g + 1], None, ALU.mult)
                    else:
                        seq(pool, "pool", P.tensor_scalar(RLU[:, n % 2, 0:w], RLU[:, n % 2, 0:w], WIP[:, i, g:g + 1],
                                                          None, ALU.mult))
                        pool.wait_ge(s["scored"], n)
                        ins = P.tensor_tensor(SC[i][:, 0:w], SC[i][:, 0:w], RLU[:, n % 2, 0:w], ALU.add)
                    ins.then_inc(s["scored"], 1)
                    n += 1
                pool.wait_ge(s["scored"], 8 * i)
                P.affine_select(out=SC[i][:, w0:w], in_=SC[i][:, w0:w], pattern=[[-1, 128]],
                                compare_op=ALU.is_ge, fill=NONE, base=0, channel_multiplier=1).then_inc(s["cut"], 1)
            for j in range(2):
                ring.read(pool, ("rbt", j))
            pool.dma_start(scratch["bias"], RBT).then_inc(s["rbt_out"], 16)
            for i in range(4):
                ring.read(pool, (1, "v", i))
                store(pool, o["new_v_prompt"][0, 0, i * 128:(i + 1) * 128].rearrange("t h d -> t (h d)"), VR[:, i, :])
            ring.read(pool, (1, "v", 4))
            store(pool, o["new_v_sample"][0, :, 0].rearrange("t h d -> t (h d)"), R1["v"])
            for i in range(4):
                ring.read(pool, ("krow1", i))
                pool.dma_start(o["new_k_prompt"][0, 0, i * 128:(i + 1) * 128].rearrange("t h d -> t (h d)"),
                               KROW[:, i, :]).then_inc(s["krow_out"], 16)
            ring.read(pool, ("sk1",))
            store(pool, o["new_k_sample"][0, :, 0].rearrange("t h d -> t (h d)"), R1["k"])
            ring.read(pool, ("kirow",))
            store(pool, o["new_kidx_prompt"][0, 0].rearrange("(i p) d -> p i d", p=128), KIROW)
            ring.read(pool, ("ski1",))
            store(pool, o["new_kidx_sample"][0, :, 0], r1ki)
        def pool_experts(pool, l):
            m = moe[l]
            xd = scratch["x1_%d" % l]
            seq(pool, "pool", P.memset(LZ.bitcast(F32), 0.0))
            ids = scratch["ids_%d" % l]
            pool.dma_start(ids.rearrange("(p t) a -> p (t a)", t=LW), LZ).then_inc(s["zeroed"], 16)
            pool.wait_ge(s["cells_ready"], l + 1)
            pool.wait_ge(s["zeroed"], 16 * (l + 1))
            for r in range(2):
                for i, (t0, n) in enumerate(TILES):
                    P.indirect_dma_start(ids, bass.IndirectOffsetOnAxis(ap=CELLI[:n, r, i:i + 1], axis=0),
                                         TOKI[:n, i:i + 1], None).then_inc(s["scattered"], 16)
            pool.wait_ge(s["scattered"], 16 * 2 * NT * (l + 1))
            pool.dma_start(LST, ids.rearrange("(p t) a -> p (t a)", t=LW)).then_inc(s["ids_in"], 16)
            pool.wait_ge(s["ids_in"], 16 * (l + 1))
            pool.wait_ge(s["table_ready"], l + 1)
            groups = pool.value_load(NGI[0:1, 0:1], min_val=0, max_val=(MTILES - NE) // GRP) + NE // GRP

            def pick(t, j):
                P.tensor_copy(IDX[:, j:j + 1], LST[:, bass.ds(t, 1)]).then_inc(m["picked"], 1)

            def fetch(t, j, first):
                pool.wait_ge(m["picked"], t + 1)
                if not (first and t < 2):
                    pool.wait_ge(m["turned_a"], t - 1)
                    pool.wait_ge(m["turned_b"], t - 1)
                pick(t + 1, (j + 1) % GRP)
                P.indirect_dma_start(XE[:, j % 2, :], None, xd, bass.IndirectOffsetOnAxis(ap=IDX[:, j:j + 1], axis=0)
                                     ).then_inc(m["gathered%d" % (j % 2)], 16)

            pick(0, 0)
            for t in range(GRP + 1):
                fetch(t, t % GRP, True)
            with pool.Fori(1, groups) as g:
                for j in range(1, GRP + 1):
                    fetch(4 * g + j, j % GRP, False)
            pool.wait_ge(s["experts_out"], l + 1)
            for i, (t0, n) in enumerate(TILES):
                for r in range(2):
                    P.indirect_dma_start(YG[:n, i, r, :], None, scratch["y"],
                                         bass.IndirectOffsetOnAxis(ap=ROWI[:n, r, i:i + 1], axis=0)
                                         ).then_inc(s["y_in%d" % i], 16)

        @block.gpsimd
        def _(pool):
            for l in range(DEPTH):
                for i in range(2):
                    ring.read(pool, (l, "km", i))
                    store(pool, o["mem_k_prompt"][l, 0, i * 128:(i + 1) * 128].rearrange("s h d -> s (h d)"),
                          MKROW[:, i, :])
                    ring.read(pool, (l, "vm", i))
                    store(pool, o["mem_v_prompt"][l, 0, i * 128:(i + 1) * 128].rearrange("s h d -> s (h d)"),
                          VM[:, i, :])
                if l == 0:
                    pool_mlstm(pool)
                else:
                    pool_dsa(pool)
                pool_stage_end(pool)
                pool.wait_ge(s_ln, 32 * (l + 1))
                for i in range(NT + 1):
                    if i < NT:
                        pool_norm(pool, 2 * l, i, lng)
                    if i >= 1:
                        t0, n = TILES[i - 1]
                        pool.wait_ge(s["x_norm"], 2 * NT * l + i)
                        pool.dma_start(scratch["x1_%d" % l][t0:t0 + n, :], X[:n, i - 1]).then_inc(s["x1_out"], 16)
                pool.wait_ge(s["x1_out"], 16 * NT * (l + 1))
                pool_stage_end(pool)
                pool_experts(pool, l)
                pool.wait_ge(s["lnf_in"], 32 * (l + 1))
                for i in range(NT + 1):
                    if i < NT:
                        pool_norm(pool, 2 * l + 1, i, lnf)
                    if i >= 1 and l == DEPTH - 1:
                        t0, n = TILES[i - 1]
                        pool.wait_ge(s["x_norm"], 2 * NT * l + NT + i)
                        store(pool, o["y_prompt"][0, t0:t0 + n, :] if i <= 4 else o["y_sample"][:, 0, :], X[:n, i - 1])
                pool_stage_end(pool)

        def sync_small0(sp):
            w = a["w_in_mlstm"][0]
            sp.dma_start(GW, w[:, 2048:2056].rearrange("(p k) n -> p k n", k=KD)).then_inc(s_l0, 16)
            sp.dma_start(CWR, a["conv_mlstm"][0]).then_inc(s_l0, 16)
            sp.dma_start(SCR, a["state_conv"][0].rearrange("b j c -> (b j) c")).then_inc(s_l0, 16)
            g = a["b_gates_mlstm"][0]
            sp.dma_start(GB[:4, 0:1], g[0:4].unsqueeze(1)).then_inc(s_l0, 16)
            sp.dma_start(GB[:4, 1:2], g[4:8].unsqueeze(1)).then_inc(s_l0, 16)
            sp.dma_start(GB[:NB, 2:10], g.partition_broadcast(NB)).then_inc(s_l0, 16)
            sp.dma_start(NGB, a["norm_mlstm"][0].partition_broadcast(128)).then_inc(s_l0, 16)
            sp.dma_start(sg[:, 44:48], a["state_m"][0]).then_inc(s_l0, 16)

        def sync_chunk(sp, l, name):
            i = chunk_no[(l, name)]
            if i >= 2:
                sp.wait_ge(ring.filled, chunk_last[i - 2])
            sp.dma_start(WS[:, i % 2], chunks[i][2]).then_inc(chunk_in[i % 2], 16)

        def sync_norm(sp, l):
            for q, n in enumerate(("ln_mix_g", "ln_mix_b")):
                sp.dma_start(lng[:, q, :], a[n][l].partition_broadcast(128)).then_inc(s_ln, 16)

        def sync_dsa(sp):
            def page(n):
                return sp.value_load(PTB[0:1, n:n + 1], min_val=0, max_val=NPOOL - 1)

            def index_keys(b):
                if b >= 2:
                    ring.full(sp, ("kxT", b - 2, 1))
                for j in range(NPG):
                    sp.dma_start(KIX[:, b % 2, j, :],
                                 a["cache_kidx"][0, bass.ds(page(b * NPG + j), 1)].rearrange("a r d -> (a r) d")
                                 ).then_inc(s["kix_in%d" % (b % 2)], 16)

            def pages(cache, at, dst, arrived):
                for j in range(2):
                    sp.dma_start(dst[:, j, :], cache[0, bass.ds(page(at + j), 1)].rearrange("a r h d -> (a r) (h d)")
                                 ).then_inc(arrived, 16)

            def keys(b):
                for q in range(4):
                    n = 4 * b + q
                    if b >= 1:
                        sp.wait_ge(s["kv_done"], n - 3)
                    pages(a["cache_k"], 2 * n, KV[:, q], s["kv_in%d" % q])

            def values(b):
                for q in range(4):
                    if b == 0 and q == 0:
                        sp.wait_ge(ring.filled, chunk_last[chunk_no[(1, "qm")]])
                    if b >= 1:
                        if q < 3:
                            sp.wait_ge(s["v_used"], 3 * (b - 1) + q + 1)
                        else:
                            ring.full(sp, ("spv", b - 1))
                    pages(a["cache_v"], 8 * b + 2 * q, VV[:, q], s["v_in%d" % q])

            def bias(h):
                if h >= 2:
                    ring.full(sp, ("al", h - 2, 3))
                v = scratch["bias"][h, 0:512]
                sp.dma_start(HK[:, h % 2, :], bass.AP(v.tensor, v.offset, [[1, 128], [1, 512]])
                             ).then_inc(s["hk_in%d" % (h % 2)], 16)

            for name in ("q", "qi"):
                sync_chunk(sp, 1, name)
            sp.wait_ge(s_l1, 16 * 5)
            keys(0)
            keys(1)
            index_keys(0)
            keys(2)
            index_keys(1)
            keys(3)
            sync_chunk(sp, 1, "k")
            sync_chunk(sp, 1, "v")
            for b in range(1, NB):
                if b + 1 < NB:
                    index_keys(b + 1)
                if b <= 4:
                    keys(b + 3)
                if b == 6:
                    sync_chunk(sp, 1, "qm")
            sync_chunk(sp, 1, "wo0")
            values(0)
            sp.wait_ge(s["rbt_out"], 16)
            sp.dma_start(OHS, a["tables"][:, 0:PAST + 2]).then_inc(s["ohs_in"], 16)
            sp.wait_ge(s["kv_done"], 4 * NB)
            steps = sorted([(4 * h - 4, bias, h) for h in range(AH)] + [(3 * b + 6, values, b) for b in range(1, NB)],
                           key=lambda v: v[0])
            for _, load, n in steps:
                load(n)
            ring.full(sp, ("p8",))
            sync_norm(sp, 1)
            ring.full(sp, ("spv", NB - 1))
            sync_chunk(sp, 1, "wo1")

        def sync_memory(sp, l):
            def keys(b):
                if b >= 2:
                    sp.wait_ge(s["mk_used"], NB * l + b - 1)
                sp.dma_start(MK2[:, b % 2], a["cache_mem_k"][l, b].rearrange("(j p) h d -> p j (h d)", p=128)
                             ).then_inc(s["mk_in%d" % (b % 2)], 16)

            keys(0)
            keys(1)
            for b in range(NB):
                sp.dma_start(MV8[:, b], a["cache_mem_v"][l, b].rearrange("(j p) h d -> p j (h d)", p=128)
                             ).then_inc(s["mv_in"], 16)
            for b in range(2, NB):
                keys(b)

        def sync_experts(sp, l):
            m = moe[l]
            up, gate, dn_ = (a[n][l] for n in ("w_exp_up", "w_exp_gate", "w_exp_down"))

            def load(j, e):
                def pick(w):
                    return w[e] if isinstance(e, int) else w[bass.ds(e, 1)].rearrange("a r n -> (a r) n")
                for q, (w, k) in enumerate(((gate, KD), (up, KD), (dn_, 2))):
                    sp.dma_start(WE[:, j, q, :], pick(w).rearrange("(p k) n -> p (k n)", k=k)
                                 ).then_inc(m["w_in%d" % j], 16)

            def put(g, j):
                t = 4 * g + j
                sp.wait_ge(m["out_a"], t + 1)
                sp.wait_ge(m["out_b"], t + 1)
                yd = scratch["y"]
                dst = yd[t * 128:(t + 1) * 128, :] if isinstance(t, int) else yd[bass.ds(t * 128, 128), :]
                sp.dma_start(dst, OUT[:, j % 2, :]).then_inc(m["put%d" % (j % 2)], 16)

            for j in range(GRP):
                load(j, j)
            with sp.Fori(0, NE // GRP - 1) as g:
                for j in range(GRP):
                    sp.wait_ge(m["down_done"], 4 * g + j + 1)
                    load(j, 4 * g + j + GRP)
                    put(g, j)
            sp.wait_ge(s["table_ready"], l + 1)
            groups = sp.value_load(NGI[0:1, 0:1], min_val=0, max_val=(MTILES - NE) // GRP) + NE // GRP
            for j in range(GRP - 1):
                put(NE // GRP - 1, j)
            with sp.If(groups > NE // GRP):
                with sp.Fori(NE // GRP, groups) as g:
                    for j in range(GRP):
                        sp.wait_ge(m["down_done"], 4 * g + j - GRP + 1)
                        load(j, sp.value_load(ETI[0:1, bass.ds(4 * g + j - NE, 1)], min_val=0, max_val=NE - 1))
                    put(g - 1, GRP - 1)
                    for j in range(GRP - 1):
                        put(g, j)
            put(groups - 1, GRP - 1)

        @block.sync
        def _(sp):
            sp.dma_start(cst, a["constants"]).then_inc(s_cst, 16)
            sp.dma_start(X[:, 0:4, :], a["x_prompt"][0].rearrange("(i p) d -> p i d", p=128)).then_inc(s_x, 16)
            sp.dma_start(X[:NB, 4, :], a["x_sample"][:, 0, :]).then_inc(s_x, 16)
            sp.dma_start(MEMROW, a["mem_prompt"][0].rearrange("(i p) d -> p i d", p=128)).then_inc(s_mem, 16)
            nst = 0
            for l in range(DEPTH):
                if l == 0:
                    sync_chunk(sp, 0, "km")
                    sync_small0(sp)
                else:
                    w = a["w_in_dsa"][0].rearrange("(p k) n -> p k n", k=KD)
                    sp.wait_ge(s["y_in4"], 32)
                    sync_chunk(sp, 1, "km")
                    sync_chunk(sp, 1, "vm")
                    sp.wait_ge(stage_done, 4 * 4)
                    sp.dma_start(KW1[:, :, 0:64], w[:, :, 2048:2112]).then_inc(s_l1, 16)
                    sp.dma_start(KW1[:, :, 64:136], w[:, :, 2048:2120]).then_inc(s_l1, 16)
                    sp.dma_start(OHP, a["tables"][:, PAST + 2:PAST + 642]).then_inc(s_l1, 16)
                    sp.dma_start(RB, a["rel_bias"]).then_inc(s_l1, 16)
                    sp.dma_start(PTB, a["page_table"].rearrange("b n -> (b n)").unsqueeze(0)).then_inc(s_l1, 16)
                if l == 0:
                    for name in ("vm", "q", "k", "v", "o", "qm"):
                        sync_chunk(sp, l, name)
                    ring.full(sp, ("memT", 1, 1))
                    sync_norm(sp, l)
                if l == 0:
                    sp.wait_ge(stage_done, 4)
                    sp.dma_start(R["n"], a["state_n"][0].rearrange("b h k -> b (h k)")).then_inc(s["n_in"], 16)
                    for b in range(NB):
                        sp.dma_start(heads(CIN[:, b, :]), a["state_C"][0, b].rearrange("h v k -> v h k")
                                     ).then_inc(s["c_in"], 16)
                    nst = 2
                else:
                    sync_dsa(sp)
                    nst = 5
                if l == 0:
                    for name in ("wo0", "wo1"):
                        sync_chunk(sp, l, name)
                sp.wait_ge(stage_done, 4 * nst)
                for w_, c0, n, name in ((WR, 0, NG, "w_router_group"), (WR, NG, NE, "w_router_expert")):
                    sp.dma_start(w_[:, :, c0:c0 + n], a[name][l].rearrange("(p k) n -> p k n", k=KD)
                                 ).then_inc(s["router_in"], 16)
                sp.dma_start(BR[:, 0:NG], a["b_router_group"][l].partition_broadcast(128)).then_inc(s["router_in"], 16)
                sp.dma_start(BR[:, NG:36], a["b_router_expert"][l].partition_broadcast(128)
                             ).then_inc(s["router_in"], 16)
                for q, n in enumerate(("ln_ffn_g", "ln_ffn_b")):
                    sp.dma_start(lnf[:, q, :], a[n][l].partition_broadcast(128)).then_inc(s["lnf_in"], 16)
                sync_memory(sp, l)
                sp.wait_ge(stage_done, 4 * (nst + 1))
                sync_experts(sp, l)
                if l == DEPTH - 1:
                    sp.wait_ge(stage_done, 4 * (nst + 2))


INS = ["x_prompt", "x_sample", "cache_k", "cache_v", "cache_kidx", "state_C", "state_n", "state_m", "state_conv",
       "cache_mem_k", "cache_mem_v", "page_table", "mem_prompt", "w_in_mlstm", "b_gates_mlstm", "conv_mlstm",
       "norm_mlstm", "w_in_dsa", "rel_bias", "w_mem_kv", "w_out", "ln_mix_g", "ln_mix_b", "ln_ffn_g", "ln_ffn_b",
       "w_router_group", "b_router_group", "w_router_expert", "b_router_expert", "w_exp_up", "w_exp_gate",
       "w_exp_down"]
OUTS = [("y_prompt", (1, SEQ, D)), ("y_sample", (NB, 1, D)),
        ("new_k_prompt", (1, 1, SEQ, AH, AD)), ("new_v_prompt", (1, 1, SEQ, AH, AD)),
        ("new_kidx_prompt", (1, 1, SEQ, AD)),
        ("new_k_sample", (1, NB, 1, AH, AD)), ("new_v_sample", (1, NB, 1, AH, AD)),
        ("new_kidx_sample", (1, NB, 1, AD)),
        ("state_C_prompt", (1, 1, MH, MD, MD)), ("state_n_prompt", (1, 1, MH, MD)), ("state_m_prompt", (1, 1, MH)),
        ("state_conv_prompt", (1, 1, 3, 2 * MW)),
        ("state_C_sample", (1, NB, MH, MD, MD)), ("state_n_sample", (1, NB, MH, MD)), ("state_m_sample", (1, NB, MH)),
        ("state_conv_sample", (1, NB, 3, 2 * MW)),
        ("mem_k_prompt", (DEPTH, 1, MEM, XH, XD)), ("mem_v_prompt", (DEPTH, 1, MEM, XH, XD))]


def kernel(**inputs):
    import numpy as np
    import concourse.bacc as bacc
    from concourse.bass_utils import run_bass_kernel_spmd

    nc = bacc.Bacc("TRN2", target_bir_lowering=False, num_devices=1)
    arrays, a, o, scratch = {}, {}, {}, {}
    table, buckets = constants()
    named = {n: np.ascontiguousarray(inputs[n]) for n in INS}
    named["constants"], named["tables"] = table, buckets
    for name, v in named.items():
        arrays[f"in_{name}"] = v
        a[name] = nc.dram_tensor(f"in_{name}", v.shape, mybir.dt.from_np(v.dtype), kind="ExternalInput").ap()
    for name, shape in OUTS:
        o[name] = nc.dram_tensor(f"out_{name}", shape, F32, kind="ExternalOutput").ap()
    scratch["bias"] = nc.dram_tensor("bias_table", (AH, 640), F32, kind="Internal").ap()
    for l in range(DEPTH):
        scratch["x1_%d" % l] = nc.dram_tensor("x1_%d" % l, (TT, D), F32, kind="Internal").ap()
        scratch["ids_%d" % l] = nc.dram_tensor("token_ids_%d" % l, (128 * LW, 1), U32, kind="Internal").ap()
    scratch["y"] = nc.dram_tensor("expert_out", (MTILES * 128, D), F32, kind="Internal").ap()
    build(nc, a, o, scratch)
    r = run_bass_kernel_spmd(nc, [arrays], core_ids=[0])
    return tuple(r.results[0][f"out_{name}"] for name, _ in OUTS)
```
